# Optimizing a Trainium2 kernel written in Bass

```python
import math
import jax, jax.numpy as jnp
from jax import lax
import numpy as np

D_MODEL = 1024
BATCH = 1
SEQ = 512
DEPTH = 1
DEC_BATCH = 8
DEC_SEQ = 8
PAST_LEN = 4096
PAGE_SIZE = 128

D_MIX = D_MODEL
DN_HEADS = 4
DN_DK = 128
DN_DV = 128
DN_QK = DN_HEADS * DN_DK
DN_V = DN_HEADS * DN_DV
DN_CONV = 4
DN_CHUNK = 64
QKV_DIM = 2 * DN_QK + DN_V
SG_GROUPS = 4
SG_CH = (D_MIX - DN_V) // SG_GROUPS
SG_WIDTH = SG_GROUPS * SG_CH
SG_CHUNK = 128
P_IN = QKV_DIM + DN_V + 2 * DN_HEADS + 2 * SG_WIDTH
MEM_LEN = 256
MEM_HEADS = 4
MEM_HD = D_MODEL // MEM_HEADS
PEER_HEADS = 8
PEER_NKEYS = 128
PEER_NEXP = PEER_NKEYS * PEER_NKEYS
PEER_DKEY = 128
PEER_TOPK = 16
PEER_BLOCK = 128
EPS = 1e-6

kernel_name = 'hymba_deltanet_sgu_peer_step'

F32 = jnp.float32

def _rmsnorm(x, g):
    xf = x.astype(F32)
    y = xf * lax.rsqrt(jnp.mean(xf * xf, axis=-1, keepdims=True) + EPS)
    return (y * g.astype(F32)).astype(x.dtype)

def _layernorm(x, g, b):
    xf = x.astype(F32)
    mu = jnp.mean(xf, axis=-1, keepdims=True)
    var = jnp.mean(jnp.square(xf - mu), axis=-1, keepdims=True)
    y = (xf - mu) * lax.rsqrt(var + EPS)
    return (y * g.astype(F32) + b.astype(F32)).astype(x.dtype)

def _l2norm(x):
    xf = x.astype(F32)
    return xf * lax.rsqrt(jnp.sum(xf * xf, axis=-1, keepdims=True) + EPS)

def _short_conv(x, buf, w):
    T = x.shape[1]
    xx = jnp.concatenate([buf.astype(x.dtype), x], axis=1)
    y = sum(xx[:, j:j + T, :] * w[j] for j in range(DN_CONV))
    return jax.nn.silu(y), xx[:, T:, :]

def _gated_delta(q, k, v, beta, g, S0):
    B, T = q.shape[0], q.shape[1]
    C = min(DN_CHUNK, T)
    n = -(-T // C)
    pad = n * C - T

    def prep(a):
        a = jnp.moveaxis(a.astype(F32), 1, 2)
        a = jnp.pad(a, [(0, 0), (0, 0), (0, pad)] + [(0, 0)] * (a.ndim - 3))
        return a.reshape(a.shape[:2] + (n, C) + a.shape[3:])

    q, k, v, beta, g = prep(q), prep(k), prep(v), prep(beta), prep(g)
    gc = jnp.cumsum(g, axis=-1)
    idx = jnp.arange(C)
    strict = idx[:, None] > idx[None, :]
    causal = idx[:, None] >= idx[None, :]
    diff = gc[..., :, None] - gc[..., None, :]
    kb = k * beta[..., None]
    A = jnp.einsum('bhncd,bhnsd->bhncs', kb, k) * jnp.exp(jnp.where(strict, diff, -jnp.inf))
    u = lax.linalg.triangular_solve(A, v * beta[..., None], left_side=True, lower=True, unit_diagonal=True)
    w = lax.linalg.triangular_solve(A, kb * jnp.exp(gc)[..., None], left_side=True, lower=True, unit_diagonal=True)
    qk = jnp.einsum('bhncd,bhnsd->bhncs', q, k) * jnp.exp(jnp.where(causal, diff, -jnp.inf))

    def step(S, xs):
        qn, kn, un, wn, gn, qkn = xs
        v_new = un - jnp.einsum('bhcd,bhde->bhce', wn, S)
        o = jnp.einsum('bhcd,bhde->bhce', qn * jnp.exp(gn)[..., None], S) + jnp.einsum('bhcs,bhse->bhce', qkn, v_new)
        glast = gn[..., -1]
        S = S * jnp.exp(glast)[..., None, None] + jnp.einsum(
            'bhcd,bhce->bhde', kn * jnp.exp(glast[..., None] - gn)[..., None], v_new)
        return S, o

    xs = tuple(jnp.moveaxis(a, 2, 0) for a in (q, k, u, w, gc, qk))
    S, o = lax.scan(step, S0.astype(F32), xs)
    o = jnp.moveaxis(o, 0, 2).reshape(B, DN_HEADS, n * C, DN_DV)[:, :, :T]
    return jnp.moveaxis(o, 1, 2), S

def _chunk_spatial_mix(v, w, b):
    B, T = v.shape[0], v.shape[1]
    nc = -(-T // SG_CHUNK)
    pad = nc * SG_CHUNK - T
    vp = jnp.pad(v, ((0, 0), (0, pad), (0, 0), (0, 0))).reshape(B, nc, SG_CHUNK, SG_GROUPS, SG_CH)
    tril = jnp.tril(jnp.ones((SG_CHUNK, SG_CHUNK), dtype=bool))
    wm = jnp.where(tril[None], w, jnp.zeros((), w.dtype))
    out = jnp.einsum('gts,bnsgc->bntgc', wm, vp) + b.T[None, None, :, :, None]
    return out.reshape(B, nc * SG_CHUNK, SG_GROUPS, SG_CH)[:, :T]

def _hybrid_mixer(n, S0, c0, w_in, conv_w, a_log, dt_bias, o_norm_g, sg_ln_g, sg_ln_b, sg_w, sg_b, w_out):
    B, T, _ = n.shape
    proj = n @ w_in
    o1 = QKV_DIM
    o2 = o1 + DN_V
    o3 = o2 + DN_HEADS
    o4 = o3 + DN_HEADS
    o5 = o4 + SG_WIDTH
    qkv, z, b_a, a_a, gu, gv = jnp.split(proj, [o1, o2, o3, o4, o5], axis=-1)
    qkv, conv_new = _short_conv(qkv, c0, conv_w)
    q, k, v = jnp.split(qkv, [DN_QK, 2 * DN_QK], axis=-1)
    q = _l2norm(q.reshape(B, T, DN_HEADS, DN_DK)) * (DN_DK ** -0.5)
    k = _l2norm(k.reshape(B, T, DN_HEADS, DN_DK))
    v = v.reshape(B, T, DN_HEADS, DN_DV)
    beta = jax.nn.sigmoid(b_a.astype(F32))
    g = -jnp.exp(a_log.astype(F32)) * jax.nn.softplus(a_a.astype(F32) + dt_bias.astype(F32))
    o, S = _gated_delta(q, k, v, beta, g, S0)
    o = _rmsnorm(o, o_norm_g) * jax.nn.silu(z.reshape(B, T, DN_HEADS, DN_DV).astype(F32))
    o_a = o.reshape(B, T, DN_V).astype(n.dtype)
    u = jax.nn.gelu(gu).reshape(B, T, SG_GROUPS, SG_CH)
    vv = _layernorm(jax.nn.gelu(gv).reshape(B, T, SG_GROUPS, SG_CH), sg_ln_g, sg_ln_b)
    o_b = (u * _chunk_spatial_mix(vv, sg_w, sg_b)).reshape(B, T, SG_WIDTH)
    y = jnp.concatenate([o_a, o_b.astype(n.dtype)], axis=-1) @ w_out
    return y, S, conv_new, vv.reshape(B, T, SG_WIDTH)

def _mem_kv(mem, g, wk, wv):
    m = _rmsnorm(mem, g)
    B, M = mem.shape[0], mem.shape[1]
    return (m @ wk).reshape(B, M, MEM_HEADS, MEM_HD), (m @ wv).reshape(B, M, MEM_HEADS, MEM_HD)

def _mem_attend(n, mk, mv, wq, wo):
    B, T, _ = n.shape
    q = (n @ wq).reshape(B, T, MEM_HEADS, MEM_HD)
    s = jnp.einsum('bthd,bmhd->bhtm', q, mk.astype(q.dtype)).astype(F32) * (MEM_HD ** -0.5)
    p = jax.nn.softmax(s, axis=-1).astype(n.dtype)
    o = jnp.einsum('bhtm,bmhd->bthd', p, mv.astype(n.dtype)).reshape(B, T, D_MODEL)
    return o @ wo

def _peer(n, wq, keys, u_tab, v_tab):
    B, T, D = n.shape
    N = B * T
    x = n.reshape(N, D)
    q = (x @ wq).reshape(N, PEER_HEADS, 2, PEER_DKEY // 2)
    s = jnp.einsum('thpd,hpkd->thpk', q, keys).astype(F32)
    sv, si = lax.top_k(s, PEER_TOPK)
    cand = sv[:, :, 0, :, None] + sv[:, :, 1, None, :]
    cv, ci = lax.top_k(cand.reshape(N, PEER_HEADS, PEER_TOPK * PEER_TOPK), PEER_TOPK)
    i1 = jnp.take_along_axis(si[:, :, 0], ci // PEER_TOPK, axis=-1)
    i2 = jnp.take_along_axis(si[:, :, 1], ci % PEER_TOPK, axis=-1)
    eidx = (i1 * PEER_NKEYS + i2).reshape(N, PEER_HEADS * PEER_TOPK)
    gate = jax.nn.softmax(cv, axis=-1).reshape(N, PEER_HEADS * PEER_TOPK)
    nb = -(-N // PEER_BLOCK)
    pad = nb * PEER_BLOCK - N
    xp = jnp.pad(x, ((0, pad), (0, 0))).reshape(nb, PEER_BLOCK, D)
    ip = jnp.pad(eidx, ((0, pad), (0, 0))).reshape(nb, PEER_BLOCK, -1)
    gp = jnp.pad(gate, ((0, pad), (0, 0))).reshape(nb, PEER_BLOCK, -1)

    def blk(args):
        xb, ib, gb = args
        h = jax.nn.gelu(jnp.einsum('tkd,td->tk', u_tab[ib], xb).astype(F32))
        return jnp.einsum('tk,tkd->td', (gb * h).astype(xb.dtype), v_tab[ib])

    out = lax.map(blk, (xp, ip, gp))
    return out.reshape(nb * PEER_BLOCK, D)[:N].reshape(B, T, D)

def _layer(h, mk, mv, S0, c0, w_in, conv_w, a_log, dt_bias, o_norm_g, sg_ln_g, sg_ln_b, sg_w, sg_b, w_out,
           norm_mix_g, norm_mem_g, w_mq, w_mo, norm_ffn_g, peer_wq, peer_keys, peer_u, peer_v):
    y, S, c, vrows = _hybrid_mixer(_rmsnorm(h, norm_mix_g), S0, c0, w_in, conv_w, a_log, dt_bias, o_norm_g,
                                   sg_ln_g, sg_ln_b, sg_w, sg_b, w_out)
    h = h + y
    h = h + _mem_attend(_rmsnorm(h, norm_mem_g), mk, mv, w_mq, w_mo)
    h = h + _peer(_rmsnorm(h, norm_ffn_g), peer_wq, peer_keys, peer_u, peer_v)
    return h, S, c, vrows

def setup_inputs(seed: int = 0) -> dict:
    key = jax.random.key(seed)
    ks = jax.random.split(key, 30)
    nrm = lambda k, shp, s: jax.random.normal(k, shp, F32) * s
    gain = lambda k, shp: 1.0 + 0.02 * jax.random.normal(k, shp, F32)
    dt = jnp.exp(jax.random.uniform(ks[10], (DEPTH, DN_HEADS), F32, math.log(1e-3), math.log(1e-1)))
    return {
        'x_prompt': nrm(ks[0], (BATCH, SEQ, D_MODEL), 1.0),
        'x_sample': nrm(ks[1], (DEC_BATCH, DEC_SEQ, D_MODEL), 1.0),
        'state_delta': nrm(ks[2], (DEPTH, DEC_BATCH, DN_HEADS, DN_DK, DN_DV), 0.1),
        'state_conv': nrm(ks[3], (DEPTH, DEC_BATCH, DN_CONV - 1, QKV_DIM), 1.0),
        'cache_mem_k': nrm(ks[4], (DEPTH, DEC_BATCH, MEM_LEN, MEM_HEADS, MEM_HD), 1.0),
        'cache_mem_v': nrm(ks[5], (DEPTH, DEC_BATCH, MEM_LEN, MEM_HEADS, MEM_HD), 1.0),
        'mem_prompt': nrm(ks[6], (BATCH, MEM_LEN, D_MODEL), 1.0),
        'w_in': nrm(ks[7], (DEPTH, D_MODEL, P_IN), D_MODEL ** -0.5),
        'conv_w': nrm(ks[8], (DEPTH, DN_CONV, QKV_DIM), DN_CONV ** -0.5),
        'a_log': jnp.log(jax.random.uniform(ks[9], (DEPTH, DN_HEADS), F32, 1.0, 16.0)),
        'dt_bias': dt + jnp.log(-jnp.expm1(-dt)),
        'o_norm_g': gain(ks[11], (DEPTH, DN_DV)),
        'sg_ln_g': gain(ks[12], (DEPTH, SG_GROUPS, SG_CH)),
        'sg_ln_b': nrm(ks[13], (DEPTH, SG_GROUPS, SG_CH), 0.02),
        'sg_w': nrm(ks[14], (DEPTH, SG_GROUPS, SG_CHUNK, SG_CHUNK), 0.5 * SG_CHUNK ** -0.5),
        'sg_b': gain(ks[15], (DEPTH, SG_GROUPS, SG_CHUNK)),
        'w_out': nrm(ks[16], (DEPTH, D_MIX, D_MODEL), D_MIX ** -0.5),
        'norm_mix_g': gain(ks[17], (DEPTH, D_MODEL)),
        'norm_mem_g': gain(ks[18], (DEPTH, D_MODEL)),
        'mem_norm_g': gain(ks[19], (DEPTH, D_MODEL)),
        'w_mq': nrm(ks[20], (DEPTH, D_MODEL, D_MODEL), D_MODEL ** -0.5),
        'w_mk': nrm(ks[21], (DEPTH, D_MODEL, D_MODEL), D_MODEL ** -0.5),
        'w_mv': nrm(ks[22], (DEPTH, D_MODEL, D_MODEL), D_MODEL ** -0.5),
        'w_mo': nrm(ks[23], (DEPTH, D_MODEL, D_MODEL), D_MODEL ** -0.5),
        'norm_ffn_g': gain(ks[24], (DEPTH, D_MODEL)),
        'peer_wq': nrm(ks[25], (DEPTH, D_MODEL, PEER_HEADS * PEER_DKEY), D_MODEL ** -0.5),
        'peer_keys': nrm(ks[26], (DEPTH, PEER_HEADS, 2, PEER_NKEYS, PEER_DKEY // 2), (PEER_DKEY // 2) ** -0.5),
        'peer_u': nrm(ks[27], (DEPTH, PEER_NEXP, D_MODEL), D_MODEL ** -0.5),
        'peer_v': nrm(ks[28], (DEPTH, PEER_NEXP, D_MODEL), (PEER_HEADS * PEER_TOPK) ** -0.5),
        'final_norm_g': gain(ks[29], (D_MODEL,)),
    }

def reference(x_prompt, x_sample, state_delta, state_conv, cache_mem_k, cache_mem_v, mem_prompt,
              w_in, conv_w, a_log, dt_bias, o_norm_g, sg_ln_g, sg_ln_b, sg_w, sg_b, w_out,
              norm_mix_g, norm_mem_g, mem_norm_g, w_mq, w_mk, w_mv, w_mo, norm_ffn_g,
              peer_wq, peer_keys, peer_u, peer_v, final_norm_g):
    hp, hs = x_prompt, x_sample
    Bp = x_prompt.shape[0]
    sd_p, sc_p, mk_p, mv_p, sd_s, sc_s, vr_s = [], [], [], [], [], [], []
    for l in range(DEPTH):
        lw = (w_in[l], conv_w[l], a_log[l], dt_bias[l], o_norm_g[l], sg_ln_g[l], sg_ln_b[l], sg_w[l], sg_b[l],
              w_out[l], norm_mix_g[l], norm_mem_g[l], w_mq[l], w_mo[l], norm_ffn_g[l],
              peer_wq[l], peer_keys[l], peer_u[l], peer_v[l])
        mk, mv = _mem_kv(mem_prompt, mem_norm_g[l], w_mk[l], w_mv[l])
        S0 = jnp.zeros((Bp, DN_HEADS, DN_DK, DN_DV), F32)
        c0 = jnp.zeros((Bp, DN_CONV - 1, QKV_DIM), hp.dtype)
        hp, Sp, cp, _ = _layer(hp, mk, mv, S0, c0, *lw)
        sd_p.append(Sp)
        sc_p.append(cp)
        mk_p.append(mk)
        mv_p.append(mv)
        hs, Ss, cs, vr = _layer(hs, cache_mem_k[l], cache_mem_v[l], state_delta[l], state_conv[l], *lw)
        sd_s.append(Ss)
        sc_s.append(cs)
        vr_s.append(vr)
    y_prompt = _rmsnorm(hp, final_norm_g)
    y_sample = _rmsnorm(hs, final_norm_g)
    state_delta_prompt = jnp.stack(sd_p)
    state_conv_prompt = jnp.stack(sc_p)
    cache_mem_k_prompt = jnp.stack(mk_p)
    cache_mem_v_prompt = jnp.stack(mv_p)
    state_delta_sample = jnp.stack(sd_s)
    state_conv_sample = jnp.stack(sc_s)
    sgu_v_rows_sample = jnp.stack(vr_s)
    return (y_prompt, y_sample, state_delta_prompt, state_conv_prompt, cache_mem_k_prompt, cache_mem_v_prompt,
            state_delta_sample, state_conv_sample, sgu_v_rows_sample)


_drawn_inputs = setup_inputs


def setup_inputs(seed=0):
    import zlib

    import numpy as np

    out = dict(_drawn_inputs(seed))
    spreads = {}
    factors = {'o_norm_g': 6.656,
     'sg_ln_g': 8.145,
     'sg_ln_b': 8.164,
     'sg_b': 6.801,
     'norm_mem_g': 8.0,
     'mem_norm_g': 2.837,
     'norm_ffn_g': 25.225,
     'final_norm_g': 8.577}
    for name, (base, spread) in spreads.items():
        noise = np.random.default_rng([zlib.crc32(name.encode()), seed]).standard_normal(out[name].shape)
        drawn = base * np.exp(spread * noise) if base else spread * noise
        out[name] = __import__('jax').numpy.asarray(drawn.astype(out[name].dtype))
    for name, factor in factors.items():
        out[name] = (out[name] * factor).astype(out[name].dtype)
    return out
```

```python
from contextlib import ExitStack

import numpy as np

import concourse.bass as bass
from concourse import mybir

F32 = mybir.dt.float32
F32R = mybir.dt.float32r
U32 = mybir.dt.uint32
ALU = mybir.AluOpType
ACT = mybir.ActivationFunctionType
AX = mybir.AxisListType.X

P = 128
D = 1024
KT = D // P
SEQ = 512
NB = 8
DS = 8
NS = NB * DS
NT = SEQ + NS
HALF = NT // 2
TILES = [(0, 128), (128, 128), (256, 128), (384, 128), (512, 64)]
H = 4
QKV_TILES = 12
CONV = 4
MEM = 256
NKEY = 128
PH = 8
TOPK = 16
EPS = 1e-6
LEVELS = 7
SAMPLE_LEVELS = 3

C_ID, C_INCL, C_STRICT, C_ONES, C_IOTA, C_LVL = 0, 128, 256, 384, 512, 640
C_INCLS = C_LVL + LEVELS * 128
C_STRICTS = C_INCLS + 64
C_BLKS = C_STRICTS + 64
C_ROWB = C_BLKS + 64
C_COLB = C_ROWB + 8
C_EPS = C_COLB + 512
C_N = C_EPS + 1

G_MIX, G_MEM, G_MEMKV, G_FFN, G_FINAL, G_O, G_N = 0, 8, 16, 24, 32, 40, 41
R_ALOG, R_DT, R_LNG, R_LNB, R_SGB, R_N = 0, 4, 8, 520, 1032, 1544


def constant_table():
    t = np.zeros((P, C_N), np.float32)
    s = np.arange(P)[:, None]
    c = np.arange(P)[None, :]
    t[:, C_ID:C_ID + P] = s == c
    t[:, C_INCL:C_INCL + P] = s <= c
    t[:, C_STRICT:C_STRICT + P] = s < c
    t[:, C_ONES:C_ONES + P] = 1
    t[:, C_IOTA:C_IOTA + P] = c
    for l in range(LEVELS):
        b = 1 << l
        t[:, C_LVL + l * P:C_LVL + (l + 1) * P] = (s // (2 * b) == c // (2 * b)) & (s // b % 2 == 0) & (c // b % 2 == 1)
    same = (s // DS == c // DS)[:, :NS]
    t[:, C_INCLS:C_INCLS + NS] = same & (s <= c)[:, :NS]
    t[:, C_STRICTS:C_STRICTS + NS] = same & (s < c)[:, :NS]
    t[:, C_BLKS:C_BLKS + NS] = same
    t[:, C_ROWB:C_ROWB + NB] = s // DS == np.arange(NB)[None, :]
    t[:, C_COLB:C_COLB + NB * NS] = (np.arange(NS)[None, :] // DS == np.arange(NB)[:, None]).reshape(1, -1)
    t[:, C_EPS] = EPS
    return t


def over(ap, axis, n):
    a = ap.unsqueeze(axis)
    shape = list(a.shape)
    shape[axis] = n
    return a.broadcast_to(shape)


def last(ap, n):
    return ap.broadcast_to(list(ap.shape)[:-1] + [n])


class Chain:

    def __init__(self, eng, sem):
        self.eng, self.sem, self.n = eng, sem, 0

    def after(self, ins):
        self.n += 1
        ins.then_inc(self.sem, 1)
        self.eng.wait_ge(self.sem, self.n)


def norm_squares(act, x, out, squares, base=0):
    for k in range(KT):
        act.activation(out[:, k, :], x[:, k, :], ACT.Square).then_inc(squares, 1)


def norm_sums(pe, cst, sq, ps, n, squares, sums):
    for k in range(KT):
        pe.wait_ge(squares, k + 1)
        for a in range(2):
            mm = pe.matmul(ps[:, a, 0:n // 2], cst[:, C_ONES:C_ONES + P], sq[:, k, a * n // 2:(a + 1) * n // 2],
                           start=(k == 0), stop=(k == KT - 1))
    mm.then_inc(sums, 1)


def norm_root(act, cst, ps, n, rstd, sums, roots):
    act.wait_ge(sums, 1)
    act.activation(rstd[:, 0:n].rearrange("p (a n) -> p a n", a=2), ps[:, 0:2, 0:n // 2], ACT.Sqrt,
                   bias=cst[:, C_EPS:C_EPS + 1], scale=1.0 / D).then_inc(roots, 1)


def norm_scale(dve, chain, gains, g0, x, n, rstd, out, roots, normed):
    dve.wait_ge(roots, 1)
    chain.after(dve.reciprocal(rstd[:, 0:n], rstd[:, 0:n]))
    for k in range(KT):
        dve.scalar_tensor_tensor(out=out[:, k, 0:n], in0=x[:, k, 0:n], scalar=gains[:, g0 + k:g0 + k + 1],
                                 in1=rstd[:, 0:n], op0=ALU.mult, op1=ALU.mult).then_inc(normed, 1)


def load_ring(sp, ring, w, loaded, products, n_tiles, before=0):
    r = len(loaded)
    for m in range(n_tiles):
        if m >= r:
            sp.wait_ge(products, before + m - r + 1)
        sp.dma_start(ring[:, m % r], w[:, :, m * P:(m + 1) * P]).then_inc(loaded[m % r], 16)


def project(pe, ring, src, ps, n, loaded, products, taken, n_tiles):
    r = len(loaded)
    for m in range(n_tiles):
        pe.wait_ge(loaded[m % r], 16 * (m // r + 1))
        if m >= 4:
            pe.wait_ge(taken, m - 3)
        for k in range(KT):
            for a in range(2):
                mm = pe.matmul(ps[:, 2 * (m % 4) + a, 0:n // 2], ring[:, m % r, k, :],
                               src[:, k, a * n // 2:(a + 1) * n // 2], start=(k == 0), stop=(k == KT - 1))
        mm.then_inc(products, 1)


def pair(ps, m, n):
    s = 2 * (m % 4)
    return ps[:, s:s + 2, 0:n // 2]


def in2(ap):
    return ap.rearrange("p (a n) -> p a n", a=2)


WHOLE = [(0, 0, HALF), (1, HALF, HALF)]


class SplitTiles:

    def __init__(self, nc, ctx, sem, name):
        sb = lambda n, s, dt=F32: ctx.enter_context(nc.sbuf_tensor(name + n, s, dt))
        self.raw = sb("w_raw", [P, 3, KT, P])
        self.hi = sb("w_hi", [P, 2, KT, P], F32R)
        self.lo = sb("w_lo", [P, 2, KT, P], F32R)
        self.loaded = [sem(f"{name}w_loaded{i}") for i in range(3)]
        self.high, self.low, self.used = sem(name + "w_high"), sem(name + "w_low"), sem(name + "w_used")

    def load(self, sp, m, src):
        if m >= 3:
            sp.wait_ge(self.low, m - 2)
        sp.dma_start(self.raw[:, m % 3], src).then_inc(self.loaded[m % 3], 16)

    def split_high(self, act, m):
        act.wait_ge(self.loaded[m % 3], 16 * (m // 3 + 1))
        if m >= 2:
            act.wait_ge(self.used, m - 1)
        act.copy(self.hi[:, m % 2], self.raw[:, m % 3]).then_inc(self.high, 1)

    def split_low(self, pool, m):
        pool.wait_ge(self.high, m + 1)
        if m >= 2:
            pool.wait_ge(self.used, m - 1)
        pool.tensor_tensor(self.lo[:, m % 2], self.raw[:, m % 3], self.hi[:, m % 2].bitcast(F32), ALU.subtract
                           ).then_inc(self.low, 1)

    def products(self, pe, m, ps, slot, xhi, xlo, chunks=WHOLE):
        pe.wait_ge(self.low, m + 1)
        for k in range(KT):
            for n, (w, x) in enumerate(((self.hi, xhi), (self.hi, xlo), (self.lo, xhi))):
                for bank, c, size in chunks:
                    mm = pe.matmul(ps[:, 2 * slot + bank, 0:size], w[:, m % 2, k, :], x[:, k, c:c + size],
                                   start=(k == 0 and n == 0), stop=(k == KT - 1 and n == 2))
        mm.then_inc(self.used, 1)


def split_input_high(act, x, xhi, ready, high):
    for k in range(KT):
        act.wait_ge(ready, k + 1)
        act.copy(xhi[:, k, :], x[:, k, 0:xhi.shape[2]]).then_inc(high, 1)


def split_input_low(dve, x, xhi, xlo, ready, high, low):
    dve.wait_ge(ready, KT)
    for k in range(KT):
        dve.wait_ge(high, k + 1)
        dve.tensor_tensor(xlo[:, k, :], x[:, k, 0:xhi.shape[2]], xhi[:, k, :].bitcast(F32), ALU.subtract
                          ).then_inc(low, 1)


def mixer_inputs(nc, io, sem, hT, cst, gains, rows, ps, cT, zT, vv, gate):
    with ExitStack() as ctx:
        def sb(name, shape, dt=F32):
            return ctx.enter_context(nc.sbuf_tensor("in_" + name, shape, dt))

        nT = sb("nT", [P, KT, NT])
        nhi = sb("nhi", [P, KT, NT], F32R)
        nlo = sb("nlo", [P, KT, NT], F32R)
        rstd = sb("rstd", [P, 2, NT])
        gw = sb("gw", [P, 4, 20])
        st = sb("st", [P, 3, 20])
        pre = sb("pre", [P, 2, 3 + SEQ + NB * (3 + DS)])
        wab = sb("wab", [P, KT, 8])
        cw = sb("cw", [P, QKV_TILES, CONV])
        stc = sb("stc", [P, QKV_TILES, NB, 3])
        scn_p = sb("scn_p", [P, QKV_TILES, 3])
        scn_s = sb("scn_s", [P, QKV_TILES, NB, 3])
        tiles = SplitTiles(nc, ctx, sem, "in_")

        h_loaded, loaded = sem("in_h_loaded"), sem("in_loaded")
        squares, sums, roots, normed = sem("in_squares"), sem("in_sums"), sem("in_roots"), sem("in_normed")
        high, low = sem("in_high"), sem("in_low")
        made, taken = sem("in_made"), sem("in_taken")
        edges, convolved, silus = sem("in_edges"), sem("in_convolved"), sem("in_silus")
        l2_done = sem("in_l2_done")
        gate_exp_in, gate_exps, gate_ln_in, gate_lns = (sem("in_gate_exp_in"), sem("in_gate_exps"),
                                                        sem("in_gate_ln_in"), sem("in_gate_lns"))
        ln_vars, ln_roots, ln_done = sem("in_ln_vars"), sem("in_ln_roots"), sem("in_ln_done")
        dve_seq, act_seq, stored, zeroed = sem("in_dve_seq"), sem("in_act_seq"), sem("in_stored"), sem("in_zeroed")

        COLS = [i * P for i in range(12)] + [2568 + i * P for i in range(4)] + [2056 + i * P for i in range(4)] \
            + [1536 + i * P for i in range(4)]
        GV, U, Z = 12, 16, 20
        ITEMS = [("ab", 0)] + [("tile", m) for m in range(13)]
        for x in range(3):
            ITEMS += [("l2", x), ("tile", 13 + x)]
        ITEMS += [("turn", x) for x in range(3)]
        for x in range(5):
            ITEMS += [("l2", 3 + x), ("tile", 16 + x)]
        ITEMS += [("tile", m) for m in range(21, 24)]
        place = {item: i for i, item in enumerate(ITEMS)}
        w_in = io["w_in"].rearrange("(k p) c -> p k c", p=P)
        ident = cst[:, C_ID:C_ID + P]
        block = ctx.enter_context(nc.Block())

        @block.sync
        def _(sp):
            for k in range(KT):
                sp.dma_start(hT[:, k, :], io["xT"][:, k, :]).then_inc(h_loaded, 16)
            sp.dma_start(cst[:, :], io["consts"]).then_inc(loaded, 16)
            sp.dma_start(gains[:, :], io["gains"]).then_inc(loaded, 16)
            sp.dma_start(wab[:, :, :], w_in[:, :, 2048:2056]).then_inc(loaded, 16)
            for m in range(3):
                tiles.load(sp, m, w_in[:, :, COLS[m]:COLS[m] + P])
            sp.dma_start(cw[:, :, :], io["conv_w"]).then_inc(loaded, 16)
            sp.dma_start(stc[:, :, :, :], io["state_conv"]).then_inc(loaded, 16)
            sp.dma_start(rows[:, :], io["rows"].partition_broadcast(P)).then_inc(loaded, 16)
            for m in range(3, len(COLS)):
                tiles.load(sp, m, w_in[:, :, COLS[m]:COLS[m] + P])
            sp.wait_ge(edges, 2 + QKV_TILES)
            sp.dma_start(io["conv_prompt"], scn_p[:, :, :]).then_inc(stored, 16)
            sp.dma_start(io["conv_sample"], scn_s[:, :, :, :]).then_inc(stored, 16)
            sp.wait_ge(ln_done, 1)
            sp.dma_start(io["vrows"], vv[0:NS, 4, :]).then_inc(stored, 16)
            sp.wait_ge(stored, 48)

        @block.gpsimd
        def _(pool):
            for m in range(len(COLS)):
                tiles.split_low(pool, m)

        @block.tensor
        def _(pe):
            pe.wait_ge(loaded, 96)
            norm_sums(pe, cst, nT, ps, NT, squares, sums)
            for i, (kind, x) in enumerate(ITEMS):
                slot = i % 4
                if i >= 4:
                    pe.wait_ge(taken, i - 3)
                if kind == "ab":
                    pe.wait_ge(normed, KT)
                    for t, (t0, n) in enumerate(TILES):
                        for k in range(KT):
                            mm = pe.matmul(ps[0:n, 0, t * 8:t * 8 + 8], nT[:, k, t0:t0 + n], wab[:, k, :],
                                           start=(k == 0), stop=(k == KT - 1))
                    mm.then_inc(made, 1)
                elif kind == "tile":
                    pe.wait_ge(low, KT)
                    tiles.products(pe, x, ps, slot, nhi, nlo)
                elif kind == "l2":
                    pe.wait_ge(silus, x + 1)
                    for a in range(2):
                        mm = pe.matmul(ps[:, 2 * slot + a, 0:HALF], cst[:, C_ONES:C_ONES + P],
                                       nT[:, x, a * HALF:(a + 1) * HALF], start=True, stop=True)
                    mm.then_inc(made, 1)
                else:
                    pe.wait_ge(taken, place["tile", GV + 3] + 1)
                    for a, (t0, n) in enumerate(TILES[2 * x:2 * x + 2]):
                        for g in range(4):
                            mm = pe.transpose(ps[0:n, 2 * slot + a, g * P:g * P + P], zT[:, g, t0:t0 + n], ident)
                    mm.then_inc(made, 1)

        @block.scalar
        def _(act):
            chain = Chain(act, act_seq)
            act.wait_ge(h_loaded, 16 * KT)
            norm_squares(act, hT, nT, squares)
            act.wait_ge(loaded, 96)
            norm_root(act, cst, ps, NT, rstd[:, 0], sums, roots)
            tiles.split_high(act, 0)
            split_input_high(act, nT, nhi, normed, high)
            act.wait_ge(zeroed, 1)

            def silu(m):
                act.wait_ge(convolved, m + 1)
                chain.after(act.activation(cT[:, m, :], cT[:, m, :], ACT.Silu))
                if m < 8:
                    act.activation(nT[:, m, :], cT[:, m, :], ACT.Square).then_inc(silus, 1)

            others = 0
            for i, (kind, x) in enumerate(ITEMS):
                s = 2 * (i % 4)
                if kind == "tile":
                    if x + 1 < len(COLS):
                        tiles.split_high(act, x + 1)
                    act.wait_ge(tiles.used, x + 1)
                else:
                    others += 1
                    act.wait_ge(made, others)
                if kind == "ab":
                    act.copy(gate[:, 0:4, :], ps[:, 0, 0:32].rearrange("p (i c) -> p i c", c=8))
                    act.copy(gate[0:NS, 4, :], ps[0:NS, 0, 32:40]).then_inc(taken, 1)
                elif kind == "l2":
                    if x >= 2:
                        act.wait_ge(l2_done, x - 1)
                    act.activation(in2(rstd[:, x % 2, :]), ps[:, s:s + 2, 0:HALF], ACT.Sqrt,
                                   bias=cst[:, C_EPS:C_EPS + 1], scale=1.0).then_inc(taken, 1)
                elif kind == "turn":
                    for a, (t0, n) in enumerate(TILES[2 * x:2 * x + 2]):
                        ins = act.copy(vv[0:n, 2 * x + a, :], ps[0:n, s + a, :])
                    ins.then_inc(taken, 1)
                elif x < QKV_TILES:
                    act.wait_ge(edges, x + 1)
                    act.copy(pre[:, x % 2, 3:3 + HALF], ps[:, s, 0:HALF])
                    act.copy(pre[:, x % 2, 3 + HALF:3 + SEQ], ps[:, s + 1, 0:SEQ - HALF])
                    act.copy(pre[:, x % 2, 3 + SEQ:].rearrange("p (b t) -> p b t", t=3 + DS)[:, :, 3:],
                             ps[:, s + 1, SEQ - HALF:HALF].rearrange("p (b t) -> p b t", t=DS)).then_inc(taken, 1)
                else:
                    out, fn = {GV: (zT[:, x % 4], ACT.Gelu_apprx_tanh), U: (cT[:, 12 + x % 4], ACT.Gelu_apprx_tanh),
                               Z: (zT[:, x % 4], ACT.Silu)}[x // 4 * 4]
                    act.activation(in2(out), ps[:, s:s + 2, 0:HALF], fn).then_inc(taken, 1)
                if kind == "tile" and 1 <= x <= QKV_TILES:
                    silu(x - 1)
            act.wait_ge(ln_vars, 1)
            act.activation(st[:, 1, :], st[:, 1, :], ACT.Sqrt, bias=cst[:, C_EPS:C_EPS + 1],
                           scale=1.0 / P).then_inc(ln_roots, 1)
            act.wait_ge(gate_exp_in, 1)
            act.activation(gw[:, 1, :], gw[:, 1, :], ACT.Exp)
            act.activation(rows[:, R_ALOG:R_ALOG + 4], rows[:, R_ALOG:R_ALOG + 4], ACT.Exp)
            act.activation(gw[:, 3, :].rearrange("p (i h) -> p i h", h=4), gate[:, :, 0:4],
                           ACT.Sigmoid).then_inc(gate_exps, 1)
            act.wait_ge(gate_ln_in, 1)
            act.activation(gw[:, 2, :], gw[:, 2, :], ACT.Ln).then_inc(gate_lns, 1)

        @block.vector
        def _(dve):
            chain = Chain(dve, dve_seq)
            dve.memset(vv[:, 4, :], 0.0)
            dve.memset(pre[:, :, 0:3], 0.0)
            dve.memset(gate[:, 4, :], 0.0).then_inc(zeroed, 1)
            dve.wait_ge(h_loaded, 16 * KT)
            dve.wait_ge(loaded, 96)
            for b in range(2):
                dve.tensor_copy(pre[:, b, 3 + SEQ:].rearrange("p (b t) -> p b t", t=3 + DS)[:, :, 0:3],
                                stc[:, b]).then_inc(edges, 1)
            norm_scale(dve, chain, gains, G_MIX, hT, NT, rstd[:, 0], nT, roots, normed)
            split_input_low(dve, nT, nhi, nlo, normed, high, low)
            for m in range(QKV_TILES):
                dve.wait_ge(taken, place["tile", m] + 1)
                pp = pre[:, m % 2, 0:3 + SEQ]
                sm = pre[:, m % 2, 3 + SEQ:].rearrange("p (b t) -> p b t", t=3 + DS)
                yp, ys = cT[:, m, 0:SEQ], cT[:, m, SEQ:].rearrange("p (b t) -> p b t", t=DS)
                dve.tensor_scalar(yp, pp[:, 0:SEQ], cw[:, m, 0:1], None, ALU.mult)
                chain.after(dve.tensor_scalar(ys, sm[:, :, 0:DS], cw[:, m, 0:1], None, ALU.mult))
                for j in range(1, CONV):
                    dve.scalar_tensor_tensor(out=yp, in0=pp[:, j:j + SEQ], scalar=cw[:, m, j:j + 1], in1=yp,
                                             op0=ALU.mult, op1=ALU.add)
                    ins = dve.scalar_tensor_tensor(out=ys, in0=sm[:, :, j:j + DS], scalar=cw[:, m, j:j + 1], in1=ys,
                                                   op0=ALU.mult, op1=ALU.add)
                    if j < CONV - 1:
                        chain.after(ins)
                ins.then_inc(convolved, 1)
                dve.tensor_copy(scn_p[:, m, :], pp[:, SEQ:SEQ + 3])
                ins = dve.tensor_copy(scn_s[:, m], sm[:, :, DS:DS + 3])
                if m + 2 < QKV_TILES:
                    chain.after(ins)
                    ins = dve.tensor_copy(sm[:, :, 0:3], stc[:, m + 2])
                ins.then_inc(edges, 1)
            g5 = lambda r: gw[:, r, :].rearrange("p (i h) -> p i h", h=4)
            chain.after(dve.tensor_tensor(g5(0), gate[:, :, 4:8], over(rows[:, R_DT:R_DT + 4], 1, 5), ALU.add))
            chain.after(dve.tensor_scalar(gw[:, 1, :], gw[:, 0, :], -1.0, None, ALU.mult))
            dve.tensor_tensor(gw[:, 1, :], gw[:, 0, :], gw[:, 1, :], ALU.min).then_inc(gate_exp_in, 1)
            for m in range(8):
                dve.wait_ge(taken, place["l2", m] + 1)
                chain.after(dve.reciprocal(rstd[:, m % 2, :], rstd[:, m % 2, :]))
                dve.scalar_tensor_tensor(out=cT[:, m, :], in0=cT[:, m, :], scalar=float(P) ** -0.5 if m < 4 else 1.0,
                                         in1=rstd[:, m % 2, :], op0=ALU.mult, op1=ALU.mult).then_inc(l2_done, 1)
            v3 = vv[:, :, :].rearrange("p i (g c) -> p (i g) c", g=4)
            sqv = nT[:, :, :].rearrange("p k n -> p (k n)")[:, 0:20 * P].rearrange("p (i c) -> p i c", i=20)
            chain.after(dve.tensor_reduce(st[:, 0, :], v3, AX, ALU.add))
            chain.after(dve.tensor_scalar(st[:, 0, :], st[:, 0, :], 1.0 / P, None, ALU.mult))
            chain.after(dve.tensor_tensor(v3, v3, last(st[:, 0, :].unsqueeze(2), P), ALU.subtract))
            chain.after(dve.tensor_tensor(sqv, v3, v3, ALU.mult))
            dve.tensor_reduce(st[:, 1, :], sqv, AX, ALU.add).then_inc(ln_vars, 1)
            dve.wait_ge(ln_roots, 1)
            chain.after(dve.reciprocal(st[:, 2, :], st[:, 1, :]))
            chain.after(dve.tensor_tensor(v3, v3, last(st[:, 2, :].unsqueeze(2), P), ALU.mult))
            chain.after(dve.tensor_tensor(vv[:, :, :], vv[:, :, :], over(rows[:, R_LNG:R_LNG + 512], 1, 5), ALU.mult))
            dve.tensor_tensor(vv[:, :, :], vv[:, :, :], over(rows[:, R_LNB:R_LNB + 512], 1, 5),
                              ALU.add).then_inc(ln_done, 1)
            dve.wait_ge(gate_exps, 1)
            dve.tensor_scalar(gw[:, 2, :], gw[:, 1, :], 1.0, None, ALU.add).then_inc(gate_ln_in, 1)
            dve.wait_ge(gate_lns, 1)
            dve.tensor_copy(gate[:, :, 4:8], g5(3))
            chain.after(dve.scalar_tensor_tensor(out=gw[:, 0, :], in0=gw[:, 0, :], scalar=0.0, in1=gw[:, 2, :],
                                                 op0=ALU.max, op1=ALU.add))
            chain.after(dve.scalar_tensor_tensor(out=gate[:, :, 0:4], in0=g5(0), scalar=-1.0,
                                                 in1=over(rows[:, R_ALOG:R_ALOG + 4], 1, 5),
                                                 op0=ALU.mult, op1=ALU.mult))


def mixer_core(nc, io, sem, cst, gains, rows, ps, cT, zT, vv, gate):
    NTILE = len(TILES)
    with ExitStack() as ctx:
        def sb(name, shape, dt=F32):
            return ctx.enter_context(nc.sbuf_tensor("dl_" + name, shape, dt))

        wT = sb("wT", [P, 4, P])
        wS = sb("wS", [NS, 4, NS])
        S0 = sb("S0", [P, H, NB, P])
        cols = sb("cols", [P, 5, 8])
        ecols = sb("ecols", [P, 5, 4, H])
        egr = sb("egr", [P, H, P])
        egl = sb("egl", [P, 4, H])
        egls = sb("egls", [P, H, NB])
        dec = sb("dec", [P, H, P])
        MT = sb("MT", [P, 5, H, P])
        QK = sb("QK", [P, 5, H, P])
        kd = sb("kd", [P, 5, H, P])
        bv = sb("bv", [P, 5, H, P])
        Dm = sb("Dm", [P, 5, H, P])
        Em = sb("Em", [P, 5, H, P])
        Mb = sb("Mb", [P, 3, H, P])
        X = sb("X", [P, 2, H, P])
        R = sb("R", [P, H, P])
        vn = sb("vn", [P, 2, H, P])
        S = sb("S", [P, 2, H, P])
        km = Dm[:, 0:4].rearrange("p a h c -> p (a h c)")[:, 0:2 * NB * NS].rearrange("p (a b t) -> p a b t", a=2, b=NB)
        vm = MT[0:NS, 0:4].rearrange("p a h c -> p (a h c)").rearrange("p (a b v) -> p a b v", a=2, b=NB)
        tmp = sb("tmp", [P, 2, 512])
        rstd = sb("rstd", [P, 2, NT])

        loaded, wS_zero, wS_loaded, states = (sem("dl_loaded"), sem("dl_wS_zero"), sem("dl_wS_loaded"),
                                              sem("dl_states"))
        prep_mm, act_a, dve_a, act_b, prep_done = (sem("dl_prep_mm"), sem("dl_act_a"), sem("dl_dve_a"),
                                                   sem("dl_act_b"), sem("dl_prep_done"))
        masked, x_mm, x_out, de_mm, de_done = (sem("dl_masked"), sem("dl_x_mm"), sem("dl_x_out"), sem("dl_de_mm"),
                                               sem("dl_de_done"))
        sg_masked, sg_mm, sg_done = sem("dl_sg_masked"), sem("dl_sg_mm"), sem("dl_sg_done")
        ks_mm, r_ready, vn_mm, vn_ready, o_mm, o_out, ds_mm, s_ready = (
            sem("dl_ks_mm"), sem("dl_r_ready"), sem("dl_vn_mm"), sem("dl_vn_ready"), sem("dl_o_mm"), sem("dl_o_out"),
            sem("dl_ds_mm"), sem("dl_s_ready"))
        km_ready, ks_done, vm_ready, ss_mm, ss_done = (sem("dl_km_ready"), sem("dl_ks_done"), sem("dl_vm_ready"),
                                                       sem("dl_ss_mm"), sem("dl_ss_done"))
        o_sq, o_sum, o_root, o_done = sem("dl_o_sq"), sem("dl_o_sum"), sem("dl_o_root"), sem("dl_o_done")
        dve_seq, act_seq, stored = sem("dl_dve_seq"), sem("dl_act_seq"), sem("dl_stored")
        ident_ready = sem("dl_ident_ready")

        STEPS = [(l, i) for l in range(LEVELS) for i in range(NTILE) if l < SAMPLE_LEVELS or i < 4]

        def previous(j):
            l, i = STEPS[j]
            return STEPS.index((l - 1, i)) if l else None

        lvl = lambda l, n: cst[0:n, C_LVL + l * P:C_LVL + l * P + n]
        ident = cst[:, C_ID:C_ID + P]
        block = ctx.enter_context(nc.Block())

        @block.sync
        def _(sp):
            sp.dma_start(wT[:, :, :], io["sg_wT"].rearrange("g s t -> s g t")).then_inc(loaded, 16)
            sp.wait_ge(wS_zero, 1)
            for b in range(NB):
                sp.dma_start(wS[b * DS:(b + 1) * DS, :, b * DS:(b + 1) * DS],
                             io["sg_wT"][:, 0:DS, 0:DS].rearrange("g s t -> s g t")).then_inc(wS_loaded, 16)
            for h in range(H):
                sp.dma_start(S0[:, h], io["state_delta"][:, h].rearrange("b k v -> k b v")).then_inc(states, 16)
            sp.wait_ge(s_ready, 4)
            sp.dma_start(io["delta_prompt"], S[:, 1]).then_inc(stored, 16)
            for h in range(H):
                sp.wait_ge(ss_done, 2 * h + 2)
                sp.dma_start(io["delta_sample"][:, h], S0[:, h]).then_inc(stored, 16)
            sp.wait_ge(stored, 16 * 5)

        @block.gpsimd
        def _(pool):
            pool.memset(wS[:, :, :], 0.0).then_inc(wS_zero, 1)
            for i, (t0, n) in enumerate(TILES):
                pool.tensor_copy(Dm[0:n, i, :, 0:n], over(ident[0:n, 0:n], 1, H))
                ins = pool.tensor_copy(Em[0:n, i, :, 0:n], over(ident[0:n, 0:n], 1, H))
            ins.then_inc(ident_ready, 1)
            for j, (l, i) in enumerate(STEPS):
                n = TILES[i][1]
                if l == 0:
                    pool.wait_ge(prep_done, i + 1)
                if j >= 3:
                    pool.wait_ge(x_mm, j - 2)
                pool.tensor_tensor(Mb[0:n, j % 3, :, 0:n], MT[0:n, i, :, 0:n], over(lvl(l, n), 1, H),
                                   ALU.mult).then_inc(masked, 1)

        @block.tensor
        def _(pe):
            for i, (t0, n) in enumerate(TILES):
                incl = cst[0:n, C_INCL:C_INCL + n] if n == P else cst[0:n, C_INCLS:C_INCLS + n]
                blk = cst[0:n, C_ONES:C_ONES + n] if n == P else cst[0:n, C_BLKS:C_BLKS + n]
                if i:
                    pe.wait_ge(prep_done, i)
                for h in range(H):
                    pe.matmul(ps[:, 0, h * n:h * n + n], gate[0:n, i, h:h + 1].broadcast_to([n, P]), incl,
                              start=True, stop=True)
                    pe.matmul(ps[:, 1, h * n:h * n + n], gate[0:n, i, 4 + h:5 + h].broadcast_to([n, P]),
                              ident[0:n, 0:n], start=True, stop=True)
                pe.matmul(ps[0:n, 2, 0:4], incl, gate[0:n, i, 0:4], start=True, stop=True)
                pe.matmul(ps[0:n, 2, 4:8], blk, gate[0:n, i, 0:4], start=True, stop=True)
                for h in range(H):
                    q, k, v = (cT[:, 4 * x + h, t0:t0 + n] for x in range(3))
                    pe.matmul(ps[0:n, 3, h * n:h * n + n], k, k, start=True, stop=True)
                    pe.matmul(ps[0:n, 4, h * n:h * n + n], k, q, start=True, stop=True)
                    pe.transpose(ps[0:n, 5, h * P:h * P + P], v, ident)
                    mm = pe.transpose(ps[0:n, 6, h * P:h * P + P], k, ident)
                mm.then_inc(prep_mm, 1)
            pe.wait_ge(prep_done, NTILE)
            pe.wait_ge(sg_masked, 1)
            for i, (t0, n) in enumerate(TILES):
                w = wT if n == P else wS
                if i >= 2:
                    pe.wait_ge(sg_done, i - 1)
                for g in range(4):
                    mm = pe.matmul(ps[:, 6 + i % 2, g * n:g * n + n], vv[0:n, i, g * P:g * P + P], w[0:n, g, 0:n],
                                   start=True, stop=True)
                mm.then_inc(sg_mm, 1)

            def x_step(j):
                l, i = STEPS[j]
                n = TILES[i][1]
                pe.wait_ge(masked, j + 1)
                if l == 0:
                    pe.wait_ge(ident_ready, 1)
                else:
                    pe.wait_ge(de_done, previous(j) + 1)
                if j >= 2:
                    pe.wait_ge(x_out, j - 1)
                for h in range(H):
                    mm = pe.matmul(ps[0:n, j % 2, h * n:h * n + n], Mb[0:n, j % 3, h, 0:n], Dm[0:n, i, h, 0:n],
                                   start=True, stop=True)
                mm.then_inc(x_mm, 1)

            def de_step(j):
                l, i = STEPS[j]
                n = TILES[i][1]
                pe.wait_ge(x_out, j + 1)
                if j >= 2:
                    pe.wait_ge(de_done, j - 1)
                for h in range(H):
                    pe.matmul(ps[0:n, 2 + j % 2, h * n:h * n + n], Em[0:n, i, h, 0:n], X[0:n, j % 2, h, 0:n],
                              start=True, stop=True)
                    mm = pe.matmul(ps[0:n, 4 + j % 2, h * n:h * n + n], X[0:n, j % 2, h, 0:n], Em[0:n, i, h, 0:n],
                                   start=True, stop=True)
                mm.then_inc(de_mm, 1)

            for j in range(len(STEPS) + 1):
                if j < len(STEPS):
                    x_step(j)
                if j:
                    de_step(j - 1)
            pe.wait_ge(de_done, len(STEPS))
            pe.wait_ge(sg_done, NTILE)

            for i in range(4):
                t0 = i * P
                if i:
                    pe.wait_ge(s_ready, i)
                    for h in range(H):
                        mm = pe.matmul(ps[:, 0, h * P:h * P + P], cT[:, 4 + h, t0:t0 + P], S[:, (i - 1) % 2, h],
                                       start=True, stop=True)
                    mm.then_inc(ks_mm, 1)
                pe.wait_ge(r_ready, i + 1)
                for h in range(H):
                    mm = pe.matmul(ps[:, 1, h * P:h * P + P], Em[:, i, h], R[:, h] if i else bv[:, 0, h],
                                   start=True, stop=True)
                mm.then_inc(vn_mm, 1)
                pe.wait_ge(vn_ready, i + 1)
                for h in range(H):
                    mm = pe.matmul(ps[:, 3, h * P:h * P + P], kd[:, i, h], vn[:, i % 2, h], start=True, stop=True)
                mm.then_inc(ds_mm, 1)
                if i:
                    pe.wait_ge(o_out, i)
                for h in range(H):
                    mm = pe.matmul(ps[:, 2, h * P:h * P + P], vn[:, i % 2, h], QK[:, i, h], start=True, stop=(i == 0))
                    if i:
                        mm = pe.matmul(ps[:, 2, h * P:h * P + P], S[:, (i - 1) % 2, h], cT[:, h, t0:t0 + P],
                                       start=False, stop=True)
                mm.then_inc(o_mm, 1)

            pe.wait_ge(states, 16 * H)
            for h in range(H):
                pe.wait_ge(km_ready, h + 1)
                for b in range(NB):
                    mm = pe.matmul(ps[0:NS, 0, h * P:h * P + P], km[:, h % 2, b], S0[:, h, b],
                                   start=(b == 0), stop=(b == NB - 1))
                mm.then_inc(ks_done, 1)
            pe.wait_ge(r_ready, 5)
            for h in range(H):
                mm = pe.matmul(ps[0:NS, 1, h * P:h * P + P], Em[0:NS, 4, h, 0:NS], R[0:NS, h], start=True, stop=True)
            mm.then_inc(vn_mm, 1)
            pe.wait_ge(vn_ready, 5)
            pe.wait_ge(o_out, 4)
            for h in range(H):
                pe.matmul(ps[:, 2, h * NS:h * NS + NS], vn[0:NS, 0, h], QK[0:NS, 4, h, 0:NS], start=True, stop=False)
                for b in range(NB):
                    c = b * DS
                    mm = pe.matmul(ps[:, 2, h * NS + c:h * NS + c + DS], S0[:, h, b], cT[:, h, SEQ + c:SEQ + c + DS],
                                   start=False, stop=(b == NB - 1))
            mm.then_inc(o_mm, 1)
            for h in range(H):
                pe.wait_ge(vm_ready, h + 1)
                for a in range(2):
                    if h >= 2:
                        pe.wait_ge(ss_done, 2 * (h - 2) + 2)
                    mm = pe.matmul(ps[:, 4 + 2 * (h % 2) + a, 0:512], kd[0:NS, 4, h],
                                   vm[:, h % 2, 4 * a:4 * a + 4].rearrange("p b v -> p (b v)"), start=True, stop=True)
                mm.then_inc(ss_mm, 1)
            for h in range(H):
                pe.wait_ge(o_sq, h + 1)
                if h == 0:
                    pe.wait_ge(o_out, 5)
                    pe.wait_ge(r_ready, 5)
                    pe.wait_ge(ss_done, 2 * H)
                for a in range(2):
                    mm = pe.matmul(ps[:, 2 * h + a, 0:HALF], cst[:, C_ONES:C_ONES + P],
                                   cT[:, h, a * HALF:(a + 1) * HALF], start=True, stop=True)
                mm.then_inc(o_sum, 1)

        @block.scalar
        def _(act):
            for i, (t0, n) in enumerate(TILES):
                act.wait_ge(prep_mm, i + 1)
                if i:
                    act.wait_ge(prep_done, i)
                act.copy(cols[0:n, i, :], ps[0:n, 2, 0:8])
                act.activation(ecols[0:n, i, 0, :], ps[0:n, 2, 0:4], ACT.Exp)
                act.activation(egr[:, :, 0:n], ps[:, 0, 0:H * n].rearrange("p (h n) -> p h n", h=H),
                               ACT.Exp).then_inc(act_a, 1)
                act.wait_ge(dve_a, i + 1)
                act.activation(dec[0:n, :, 0:n], dec[0:n, :, 0:n], ACT.Exp)
                act.activation(ecols[0:n, i, 2, :], ecols[0:n, i, 1, :], ACT.Exp).then_inc(act_b, 1)
            for j, (l, i) in enumerate(STEPS):
                n = TILES[i][1]
                act.wait_ge(x_mm, j + 1)
                if j >= 2:
                    act.wait_ge(de_mm, j - 1)
                act.copy(X[0:n, j % 2, :, 0:n], ps[0:n, j % 2, 0:H * n].rearrange("p (h n) -> p h n", h=H)
                         ).then_inc(x_out, 1)
            for i in range(5):
                t0, n = TILES[i]
                act.wait_ge(vn_mm, i + 1)
                if i >= 2:
                    act.wait_ge(o_mm, i - 1)
                act.copy(vn[0:n, i % 2, :, :], ps[0:n, 1, 0:512].rearrange("p (h v) -> p h v", h=H)
                         ).then_inc(vn_ready, 1)
                act.wait_ge(o_mm, i + 1)
                act.copy(cT[:, 8:12, t0:t0 + n], ps[:, 2, 0:H * n].rearrange("p (h n) -> p h n", h=H)
                         ).then_inc(o_out, 1)
            act.wait_ge(o_out, 5)
            for h in range(H):
                act.activation(cT[:, h], cT[:, 8 + h], ACT.Square).then_inc(o_sq, 1)
            for h in range(H):
                act.wait_ge(o_sum, h + 1)
                if h >= 2:
                    act.wait_ge(o_done, h - 1)
                act.activation(in2(rstd[:, h % 2]), pair(ps, h, NT), ACT.Sqrt, bias=cst[:, C_EPS:C_EPS + 1],
                               scale=1.0 / P).then_inc(o_root, 1)

        @block.vector
        def _(dve):
            chain = Chain(dve, dve_seq)
            hn = lambda bank, n, p=P: ps[0:p, bank, 0:H * n].rearrange("p (h n) -> p h n", h=H)
            for i, (t0, n) in enumerate(TILES):
                beta, gc = gate[0:n, i, 4:8], cols[0:n, i, 0:4]
                dve.wait_ge(act_a, i + 1)
                for h in range(H):
                    dve.tensor_scalar(dec[0:n, h, 0:n], ps[0:n, 0, h * n:h * n + n], cols[0:n, i, h:h + 1], 0.0,
                                      ALU.subtract, ALU.min)
                dve.tensor_tensor(ecols[0:n, i, 1, :], cols[0:n, i, 4:8], gc, ALU.subtract).then_inc(dve_a, 1)
                dve.tensor_tensor(bv[0:n, i], hn(5, P, n), last(beta.unsqueeze(2), P), ALU.mult)
                dve.tensor_tensor(cT[:, 0:4, t0:t0 + n], cT[:, 0:4, t0:t0 + n], egr[:, :, 0:n], ALU.mult)
                dve.tensor_tensor(ecols[0:n, i, 3, :], beta, ecols[0:n, i, 0, :], ALU.mult)
                if n == P:
                    dve.tensor_copy(egl[:, i, :], egr[:, :, P - 1])
                else:
                    dve.tensor_copy(egls[:, :, :], egr[:, :, DS - 1:NS:DS])
                dve.wait_ge(act_b, i + 1)
                d = dec[0:n, :, 0:n]
                m = cst[0:n, C_INCL:C_INCL + n] if n == P else cst[0:n, C_INCLS:C_INCLS + n]
                chain.after(dve.tensor_tensor(d, d, over(m, 1, H), ALU.mult))
                dve.tensor_tensor(QK[0:n, i, :, 0:n], hn(4, n, n), d, ALU.mult)
                chain.after(dve.tensor_tensor(MT[0:n, i, :, 0:n], hn(3, n, n), d, ALU.mult))
                dve.tensor_tensor(MT[0:n, i, :, 0:n], MT[0:n, i, :, 0:n], hn(1, n, n), ALU.mult)
                dve.tensor_tensor(kd[0:n, i], hn(6, P, n), last(ecols[0:n, i, 2, :].unsqueeze(2), P),
                                  ALU.mult).then_inc(prep_done, 1)
            dve.wait_ge(loaded, 16)
            dve.wait_ge(wS_loaded, 16 * NB)
            dve.tensor_tensor(wT[:, :, :], wT[:, :, :], over(cst[:, C_INCL:C_INCL + P], 1, 4), ALU.mult)
            dve.tensor_tensor(wS[:, :, :], wS[:, :, :], over(cst[0:NS, C_INCLS:C_INCLS + NS], 1, 4),
                              ALU.mult).then_inc(sg_masked, 1)
            bias = rows[:, R_SGB:R_SGB + 512].rearrange("p (g t) -> p g t", g=4)
            for i, (t0, n) in enumerate(TILES):
                dve.wait_ge(sg_mm, i + 1)
                if n == P:
                    t3 = tmp[:, i % 2, 0:4 * n].rearrange("p (g t) -> p g t", g=4)
                    chain.after(dve.tensor_tensor(t3, hn(6 + i % 2, n), bias, ALU.add))
                else:
                    t3 = tmp[:, i % 2, 0:4 * n].rearrange("p (g t) -> p g t", g=4)
                    t4 = tmp[:, i % 2, 0:4 * n].rearrange("p (g b t) -> p g b t", g=4, b=NB)
                    s4 = ps[:, 6 + i % 2, 0:4 * n].rearrange("p (g b t) -> p g b t", g=4, b=NB)
                    chain.after(dve.tensor_tensor(t4, s4, over(bias[:, :, 0:DS], 2, NB), ALU.add))
                dve.tensor_tensor(cT[:, 12:16, t0:t0 + n], t3, cT[:, 12:16, t0:t0 + n], ALU.mult).then_inc(sg_done, 1)
            for j, (l, i) in enumerate(STEPS):
                n = TILES[i][1]
                dve.wait_ge(de_mm, j + 1)
                if l:
                    dve.wait_ge(de_done, previous(j) + 1)
                dve.tensor_tensor(Dm[0:n, i, :, 0:n], Dm[0:n, i, :, 0:n], hn(2 + j % 2, n, n), ALU.subtract)
                dve.tensor_tensor(Em[0:n, i, :, 0:n], Em[0:n, i, :, 0:n], hn(4 + j % 2, n, n),
                                  ALU.subtract).then_inc(de_done, 1)
            dve.wait_ge(de_done, len(STEPS))
            for i in range(4):
                if i:
                    dve.wait_ge(ks_mm, i)
                    t3 = tmp[:, 0, :].rearrange("p (h v) -> p h v", h=H)
                    chain.after(dve.tensor_tensor(t3, hn(0, P), last(ecols[:, i, 3, :].unsqueeze(2), P), ALU.mult))
                    dve.tensor_tensor(R[:, :, :], bv[:, i], t3, ALU.subtract).then_inc(r_ready, 1)
                else:
                    dve.tensor_copy(tmp[:, 0, 0:1], ecols[:, 0, 3, 0:1]).then_inc(r_ready, 1)
                dve.wait_ge(ds_mm, i + 1)
                if i >= 2:
                    dve.wait_ge(o_mm, i)
                if i == 0:
                    dve.tensor_copy(S[:, 0], hn(3, P)).then_inc(s_ready, 1)
                else:
                    for h in range(H):
                        ins = dve.scalar_tensor_tensor(out=S[:, i % 2, h], in0=S[:, (i - 1) % 2, h],
                                                       scalar=egl[:, i, h:h + 1], in1=ps[:, 3, h * P:h * P + P],
                                                       op0=ALU.mult, op1=ALU.add)
                    ins.then_inc(s_ready, 1)
            colb = cst[:, C_COLB:C_COLB + NB * NS].rearrange("p (b t) -> p b t", b=NB)
            for h in range(H):
                if h >= 2:
                    dve.wait_ge(ks_done, h - 1)
                dve.tensor_tensor(km[:, h % 2], over(cT[:, 4 + h, SEQ:NT], 1, NB), colb, ALU.mult).then_inc(km_ready, 1)
            dve.wait_ge(ks_done, H)
            t3 = tmp[0:NS, 0, :].rearrange("p (h v) -> p h v", h=H)
            chain.after(dve.tensor_tensor(t3, hn(0, P, NS), last(ecols[0:NS, 4, 3, :].unsqueeze(2), P), ALU.mult))
            dve.tensor_tensor(R[0:NS], bv[0:NS, 4], t3, ALU.subtract).then_inc(r_ready, 1)
            dve.wait_ge(vn_ready, 5)
            for h in range(H):
                if h >= 2:
                    dve.wait_ge(ss_mm, h - 1)
                dve.tensor_tensor(vm[:, h % 2], over(vn[0:NS, 0, h], 1, NB),
                                  last(cst[0:NS, C_ROWB:C_ROWB + NB].unsqueeze(2), P), ALU.mult).then_inc(vm_ready, 1)
                if h >= 1:
                    sample_state(dve, chain, h - 1, ss_mm, ss_done, S0, egls, ps)
            sample_state(dve, chain, H - 1, ss_mm, ss_done, S0, egls, ps)
            for h in range(H):
                dve.wait_ge(o_root, h + 1)
                chain.after(dve.reciprocal(rstd[:, h % 2], rstd[:, h % 2]))
                chain.after(dve.scalar_tensor_tensor(out=cT[:, 8 + h], in0=cT[:, 8 + h], scalar=gains[:, G_O:G_O + 1],
                                                     in1=rstd[:, h % 2], op0=ALU.mult, op1=ALU.mult))
                dve.tensor_tensor(cT[:, 8 + h], cT[:, 8 + h], zT[:, h], ALU.mult).then_inc(o_done, 1)


def sample_state(dve, chain, h, ss_mm, ss_done, S0, egls, ps):
    dve.wait_ge(ss_mm, h + 1)
    chain.after(dve.tensor_tensor(S0[:, h], S0[:, h], last(egls[:, h, :].unsqueeze(2), P), ALU.mult))
    for a in range(2):
        dve.tensor_tensor(S0[:, h, 4 * a:4 * a + 4], S0[:, h, 4 * a:4 * a + 4],
                          ps[:, 4 + 2 * (h % 2) + a, 0:512].rearrange("p (b v) -> p b v", b=4), ALU.add
                          ).then_inc(ss_done, 1)


def mixer_output(nc, io, sem, hT, ps, cT):
    with ExitStack() as ctx:
        ohi = ctx.enter_context(nc.sbuf_tensor("ou_ohi", [P, KT, NT], F32R))
        olo = ctx.enter_context(nc.sbuf_tensor("ou_olo", [P, KT, NT], F32R))
        tiles = SplitTiles(nc, ctx, sem, "ou_")
        high, low, added = sem("ou_high"), sem("ou_low"), sem("ou_added")
        w = io["w_out"].rearrange("(k p) c -> p k c", p=P)
        block = ctx.enter_context(nc.Block())

        @block.sync
        def _(sp):
            for m in range(KT):
                tiles.load(sp, m, w[:, :, m * P:(m + 1) * P])

        @block.gpsimd
        def _(pool):
            for m in range(KT):
                tiles.split_low(pool, m)

        @block.scalar
        def _(act):
            for k in range(KT):
                act.copy(ohi[:, k, :], cT[:, 8 + k, :]).then_inc(high, 1)
                if k == 3:
                    tiles.split_high(act, 0)
            for m in range(1, KT):
                tiles.split_high(act, m)

        @block.tensor
        def _(pe):
            pe.wait_ge(low, KT)
            for m in range(KT):
                if m >= 4:
                    pe.wait_ge(added, m - 3)
                tiles.products(pe, m, ps, m % 4, ohi, olo)

        @block.vector
        def _(dve):
            for k in range(KT):
                dve.wait_ge(high, k + 1)
                dve.tensor_tensor(olo[:, k, :], cT[:, 8 + k, :], ohi[:, k, :].bitcast(F32), ALU.subtract
                                  ).then_inc(low, 1)
            for m in range(KT):
                dve.wait_ge(tiles.used, m + 1)
                dve.tensor_tensor(in2(hT[:, m]), in2(hT[:, m]), pair(ps, m, NT), ALU.add).then_inc(added, 1)


def memory_attention(nc, io, sem, hT, cst, gains, ps):
    SCALE = float(2 * P) ** -0.5
    ident = cst[:, C_ID:C_ID + P]
    with ExitStack() as ctx:
        def sb(name, shape, dt=F32):
            return ctx.enter_context(nc.sbuf_tensor("at_" + name, shape, dt))

        memT = sb("memT", [P, KT, MEM])
        mkT = sb("mkT", [P, KT, MEM])
        mv = sb("mv", [P, 2, D])
        nT = sb("nT", [P, KT, NT])
        qT = sb("qT", [P, KT, NT])
        rstd = sb("rstd", [P, NT])
        ring = sb("ring", [P, 4, KT, P])
        wv = sb("wv", [P, KT, 512])
        qm = sb("qm", [P, KT, NB, NS])
        kc = sb("kc", [P, 2, KT, MEM])
        vc = sb("vc", [P, 2, 2, D])
        prob = sb("prob", [P, 2, 4, MEM])
        probT = sb("probT", [P, 2, 8, P])
        small = sb("small", [P, 2, 4, 4])

        mem_loaded = sem("at_mem_loaded")
        wv_loaded, wv_used = sem("at_wv_loaded"), sem("at_mv_mm")
        w_loaded = [sem(f"at_w_loaded{i}") for i in range(4)]
        squares_m, sums_m, roots_m, normed_m = (sem("at_squares_m"), sem("at_sums_m"), sem("at_roots_m"),
                                                sem("at_normed_m"))
        squares, sums, roots, normed = sem("at_squares"), sem("at_sums"), sem("at_roots"), sem("at_normed")
        products, taken, mv_taken = sem("at_products"), sem("at_taken"), sem("at_mv_taken")
        kc_loaded = [sem(f"at_kc_loaded{i}") for i in range(2)]
        vc_loaded = [sem(f"at_vc_loaded{i}") for i in range(2)]
        kc_used, vc_used = sem("at_kc_used"), sem("at_vc_used")
        scores, maxed, exped, scaled = sem("at_scores"), sem("at_maxed"), sem("at_exped"), sem("at_scaled")
        turned, turned_out, mixed, mixed_out = (sem("at_turned"), sem("at_turned_out"), sem("at_mixed"),
                                                sem("at_mixed_out"))
        qm_ready, added, dve_seq, act_seq, stored = (sem("at_qm_ready"), sem("at_added"), sem("at_dve_seq"),
                                                     sem("at_act_seq"), sem("at_stored"))
        wk, wvv, wq, wo = (io[n].rearrange("(k p) c -> p k c", p=P) for n in ("w_mk", "w_mv", "w_mq", "w_mo"))
        block = ctx.enter_context(nc.Block())

        @block.sync
        def _(sp):
            sp.dma_start(memT[:, :, :], io["memT"]).then_inc(mem_loaded, 16)
            for m in range(3 * KT):
                w = (wk, wq, wo)[m // KT]
                if m >= 4:
                    sp.wait_ge(products, m - 3)
                sp.dma_start(ring[:, m % 4], w[:, :, (m % KT) * P:(m % KT + 1) * P]).then_inc(w_loaded[m % 4], 16)
                if m == 3:
                    sp.dma_start(wv[:, :, :], wvv[:, :, 0:512]).then_inc(wv_loaded, 16)
                    for b in range(2):
                        sp.dma_start(kc[:, b], io["cacheT"][b]).then_inc(kc_loaded[b], 16)
                        sp.dma_start(vc[:, b], io["cache_v"][b]).then_inc(vc_loaded[b], 16)
                if m == 11:
                    sp.wait_ge(wv_used, 2)
                    sp.dma_start(wv[:, :, :], wvv[:, :, 512:1024]).then_inc(wv_loaded, 16)
                    sp.wait_ge(taken, KT)
                    sp.dma_start(io["mem_k"], mkT[:, :, :]).then_inc(stored, 16)
                if m == 2 * KT + 3:
                    for b in range(2, NB):
                        sp.wait_ge(kc_used, b - 1)
                        sp.dma_start(kc[:, b % 2], io["cacheT"][b]).then_inc(kc_loaded[b % 2], 16)
                    for b in range(2, NB):
                        sp.wait_ge(vc_used, b - 1)
                        sp.dma_start(vc[:, b % 2], io["cache_v"][b]).then_inc(vc_loaded[b % 2], 16)
            sp.wait_ge(mv_taken, 4)
            sp.dma_start(io["mem_v"], mv[:, :, :]).then_inc(stored, 16)
            sp.wait_ge(stored, 32)

        @block.tensor
        def _(pe):
            pe.wait_ge(mem_loaded, 16)
            norm_sums(pe, cst, mkT, ps, MEM, squares_m, sums_m)
            pe.wait_ge(normed_m, KT)

            def products_of(src, n, m0):
                for m in range(m0, m0 + KT):
                    pe.wait_ge(w_loaded[m % 4], 16 * (m // 4 + 1))
                    if m >= 4:
                        pe.wait_ge(taken, m - 3)
                    for k in range(KT):
                        for a in range(2):
                            mm = pe.matmul(ps[:, 2 * (m % 4) + a, 0:n // 2], ring[:, m % 4, k, :],
                                           src[:, k, a * n // 2:(a + 1) * n // 2], start=(k == 0), stop=(k == KT - 1))
                    mm.then_inc(products, 1)

            products_of(memT, MEM, 0)
            pe.wait_ge(taken, KT)
            norm_sums(pe, cst, nT, ps, NT, squares, sums)
            for a in range(2):
                pe.wait_ge(wv_loaded, 16 * (a + 1))
                if a == 1:
                    pe.wait_ge(normed, KT)
                    products_of(nT, NT, KT)
                    pe.wait_ge(taken, 2 * KT)
                for i in range(2):
                    for k in range(KT):
                        mm = pe.matmul(ps[:, 4 + 2 * a + i, 0:512], memT[:, k, i * P:(i + 1) * P], wv[:, k, :],
                                       start=(k == 0), stop=(k == KT - 1))
                    mm.then_inc(wv_used, 1)
                if a == 0:
                    pe.wait_ge(mv_taken, 2)

            pe.wait_ge(mv_taken, 4)

            def score(i):
                t0, n = TILES[i]
                if i:
                    pe.wait_ge(exped, i)
                if n == P:
                    for h in range(4):
                        for e in range(2):
                            mm = pe.matmul(ps[:, h // 2, (h % 2) * MEM:(h % 2 + 1) * MEM], qT[:, 2 * h + e, t0:t0 + P],
                                           mkT[:, 2 * h + e, :], start=(e == 0), stop=(e == 1))
                else:
                    pe.wait_ge(qm_ready, 1)
                    for b in range(NB):
                        pe.wait_ge(kc_loaded[b % 2], 16 * (b // 2 + 1))
                        for h in range(4):
                            for e in range(2):
                                mm = pe.matmul(ps[0:n, h // 2, (h % 2) * MEM:(h % 2 + 1) * MEM], qm[:, 2 * h + e, b],
                                               kc[:, b % 2, 2 * h + e, :], start=(b == 0 and h % 2 == 0 and e == 0),
                                               stop=(b == NB - 1 and e == 1), skip_group_check=True)
                        mm.then_inc(kc_used, 1)
                    mm = pe.matmul(ps[:, 7, 0:1], ident, ident[:, 0:1], start=True, stop=True)
                mm.then_inc(scores, 1)

            def turn(i):
                t0, n = TILES[i]
                pe.wait_ge(scaled, i + 1)
                if i:
                    pe.wait_ge(turned_out, i)
                for j in range(8):
                    h, m = j // 2, j % 2
                    mm = pe.transpose(ps[:, 2 + j // 4, (j % 4) * P:(j % 4) * P + n],
                                      prob[0:n, i % 2, h, m * P:(m + 1) * P], ident[0:n, 0:n])
                mm.then_inc(turned, 1)

            def mix(i):
                t0, n = TILES[i]
                pe.wait_ge(turned_out, i + 1)
                if i:
                    pe.wait_ge(mixed_out, i)
                if n == P:
                    for j in range(8):
                        h = j // 2
                        for m in range(2):
                            mm = pe.matmul(ps[:, 4 + j // 4, (j % 4) * P:(j % 4) * P + n], mv[:, m, j * P:(j + 1) * P],
                                           probT[:, i % 2, 2 * h + m, 0:n], start=(m == 0), stop=(m == 1))
                else:
                    for b in range(NB):
                        pe.wait_ge(vc_loaded[b % 2], 16 * (b // 2 + 1))
                        for j in range(8):
                            h, c = j // 2, (j % 4) * P + b * DS
                            for m in range(2):
                                mm = pe.matmul(ps[:, 4 + j // 4, c:c + DS], vc[:, b % 2, m, j * P:(j + 1) * P],
                                               probT[:, i % 2, 2 * h + m, b * DS:(b + 1) * DS],
                                               start=(m == 0), stop=(m == 1))
                        mm.then_inc(vc_used, 1)
                    mm = pe.matmul(ps[:, 7, 0:1], ident, ident[:, 0:1], start=True, stop=True)
                mm.then_inc(mixed, 1)

            for i in range(len(TILES) + 2):
                if i < len(TILES):
                    score(i)
                if 1 <= i <= len(TILES):
                    turn(i - 1)
                if i >= 2:
                    mix(i - 2)
            pe.wait_ge(mixed_out, len(TILES))
            for m in range(2 * KT, 3 * KT):
                pe.wait_ge(w_loaded[m % 4], 16 * (m // 4 + 1))
                if m >= 2 * KT + 4:
                    pe.wait_ge(added, m - 2 * KT - 3)
                for k in range(KT):
                    for a in range(2):
                        mm = pe.matmul(ps[:, 2 * (m % 4) + a, 0:HALF], ring[:, m % 4, k, :],
                                       nT[:, k, a * HALF:(a + 1) * HALF], start=(k == 0), stop=(k == KT - 1))
                mm.then_inc(products, 1)

        @block.scalar
        def _(act):
            act.wait_ge(mem_loaded, 16)
            norm_squares(act, memT, mkT, squares_m)
            norm_root(act, cst, ps, MEM, rstd, sums_m, roots_m)
            for m in range(KT):
                act.wait_ge(products, m + 1)
                act.copy(in2(mkT[:, m]), pair(ps, m, MEM)).then_inc(taken, 1)
            norm_squares(act, hT, nT, squares)
            norm_root(act, cst, ps, NT, rstd, sums, roots)
            for i in range(2):
                act.wait_ge(wv_used, i + 1)
                act.copy(mv[:, i, 0:512], ps[:, 4 + i, :]).then_inc(mv_taken, 1)
            for m in range(KT):
                act.wait_ge(products, KT + m + 1)
                act.copy(in2(qT[:, m]), pair(ps, m, NT)).then_inc(taken, 1)
            for i in range(2):
                act.wait_ge(wv_used, 3 + i)
                act.copy(mv[:, i, 512:1024], ps[:, 6 + i, :]).then_inc(mv_taken, 1)

            def turn_out(i):
                n = TILES[i][1]
                act.wait_ge(turned, i + 1)
                if i >= 2:
                    act.wait_ge(mixed, i - 1)
                act.copy(probT[:, i % 2, :, 0:n].rearrange("p (a j) n -> p a j n", a=2),
                         ps[:, 2:4, :].rearrange("p a (j n) -> p a j n", j=4)[:, :, :, 0:n]).then_inc(turned_out, 1)

            def mix_out(i):
                t0, n = TILES[i]
                act.wait_ge(mixed, i + 1)
                act.copy(nT[:, :, t0:t0 + n].rearrange("p (a j) n -> p a j n", a=2),
                         ps[:, 4:6, :].rearrange("p a (j n) -> p a j n", j=4)[:, :, :, 0:n]).then_inc(mixed_out, 1)

            for i in range(len(TILES) + 2):
                if i < len(TILES):
                    n = TILES[i][1]
                    act.wait_ge(maxed, i + 1)
                    if i >= 2:
                        act.wait_ge(turned, i - 1)
                    for h in range(4):
                        ins = act.activation(prob[0:n, i % 2, h, :], ps[0:n, h // 2, (h % 2) * MEM:(h % 2 + 1) * MEM],
                                             ACT.Exp, bias=small[0:n, i % 2, 1, h:h + 1], scale=SCALE,
                                             accum_out=small[0:n, i % 2, 2, h:h + 1])
                    ins.then_inc(exped, 1)
                if 1 <= i <= len(TILES):
                    turn_out(i - 1)
                if i >= 2:
                    mix_out(i - 2)

        @block.vector
        def _(dve):
            chain = Chain(dve, dve_seq)
            norm_scale(dve, chain, gains, G_MEMKV, memT, MEM, rstd, memT, roots_m, normed_m)
            dve.wait_ge(normed_m, KT)
            norm_scale(dve, chain, gains, G_MEM, hT, NT, rstd, nT, roots, normed)
            dve.wait_ge(taken, 2 * KT)
            colb = cst[:, C_COLB:C_COLB + NB * NS].rearrange("p (b t) -> p b t", b=NB)
            for k in range(KT):
                ins = dve.tensor_tensor(qm[:, k], over(qT[:, k, SEQ:NT], 1, NB), colb, ALU.mult)
            ins.then_inc(qm_ready, 1)
            for i, (t0, n) in enumerate(TILES):
                s = small[0:n, i % 2]
                dve.wait_ge(scores, i + 1)
                if i >= 2:
                    dve.wait_ge(exped, i - 1)
                chain.after(dve.tensor_reduce(s[:, 0, :].rearrange("p (a h) -> p a h", a=2),
                                              ps[0:n, 0:2, :].rearrange("p a (h m) -> p a h m", h=2), AX, ALU.max))
                dve.tensor_scalar(s[:, 1, :], s[:, 0, :], -SCALE, None, ALU.mult).then_inc(maxed, 1)
                dve.wait_ge(exped, i + 1)
                chain.after(dve.reciprocal(s[:, 3, :], s[:, 2, :]))
                dve.tensor_tensor(prob[0:n, i % 2], prob[0:n, i % 2], last(s[:, 3, :].unsqueeze(2), MEM),
                                  ALU.mult).then_inc(scaled, 1)
            for m in range(KT):
                dve.wait_ge(products, 2 * KT + m + 1)
                dve.tensor_tensor(in2(hT[:, m]), in2(hT[:, m]), pair(ps, m, NT), ALU.add).then_inc(added, 1)


def peer_scores(nc, io, sem, hT, cst, gains, ps, xhi, xlo, scores_sb):
    with ExitStack() as ctx:
        def sb(name, shape, dt=F32):
            return ctx.enter_context(nc.sbuf_tensor("ps_" + name, shape, dt))

        nT = sb("nT", [P, KT, NT])
        qT = sb("qT", [P, KT, NT])
        rstd = sb("rstd", [P, NT])
        ring = sb("ring", [P, 4, KT, P])
        kbd = sb("kbd", [P, PH, 2 * NKEY])
        squares, sums, roots, normed = sem("ps_squares"), sem("ps_sums"), sem("ps_roots"), sem("ps_normed")
        loaded = [sem(f"ps_loaded{i}") for i in range(4)]
        products, taken = sem("ps_products"), sem("ps_taken")
        keys_zero, keys_loaded = sem("ps_keys_zero"), sem("ps_keys_loaded")
        score_mm, score_out, high, dve_seq, zeroed = (sem("ps_score_mm"), sem("ps_score_out"), sem("ps_high"),
                                                      sem("ps_dve_seq"), sem("ps_zeroed"))
        block = ctx.enter_context(nc.Block())

        @block.sync
        def _(sp):
            sp.wait_ge(keys_zero, 1)
            sp.dma_start(kbd[0:64, :, 0:NKEY], io["keysT"][0:64]).then_inc(keys_loaded, 16)
            sp.dma_start(kbd[64:P, :, NKEY:2 * NKEY], io["keysT"][64:P]).then_inc(keys_loaded, 16)
            load_ring(sp, ring, io["peer_wq"].rearrange("(k p) c -> p k c", p=P), loaded, products, KT)

        @block.gpsimd
        def _(pool):
            pool.memset(kbd[:, :, :], 0.0).then_inc(keys_zero, 1)
            pool.memset(scores_sb[:, 4], 0.0).then_inc(zeroed, 1)

        @block.tensor
        def _(pe):
            norm_sums(pe, cst, nT, ps, NT, squares, sums)
            pe.wait_ge(normed, KT)
            project(pe, ring, nT, ps, NT, loaded, products, taken, KT)
            pe.wait_ge(taken, KT)
            pe.wait_ge(keys_loaded, 32)
            for c in range(2 * len(TILES)):
                t0, n = TILES[c // 2]
                if c >= 4:
                    pe.wait_ge(score_out, c - 3)
                for x in range(4):
                    h = 4 * (c % 2) + x
                    mm = pe.matmul(ps[0:n, 2 * (c % 4) + x // 2, (x % 2) * 256:(x % 2 + 1) * 256],
                                   qT[:, h, t0:t0 + n], kbd[:, h, :], start=True, stop=True)
                mm.then_inc(score_mm, 1)

        @block.scalar
        def _(act):
            norm_squares(act, hT, nT, squares)
            norm_root(act, cst, ps, NT, rstd, sums, roots)
            for k in range(KT):
                act.wait_ge(normed, k + 1)
                act.copy(xhi[:, k, :], nT[:, k, :]).then_inc(high, 1)
            for m in range(KT):
                act.wait_ge(products, m + 1)
                act.copy(in2(qT[:, m]), pair(ps, m, NT)).then_inc(taken, 1)
            act.wait_ge(zeroed, 1)
            for c in range(2 * len(TILES)):
                n = TILES[c // 2][1]
                act.wait_ge(score_mm, c + 1)
                act.copy(scores_sb[0:n, c // 2, 8 * (c % 2):8 * (c % 2) + 8, :].rearrange("p (a x) k -> p a (x k)", a=2),
                         ps[0:n, 2 * (c % 4):2 * (c % 4) + 2, :]).then_inc(score_out, 1)

        @block.vector
        def _(dve):
            chain = Chain(dve, dve_seq)
            norm_scale(dve, chain, gains, G_FFN, hT, NT, rstd, nT, roots, normed)
            dve.wait_ge(normed, KT)
            for k in range(KT):
                dve.wait_ge(high, k + 1)
                dve.tensor_tensor(xlo[:, k, :], nT[:, k, :], xhi[:, k, :].bitcast(F32), ALU.subtract)


class ExpertLoop:

    def __init__(self, nc, ctx, sem, name, io, j0, count, ps, xhi, xlo):
        sb = lambda n, s, dt=F32: ctx.enter_context(nc.sbuf_tensor(name + n, s, dt))
        self.u = sb("u", [P, 4, KT, P])
        self.uhi = sb("uhi", [P, 2, KT, P], F32R)
        self.ulo = sb("ulo", [P, 2, KT, P], F32R)
        self.h = sb("h", [P, 2, 2, NT])
        self.u_loaded = [sem(f"{name}u_loaded{i}") for i in range(4)]
        self.high, self.low, self.products, self.gelus = (sem(name + "high"), sem(name + "low"),
                                                          sem(name + "products"), sem(name + "gelus"))
        self.h_stored = [sem(f"{name}h_stored{i}") for i in range(2)]
        self.io, self.j0, self.count, self.ps, self.x = io, j0, count, ps, (xhi, xlo)

    def load(self, sp, j, slot):
        sp.dma_start(self.u[:, slot], self.io["uT"][self.j0 + j]).then_inc(self.u_loaded[slot], 16)

    def store(self, sp, group, c):
        sp.dma_start(self.io["acts"][self.j0 // 4 + group, :, 2 * c:2 * c + 2, :], self.h[:, c]
                     ).then_inc(self.h_stored[c], 16)

    def sync_step(self, sp, g, first=False, last=False):
        for b in range(4):
            j = 4 * g + b
            if not (last and b):
                if not (first and b == 0):
                    sp.wait_ge(self.low, j)
                self.load(sp, j + 3, (b + 3) % 4)
            if b % 2 == 0 and not (first and b == 0):
                sp.wait_ge(self.gelus, j)
                self.store(sp, g if b else g - 1, 0 if b else 1)

    def scalar_high(self, act, j, b, g, wait_products=True):
        act.wait_ge(self.u_loaded[b], 16 * g + 16)
        if wait_products:
            act.wait_ge(self.products, j - 1)
        act.copy(self.uhi[:, b % 2], self.u[:, b]).then_inc(self.high, 1)

    def scalar_tile(self, act, g, b, first=False, last=False):
        j = 4 * g + b
        if not (last and b == 3):
            self.scalar_high(act, j + 1, (b + 1) % 4, g + (b + 1) // 4, not (first and b == 0))
        act.wait_ge(self.products, j + 1)
        if b % 2 == 0 and not first:
            act.wait_ge(self.h_stored[b // 2], 16 * g)
        act.activation(in2(self.h[:, b // 2, b % 2]), self.ps[:, 2 * (b % 2):2 * (b % 2) + 2, 0:HALF],
                       ACT.Gelu_apprx_tanh).then_inc(self.gelus, 1)

    def pool_step(self, pool, g, first=False):
        for b in range(4):
            j = 4 * g + b
            pool.wait_ge(self.high, j + 1)
            if not (first and b < 2):
                pool.wait_ge(self.products, j - 1)
            pool.tensor_tensor(self.ulo[:, b % 2], self.u[:, b], self.uhi[:, b % 2].bitcast(F32), ALU.subtract
                               ).then_inc(self.low, 1)

    def tensor_tile(self, pe, g, b, first=False):
        j = 4 * g + b
        pe.wait_ge(self.low, j + 1)
        if not (first and b < 2):
            pe.wait_ge(self.gelus, j - 1)
        xhi, xlo = self.x
        for k in range(KT):
            for n, (w, x) in enumerate(((self.uhi, xhi), (self.uhi, xlo), (self.ulo, xhi))):
                for a in range(2):
                    mm = pe.matmul(self.ps[:, 2 * (b % 2) + a, 0:HALF], w[:, b % 2, k, :],
                                   x[:, k, a * HALF:(a + 1) * HALF], start=(k == 0 and n == 0),
                                   stop=(k == KT - 1 and n == 2))
        mm.then_inc(self.products, 1)

    def run(self, eng, step):
        n = self.count // 4
        step(0, first=True)
        with eng.Fori(1, n - 1) as g:
            step(g)
        step(n - 1, last=True)

    def finish_sync(self, sp):
        n = self.count // 4
        sp.wait_ge(self.gelus, self.count)
        self.store(sp, n - 1, 1)
        for c in range(2):
            sp.wait_ge(self.h_stored[c], 16 * n)


LOWEST = -3.0e38


def peer_select(nc, io, sem, cst, ps, xhi, xlo, scores_sb, picks, drops):
    COUNT = 56
    with ExitStack() as ctx:
        def sb(name, shape, dt=F32):
            return ctx.enter_context(nc.sbuf_tensor("se_" + name, shape, dt))

        loop = ExpertLoop(nc, ctx, sem, "se_", io, 0, COUNT, ps, xhi, xlo)
        s = sb("s", [P, 16, NKEY])
        r = sb("r", [P, 16, NKEY])
        best = sb("best", [P, 16, TOPK])
        where = sb("where", [P, 16, TOPK], U32)
        wheref = sb("wheref", [P, PH, 2, TOPK])
        cand = sb("cand", [P, PH, TOPK * TOPK])
        top = sb("top", [P, PH, TOPK])
        topi = sb("topi", [P, PH, TOPK], U32)
        parts = sb("parts", [P, 2, PH * TOPK], U32)
        partsf = sb("partsf", [P, 2, PH * TOPK])
        idle = sb("idle", [P, 2])
        seq = sem("se_seq")
        block = ctx.enter_context(nc.Block())

        @block.sync
        def _(sp):
            for j in range(3):
                loop.load(sp, j, j)
            loop.run(sp, lambda g, first=False, last=False: loop.sync_step(sp, g, first, last))
            loop.finish_sync(sp)

        @block.scalar
        def _(act):
            loop.scalar_high(act, 0, 0, 0, False)

            def step(g, first=False, last=False):
                for b in range(4):
                    loop.scalar_tile(act, g, b, first, last)

            loop.run(act, step)

        @block.gpsimd
        def _(pool):
            loop.run(pool, lambda g, first=False, last=False: loop.pool_step(pool, g, first))

        @block.tensor
        def _(pe):
            def step(g, first=False, last=False):
                for b in range(4):
                    loop.tensor_tile(pe, g, b, first)

            loop.run(pe, step)

        @block.vector
        def _(dve):
            STEPS = 19
            iota16 = cst[:, C_IOTA:C_IOTA + TOPK]
            dve.memset(idle[:, :], 0.0)
            with dve.Fori(0, len(TILES)) as i:
                done = 0

                def after(ins, search=False):
                    nonlocal done
                    done += 1
                    ins.then_inc(seq, 1)
                    dve.wait_ge(seq, i * STEPS + done)
                    if search:
                        dve.tensor_copy(idle[:, 0:1], idle[:, 1:2])

                after(dve.tensor_copy(s[:, :, :], scores_sb[:, bass.ds(i, 1)].rearrange("p o c k -> p (o c) k")), True)
                for c in range(16):
                    ins = dve.max(best[:, c, 0:8], s[:, c, :])
                after(ins, True)
                for c in range(16):
                    dve.max_index(where[:, c, 0:8], best[:, c, 0:8], s[:, c, :])
                    ins = dve.match_replace(r[:, c, :], best[:, c, 0:8], s[:, c, :], LOWEST)
                after(ins, True)
                for c in range(16):
                    ins = dve.max(best[:, c, 8:16], r[:, c, :])
                after(ins, True)
                for c in range(16):
                    ins = dve.max_index(where[:, c, 8:16], best[:, c, 8:16], r[:, c, :])
                b4 = best[:, :, :].rearrange("p (h q) a -> p h q a", q=2)
                after(dve.tensor_tensor(cand[:, :, :].rearrange("p h (a b) -> p h a b", a=TOPK),
                                        last(b4[:, :, 0, :].unsqueeze(3), TOPK), over(b4[:, :, 1, :], 2, TOPK), ALU.add))
                dve.tensor_copy(wheref[:, :, :, :], where[:, :, :].rearrange("p (h q) a -> p h q a", q=2))
                for h in range(PH):
                    ins = dve.max(top[:, h, 0:8], cand[:, h, :])
                after(ins, True)
                rc = r[:, :, :].rearrange("p (h q) k -> p h (q k)", q=2)
                for h in range(PH):
                    dve.max_index(topi[:, h, 0:8], top[:, h, 0:8], cand[:, h, :])
                    ins = dve.match_replace(rc[:, h], top[:, h, 0:8], cand[:, h, :], LOWEST)
                after(ins, True)
                for h in range(PH):
                    ins = dve.max(top[:, h, 8:16], rc[:, h])
                after(ins, True)
                for h in range(PH):
                    ins = dve.max_index(topi[:, h, 8:16], top[:, h, 8:16], rc[:, h])
                after(ins, True)
                dve.tensor_tensor(drops[:, bass.ds(i, 1)].rearrange("p o (h a) -> p (o h) a", h=PH), top[:, :, :],
                                  last(top[:, :, 0:1], TOPK), ALU.subtract)
                flat = topi[:, :, :].rearrange("p h a -> p (h a)")
                dve.tensor_scalar(parts[:, 0], flat, 4, None, ALU.logical_shift_right)
                after(dve.tensor_scalar(parts[:, 1], flat, TOPK - 1, None, ALU.bitwise_and))
                after(dve.tensor_copy(partsf[:, :, :], parts[:, :, :]))
                eq = s[:, :, :].rearrange("p c k -> p (c k)").rearrange("p (j a) -> p j a", a=TOPK)
                for q in range(2):
                    after(dve.tensor_tensor(eq, last(partsf[:, q].unsqueeze(2), TOPK), over(iota16, 1, PH * TOPK),
                                            ALU.is_equal))
                    e4 = eq.rearrange("p (h j) a -> p h j a", h=PH)
                    after(dve.tensor_tensor(e4, e4, over(wheref[:, :, q, :], 2, TOPK), ALU.mult))
                    after(dve.tensor_reduce(picks[:, bass.ds(i, 1), q].rearrange("p o j -> p (o j)"), eq, AX, ALU.add))
                for _ in range(STEPS - done):
                    after(dve.tensor_copy(partsf[:, 0, 0:1], parts[:, 0, 0:1]))
                assert done == STEPS


def peer_spread(nc, io, sem, cst, ps, xhi, xlo, picks, drops):
    COUNT = 72
    with ExitStack() as ctx:
        def sb(name, shape, dt=F32):
            return ctx.enter_context(nc.sbuf_tensor("sp_" + name, shape, dt))

        loop = ExpertLoop(nc, ctx, sem, "sp_", io, 56, COUNT, ps, xhi, xlo)
        pickT = sb("pickT", [P, 4, NT])
        gate_hi = sb("gate_hi", [P, NT], F32R)
        cur = sb("cur", [P, 4, 32])
        hot1 = sb("hot1", [P, 2, 8, P], F32R)
        hot2 = sb("hot2", [P, 2, 2, 8, P], F32R)
        spread = sb("spread", [P, P, 32])
        total = sb("total", [P, 2, 5 * PH])
        exps, gates, turned, turned_out = sem("sp_exps"), sem("sp_gates"), sem("sp_turned"), sem("sp_turned_out")
        hots, spread_mm, spread_out, seq, cur_seq = (sem("sp_hots"), sem("sp_spread_mm"), sem("sp_spread_out"),
                                                     sem("sp_seq"), sem("sp_cur_seq"))
        spread_stored = sem("sp_spread_stored")
        ident = cst[:, C_ID:C_ID + P]
        iota = cst[:, C_IOTA:C_IOTA + P]
        block = ctx.enter_context(nc.Block())

        @block.sync
        def _(sp):
            for j in range(3):
                loop.load(sp, j, j)

            def store_spread(g):
                sp.wait_ge(spread_out, 4 * g + 4)
                sp.dma_start(io["gates"][g], spread[:, :, :]).then_inc(spread_stored, 16)

            def step(g, first=False, last=False):
                loop.sync_step(sp, g, first, last)
                if not last:
                    store_spread(g)

            loop.run(sp, step)
            loop.finish_sync(sp)
            store_spread(COUNT // 4 - 1)
            sp.wait_ge(spread_stored, 16 * (COUNT // 4))

        @block.scalar
        def _(act):
            act.activation(drops[:, :, :], drops[:, :, :], ACT.Exp).then_inc(exps, 1)
            loop.scalar_high(act, 0, 0, 0, False)

            def take(g, b, fresh=False):
                act.wait_ge(spread_mm, 4 * g + b + 1)
                if b == 0 and not fresh:
                    act.wait_ge(spread_stored, 16 * g)
                for x in range(2):
                    ins = act.copy(spread[:, :, 8 * b + 4 * x:8 * b + 4 * x + 4],
                                   ps[:, 4 + 2 * (b % 2) + x, :].rearrange("p (t e) -> p e t", t=4))
                ins.then_inc(spread_out, 1)

            def step(g, first=False, last=False):
                for b in range(4):
                    loop.scalar_tile(act, g, b, first, last)
                    if b:
                        take(g, b - 1, first)
                    elif not first:
                        take(g - 1, 3)

            loop.run(act, step)
            take(COUNT // 4 - 1, 3)

        @block.gpsimd
        def _(pool):
            loop.run(pool, lambda g, first=False, last=False: loop.pool_step(pool, g, first))

        @block.tensor
        def _(pe):
            pe.wait_ge(gates, 1)
            for i, (t0, n) in enumerate(TILES):
                if i >= 2:
                    pe.wait_ge(turned_out, i - 1)
                for q in range(3):
                    mm = pe.transpose(ps[:, 4 + i % 2, q * P:q * P + n], picks[0:n, i, q, :], ident[0:n, 0:n])
                mm.then_inc(turned, 1)
            pe.wait_ge(turned_out, len(TILES))

            def step(g, first=False, last=False):
                for b in range(4):
                    loop.tensor_tile(pe, g, b, first)
                    j = 4 * g + b
                    pe.wait_ge(hots, j + 1)
                    if not (first and b < 2):
                        pe.wait_ge(spread_out, j - 1)
                    for t in range(8):
                        for x in range(2):
                            mm = pe.matmul(ps[:, 4 + 2 * (b % 2) + t // 4, (t % 4) * P:(t % 4 + 1) * P],
                                           hot1[:, b % 2, t], hot2[:, b % 2, x, t], start=(x == 0), stop=(x == 1))
                    mm.then_inc(spread_mm, 1)

            loop.run(pe, step)

        @block.vector
        def _(dve):
            chain = Chain(dve, seq)
            dve.wait_ge(exps, 1)
            d3 = drops[:, :, :].rearrange("p i (h a) -> p (i h) a", a=TOPK)
            chain.after(dve.tensor_reduce(total[:, 0], d3, AX, ALU.add))
            chain.after(dve.reciprocal(total[:, 1], total[:, 0]))
            dve.tensor_tensor(picks[:, :, 2, :].rearrange("p i (h a) -> p i h a", a=TOPK),
                              drops[:, :, :].rearrange("p i (h a) -> p i h a", a=TOPK),
                              last(total[:, 1].rearrange("p (i h) -> p i h", h=PH).unsqueeze(3), TOPK),
                              ALU.mult).then_inc(gates, 1)
            for i, (t0, n) in enumerate(TILES):
                dve.wait_ge(turned, i + 1)
                dve.tensor_copy(pickT[:, 0:3, t0:t0 + n],
                                ps[:, 4 + i % 2, 0:3 * P].rearrange("p (q t) -> p q t", q=3)[:, :, 0:n]
                                ).then_inc(turned_out, 1)
            dve.wait_ge(turned_out, len(TILES))
            chain.after(dve.tensor_copy(gate_hi[:, :], pickT[:, 2, :]))
            chain.after(dve.tensor_tensor(pickT[:, 3, :], pickT[:, 2, :], gate_hi[:, :].bitcast(F32), ALU.subtract))
            chain.after(dve.tensor_copy(pickT[:, 2, :], gate_hi[:, :].bitcast(F32)))

            def step(g, first=False, last=False):
                if not first:
                    dve.wait_ge(hots, 4 * g)
                dve.tensor_copy(cur[:, :, :], pickT[:, :, bass.ds(32 * g, 32)]).then_inc(cur_seq, 1)
                dve.wait_ge(cur_seq, g + 1)
                for b in range(4):
                    j = 4 * g + b
                    if not (first and b < 2):
                        dve.wait_ge(spread_mm, j - 1)
                    for t in range(8):
                        c = 8 * b + t
                        dve.tensor_scalar(hot1[:, b % 2, t], iota, cur[:, 0, c:c + 1], None, ALU.is_equal)
                        for x in range(2):
                            ins = dve.tensor_scalar(hot2[:, b % 2, x, t], iota, cur[:, 1, c:c + 1],
                                                    cur[:, 2 + x, c:c + 1], ALU.is_equal, ALU.mult)
                    ins.then_inc(hots, 1)

            loop.run(dve, step)


def peer_output(nc, io, sem, hT, ps):
    GROUPS = NKEY // 4
    with ExitStack() as ctx:
        def sb(name, shape, dt=F32):
            return ctx.enter_context(nc.sbuf_tensor("po_" + name, shape, dt))

        v = sb("v", [P, 2, 2, D])
        w = sb("w", [P, 2, 4, NT])
        g_sb = sb("g", [P, 2, NT // 32, 4, 32])
        whi = sb("whi", [P, 2, 4, NT], F32R)
        wlo = sb("wlo", [P, 2, 4, NT], F32R)
        vhi = sb("vhi", [P, 2, 4, D], F32R)
        vlo = sb("vlo", [P, 2, 4, D], F32R)
        v_loaded = [sem(f"po_v_loaded{i}") for i in range(2)]
        hg_loaded = [sem(f"po_hg_loaded{i}") for i in range(2)]
        gg_loaded = [sem(f"po_gg_loaded{i}") for i in range(2)]
        v_high, v_low, weighted, w_high, w_low = (sem("po_v_high"), sem("po_v_low"), sem("po_weighted"),
                                                  sem("po_w_high"), sem("po_w_low"))
        products, added = sem("po_products"), sem("po_added")
        block = ctx.enter_context(nc.Block())
        v_dram = io["peer_v"].rearrange("(p e) d -> p e d", p=P)
        g_dram = io["gates"].rearrange("k p e t -> p k e t")

        def run(eng, step):
            step(0, first=True)
            with eng.Fori(1, GROUPS // 2 - 1) as u:
                step(u)
            step(GROUPS // 2 - 1, last=True)

        @block.sync
        def _(sp):
            def load(q, s, waits=True):
                for c in range(2):
                    if waits:
                        sp.wait_ge(v_low, 4 * q - 2 + 2 * c)
                    sp.dma_start(v[:, c], v_dram[:, bass.ds(4 * q + 2 * c, 2), :]).then_inc(v_loaded[c], 16)

            def load_w(q, s, waits=True):
                if waits:
                    sp.wait_ge(w_low, q - 1)
                sp.dma_start(w[:, s], io["acts"][q]).then_inc(hg_loaded[s], 16)
                sp.dma_start(g_sb[:, s], g_dram[:, :, bass.ds(4 * q, 4), :]).then_inc(gg_loaded[s], 16)

            load_w(0, 0, False)
            load(0, 0, False)
            load_w(1, 1, False)

            def step(u, first=False, last=False):
                load(2 * u + 1, 1)
                if not last:
                    load_w(2 * u + 2, 0)
                    load(2 * u + 2, 0)
                    load_w(2 * u + 3, 1)

            run(sp, step)

        @block.scalar
        def _(act):
            def split(q, u, s, free):
                if free:
                    act.wait_ge(products, 8 * q - 8)
                for b in range(4):
                    if b % 2 == 0:
                        act.wait_ge(v_loaded[b // 2], 16 * q + 16)
                    act.copy(vhi[:, s, b], v[:, b // 2, b % 2]).then_inc(v_high, 1)
                act.wait_ge(weighted, q + 1)
                act.copy(whi[:, s], w[:, s]).then_inc(w_high, 1)

            split(0, 0, 0, False)

            def step(u, first=False, last=False):
                split(2 * u + 1, u, 1, not first)
                if not last:
                    split(2 * u + 2, u + 1, 0, True)

            run(act, step)

        @block.gpsimd
        def _(pool):
            def split(q, s, free):
                if free:
                    pool.wait_ge(products, 8 * q - 8)
                for b in range(4):
                    pool.wait_ge(v_high, 4 * q + b + 1)
                    pool.tensor_tensor(vlo[:, s, b], v[:, b // 2, b % 2], vhi[:, s, b].bitcast(F32), ALU.subtract
                                       ).then_inc(v_low, 1)

            split(0, 0, False)

            def step(u, first=False, last=False):
                split(2 * u + 1, 1, not first)
                if not last:
                    split(2 * u + 2, 0, True)

            run(pool, step)

        @block.tensor
        def _(pe):
            def group(q, s, first=False):
                pe.wait_ge(v_low, 4 * q + 4)
                pe.wait_ge(w_low, q + 1)
                for m in range(KT):
                    if not (first and m < 4):
                        pe.wait_ge(added, 8 * q + m - 3)
                    for b in range(4):
                        for n, (x, y) in enumerate(((vhi, whi), (vhi, wlo), (vlo, whi))):
                            for a in range(2):
                                mm = pe.matmul(ps[:, 2 * (m % 4) + a, 0:HALF], x[:, s, b, m * P:(m + 1) * P],
                                               y[:, s, b, a * HALF:(a + 1) * HALF], start=(b == 0 and n == 0),
                                               stop=(b == 3 and n == 2))
                    mm.then_inc(products, 1)

            def step(u, first=False, last=False):
                group(2 * u, 0, first)
                group(2 * u + 1, 1)

            run(pe, step)

        @block.vector
        def _(dve):
            def weigh(q, u, s):
                dve.wait_ge(hg_loaded[s], 16 * u + 16)
                dve.wait_ge(gg_loaded[s], 16 * u + 16)
                for b in range(4):
                    x = w[:, s, b].rearrange("p (k t) -> p k t", t=32)
                    ins = dve.tensor_tensor(x, x, g_sb[:, s, :, b, :], ALU.mult)
                ins.then_inc(weighted, 1)

            def rest(q, s):
                dve.wait_ge(w_high, q + 1)
                dve.tensor_tensor(wlo[:, s], w[:, s], whi[:, s].bitcast(F32), ALU.subtract).then_inc(w_low, 1)

            def add(q, m):
                dve.wait_ge(products, 8 * q + m + 1)
                dve.tensor_tensor(in2(hT[:, m]), in2(hT[:, m]), pair(ps, m, NT), ALU.add).then_inc(added, 1)

            def group(q, after, u, s, prepare=True):
                if prepare:
                    weigh(after, u, s)
                for m in range(4):
                    add(q, m)
                if prepare:
                    rest(after, s)
                for m in range(4, KT):
                    add(q, m)

            weigh(0, 0, 0)
            rest(0, 0)

            def step(u, first=False, last=False):
                group(2 * u, 2 * u + 1, u, 1)
                group(2 * u + 1, 2 * u + 2, u + 1, 0, not last)

            run(dve, step)


def final_norm(nc, io, sem, hT, cst, gains, ps):
    with ExitStack() as ctx:
        nT = ctx.enter_context(nc.sbuf_tensor("fn_nT", [P, KT, NT], F32))
        rstd = ctx.enter_context(nc.sbuf_tensor("fn_rstd", [P, NT], F32))
        squares, sums, roots, normed = sem("fn_squares"), sem("fn_sums"), sem("fn_roots"), sem("fn_normed")
        dve_seq, stored = sem("fn_dve_seq"), sem("fn_stored")
        block = ctx.enter_context(nc.Block())

        @block.sync
        def _(sp):
            for k in range(2):
                sp.wait_ge(normed, 4 * k + 4)
                sp.dma_start(io["y"][:, 4 * k:4 * k + 4], nT[:, 4 * k:4 * k + 4]).then_inc(stored, 16)
            sp.wait_ge(stored, 32)

        @block.tensor
        def _(pe):
            norm_sums(pe, cst, nT, ps, NT, squares, sums)

        @block.scalar
        def _(act):
            norm_squares(act, hT, nT, squares)
            norm_root(act, cst, ps, NT, rstd, sums, roots)

        @block.vector
        def _(dve):
            norm_scale(dve, Chain(dve, dve_seq), gains, G_FINAL, hT, NT, rstd, nT, roots, normed)


def build(nc, io):
    with ExitStack() as ctx:
        def sb(name, shape, dt=F32):
            return ctx.enter_context(nc.sbuf_tensor(name, shape, dt))

        held = []

        def sem(name):
            held.append(nc.alloc_semaphore(name=name))
            return held[-1]

        def free_semaphores():
            nc.clear_and_free_semaphores(list(held))
            held.clear()
            nc.all_engine_barrier()

        ps = ctx.enter_context(nc.psum_tensor("ps", [P, 8, 512], F32))
        hT = sb("hT", [P, KT, NT])
        cst = sb("cst", [P, C_N])
        gains = sb("gains", [P, G_N])
        rows = sb("rows", [P, R_N])
        with ExitStack() as mixer:
            cT = mixer.enter_context(nc.sbuf_tensor("cT", [P, 16, NT], F32))
            zT = mixer.enter_context(nc.sbuf_tensor("zT", [P, H, NT], F32))
            vv = mixer.enter_context(nc.sbuf_tensor("vv", [P, 5, 512], F32))
            gate = mixer.enter_context(nc.sbuf_tensor("gate", [P, 5, 8], F32))
            mixer_inputs(nc, io, sem, hT, cst, gains, rows, ps, cT, zT, vv, gate)
            mixer_core(nc, io, sem, cst, gains, rows, ps, cT, zT, vv, gate)
            mixer_output(nc, io, sem, hT, ps, cT)
        free_semaphores()
        memory_attention(nc, io, sem, hT, cst, gains, ps)
        free_semaphores()
        with ExitStack() as peer:
            picks = peer.enter_context(nc.sbuf_tensor("picks", [P, 5, 3, P], F32))
            drops = peer.enter_context(nc.sbuf_tensor("drops", [P, 5, P], F32))
            xhi = peer.enter_context(nc.sbuf_tensor("xhi", [P, KT, NT], F32R))
            xlo = peer.enter_context(nc.sbuf_tensor("xlo", [P, KT, NT], F32R))
            with ExitStack() as select:
                scores_sb = select.enter_context(nc.sbuf_tensor("scores", [P, 5, 16, NKEY], F32))
                peer_scores(nc, io, sem, hT, cst, gains, ps, xhi, xlo, scores_sb)
                peer_select(nc, io, sem, cst, ps, xhi, xlo, scores_sb, picks, drops)
            peer_spread(nc, io, sem, cst, ps, xhi, xlo, picks, drops)
        peer_output(nc, io, sem, hT, ps)
        final_norm(nc, io, sem, hT, cst, gains, ps)


def feature_major(a):
    a = np.asarray(a)
    return np.ascontiguousarray(a.T.reshape(-1, P, a.shape[0]).transpose(1, 0, 2))


def token_major(a):
    return np.ascontiguousarray(a.transpose(2, 1, 0).reshape(a.shape[2], -1))


def layouts(x):
    g = lambda a: np.asarray(a).reshape(-1, P).T
    return {
        "xT": feature_major(np.concatenate([np.asarray(x["x_prompt"]).reshape(SEQ, D),
                                            np.asarray(x["x_sample"]).reshape(NS, D)])),
        "consts": constant_table(),
        "gains": np.ascontiguousarray(np.concatenate(
            [g(x[k]) for k in ("norm_mix_g", "norm_mem_g", "mem_norm_g", "norm_ffn_g", "final_norm_g", "o_norm_g")], 1)),
        "rows": np.concatenate([np.asarray(x[k]).reshape(-1) for k in
                                ("a_log", "dt_bias", "sg_ln_g", "sg_ln_b", "sg_b")]),
        "w_in": np.asarray(x["w_in"])[0],
        "w_out": np.asarray(x["w_out"])[0],
        "conv_w": np.ascontiguousarray(np.asarray(x["conv_w"])[0].T.reshape(QKV_TILES, P, CONV).transpose(1, 0, 2)),
        "state_conv": np.ascontiguousarray(np.asarray(x["state_conv"])[0].transpose(2, 0, 1)
                                           .reshape(QKV_TILES, P, NB, 3).transpose(1, 0, 2, 3)),
        "sg_wT": np.ascontiguousarray(np.asarray(x["sg_w"])[0].transpose(0, 2, 1)),
        "state_delta": np.asarray(x["state_delta"])[0],
        "memT": feature_major(np.asarray(x["mem_prompt"])[0]),
        **{k: np.asarray(x[k])[0] for k in ("w_mq", "w_mk", "w_mv", "w_mo")},
        "cacheT": np.ascontiguousarray(np.asarray(x["cache_mem_k"])[0].reshape(NB, MEM, KT, P).transpose(0, 3, 2, 1)),
        "cache_v": np.ascontiguousarray(np.asarray(x["cache_mem_v"])[0].reshape(NB, 2, P, D).transpose(0, 2, 1, 3)),
        "peer_wq": np.asarray(x["peer_wq"])[0],
        "keysT": np.ascontiguousarray(np.asarray(x["peer_keys"])[0].transpose(1, 3, 0, 2).reshape(P, PH, NKEY)),
        "uT": np.ascontiguousarray(np.asarray(x["peer_u"])[0].reshape(NKEY, NKEY, KT, P).transpose(1, 3, 2, 0)),
        "peer_v": np.asarray(x["peer_v"])[0],
    }


OUTPUTS = {
    "y": (P, KT, NT), "delta_prompt": (P, H, P), "conv_prompt": (P, QKV_TILES, 3), "mem_k": (P, KT, MEM),
    "mem_v": (P, 2, D), "delta_sample": (P, H, NB, P), "conv_sample": (P, QKV_TILES, NB, 3), "vrows": (NS, 512),
}


def make(nc, x):
    arrays = layouts(x)
    io = {n: nc.dram_tensor("in_" + n, list(a.shape), F32, kind="ExternalInput").ap() for n, a in arrays.items()}
    io |= {n: nc.dram_tensor("out_" + n, list(s), F32, kind="ExternalOutput").ap() for n, s in OUTPUTS.items()}
    io["acts"] = nc.dram_tensor("acts", [NKEY // 4, P, 4, NT], F32, kind="Internal").ap()
    io["gates"] = nc.dram_tensor("gates", [NT // 32, P, P, 32], F32, kind="Internal").ap()
    build(nc, io)
    return {"in_" + n: a for n, a in arrays.items()}


def kernel(**inputs):
    import concourse.bacc as bacc
    from concourse.bass_utils import run_bass_kernel_spmd

    nc = bacc.Bacc("TRN2", target_bir_lowering=False, num_devices=1)
    arrays = make(nc, inputs)
    r = run_bass_kernel_spmd(nc, [arrays], core_ids=[0]).results[0]
    o = {n: np.asarray(r["out_" + n]) for n in OUTPUTS}
    y = token_major(o["y"])
    rows_of = lambda a: a.transpose(2, 1, 0).reshape(a.shape[2], -1)
    return (
        y[:SEQ].reshape(1, SEQ, D),
        y[SEQ:].reshape(NB, DS, D),
        np.ascontiguousarray(o["delta_prompt"].transpose(1, 0, 2))[None, None],
        np.ascontiguousarray(rows_of(o["conv_prompt"])).reshape(1, 1, 3, -1),
        np.ascontiguousarray(token_major(o["mem_k"])).reshape(1, 1, MEM, 4, 256),
        np.ascontiguousarray(o["mem_v"].transpose(1, 0, 2)).reshape(1, 1, MEM, 4, 256),
        np.ascontiguousarray(o["delta_sample"].transpose(2, 1, 0, 3))[None],
        np.ascontiguousarray(o["conv_sample"].transpose(2, 3, 1, 0)).reshape(1, NB, 3, -1),
        o["vrows"].reshape(1, NB, DS, 512),
    )
```

```python
from contextlib import ExitStack

import numpy as np

import concourse.bass as bass
from concourse import mybir

F32 = mybir.dt.float32
F32R = mybir.dt.float32r
BF16 = mybir.dt.bfloat16
U32 = mybir.dt.uint32
ALU = mybir.AluOpType
ACT = mybir.ActivationFunctionType
AX = mybir.AxisListType.X

P = 128
D = 1024
KT = D // P
SEQ = 512
NB = 8
DS = 8
NS = NB * DS
NT = SEQ + NS
HALF = NT // 2
TILES = [(0, 128), (128, 128), (256, 128), (384, 128), (512, 64)]
H = 4
QKV_TILES = 12
CONV = 4
MEM = 256
NKEY = 128
PH = 8
TOPK = 16
EPS = 1e-6
LEVELS = 7
SAMPLE_LEVELS = 3

C_ID, C_INCL, C_STRICT, C_ONES, C_IOTA, C_LVL = 0, 128, 256, 384, 512, 640
C_INCLS = C_LVL + LEVELS * 128
C_STRICTS = C_INCLS + 64
C_BLKS = C_STRICTS + 64
C_ROWB = C_BLKS + 64
C_COLB = C_ROWB + 8
C_EPS = C_COLB + 512
C_N = C_EPS + 1

G_MIX, G_MEM, G_MEMKV, G_FFN, G_FINAL, G_O, G_N = 0, 8, 16, 24, 32, 40, 41
R_ALOG, R_DT, R_LNG, R_LNB, R_SGB, R_N = 0, 4, 8, 520, 1032, 1544


def constant_table():
    t = np.zeros((P, C_N), np.float32)
    s = np.arange(P)[:, None]
    c = np.arange(P)[None, :]
    t[:, C_ID:C_ID + P] = s == c
    t[:, C_INCL:C_INCL + P] = s <= c
    t[:, C_STRICT:C_STRICT + P] = s < c
    t[:, C_ONES:C_ONES + P] = 1
    t[:, C_IOTA:C_IOTA + P] = c
    for l in range(LEVELS):
        b = 1 << l
        t[:, C_LVL + l * P:C_LVL + (l + 1) * P] = (s // (2 * b) == c // (2 * b)) & (s // b % 2 == 0) & (c // b % 2 == 1)
    same = (s // DS == c // DS)[:, :NS]
    t[:, C_INCLS:C_INCLS + NS] = same & (s <= c)[:, :NS]
    t[:, C_STRICTS:C_STRICTS + NS] = same & (s < c)[:, :NS]
    t[:, C_BLKS:C_BLKS + NS] = same
    t[:, C_ROWB:C_ROWB + NB] = s // DS == np.arange(NB)[None, :]
    t[:, C_COLB:C_COLB + NB * NS] = (np.arange(NS)[None, :] // DS == np.arange(NB)[:, None]).reshape(1, -1)
    t[:, C_EPS] = EPS
    return t


def over(ap, axis, n):
    a = ap.unsqueeze(axis)
    shape = list(a.shape)
    shape[axis] = n
    return a.broadcast_to(shape)


def last(ap, n):
    return ap.broadcast_to(list(ap.shape)[:-1] + [n])


class Chain:

    def __init__(self, eng, sem):
        self.eng, self.sem, self.n = eng, sem, 0

    def after(self, ins):
        self.n += 1
        ins.then_inc(self.sem, 1)
        self.eng.wait_ge(self.sem, self.n)


def norm_squares(act, x, out, squares):
    for k in range(KT):
        act.activation(out[:, k, :], x[:, k, :], ACT.Square).then_inc(squares, 1)


def norm_sums(pe, cst, sq, ps, n, squares, sums, bank=0):
    for k in range(KT):
        pe.wait_ge(squares, k + 1)
        for a in range(2):
            mm = pe.matmul(ps[:, bank + a, 0:n // 2], cst[:, C_ONES:C_ONES + P], sq[:, k, a * n // 2:(a + 1) * n // 2],
                           start=(k == 0), stop=(k == KT - 1))
    mm.then_inc(sums, 1)


def norm_root(act, cst, ps, n, rstd, sums, roots, bank=0):
    act.wait_ge(sums, 1)
    act.activation(rstd[:, 0:n].rearrange("p (a n) -> p a n", a=2), ps[:, bank:bank + 2, 0:n // 2], ACT.Sqrt,
                   bias=cst[:, C_EPS:C_EPS + 1], scale=1.0 / D).then_inc(roots, 1)


def norm_scale(dve, chain, gains, g0, x, n, rstd, out, roots, normed, follow=None):
    dve.wait_ge(roots, 1)
    chain.after(dve.reciprocal(rstd[:, 0:n], rstd[:, 0:n]))
    for k in range(KT):
        dve.scalar_tensor_tensor(out=out[:, k, 0:n], in0=x[:, k, 0:n], scalar=gains[:, g0 + k:g0 + k + 1],
                                 in1=rstd[:, 0:n], op0=ALU.mult, op1=ALU.mult).then_inc(normed, 1)
        if follow and k >= 2:
            follow(k - 2)
    if follow:
        follow(KT - 2)
        follow(KT - 1)


def pair(ps, m, n):
    s = 2 * (m % 4)
    return ps[:, s:s + 2, 0:n // 2]


def in2(ap):
    return ap.rearrange("p (a n) -> p a n", a=2)


WHOLE = [(0, 0, HALF), (1, HALF, HALF)]


class SplitTiles:

    def __init__(self, nc, ctx, sem, name):
        sb = lambda n, s, dt=F32: ctx.enter_context(nc.sbuf_tensor(name + n, s, dt))
        self.raw = sb("w_raw", [P, 3, KT, P])
        self.hi = sb("w_hi", [P, 2, KT, P], F32R)
        self.lo = sb("w_lo", [P, 2, KT, P], F32R)
        self.loaded = [sem(f"{name}w_loaded{i}") for i in range(3)]
        self.high, self.low, self.used = sem(name + "w_high"), sem(name + "w_low"), sem(name + "w_used")

    def load(self, sp, m, src):
        if m >= 3:
            sp.wait_ge(self.low, m - 2)
        sp.dma_start(self.raw[:, m % 3], src).then_inc(self.loaded[m % 3], 16)

    def split_high(self, act, m):
        act.wait_ge(self.loaded[m % 3], 16 * (m // 3 + 1))
        if m >= 2:
            act.wait_ge(self.used, m - 1)
        act.copy(self.hi[:, m % 2], self.raw[:, m % 3]).then_inc(self.high, 1)

    def split_low(self, pool, m):
        pool.wait_ge(self.high, m + 1)
        if m >= 2:
            pool.wait_ge(self.used, m - 1)
        pool.tensor_tensor(self.lo[:, m % 2], self.raw[:, m % 3], self.hi[:, m % 2].bitcast(F32), ALU.subtract
                           ).then_inc(self.low, 1)

    def products(self, pe, m, ps, slot, xhi, xlo, chunks=WHOLE, parts=None):
        pe.wait_ge(self.low, m + 1)
        for k in range(KT):
            if parts is not None:
                pe.wait_ge(parts, k + 1)
            for n, (w, x) in enumerate(((self.hi, xhi), (self.hi, xlo), (self.lo, xhi))):
                for bank, c, size in chunks:
                    mm = pe.matmul(ps[:, 2 * slot + bank, 0:size], w[:, m % 2, k, :], x[:, k, c:c + size],
                                   start=(k == 0 and n == 0), stop=(k == KT - 1 and n == 2))
        mm.then_inc(self.used, 1)


def split_input_high(act, x, xhi, ready, high):
    for k in range(KT):
        act.wait_ge(ready, k + 1)
        act.copy(xhi[:, k, :], x[:, k, 0:xhi.shape[2]]).then_inc(high, 1)


def split_input_low(dve, x, xhi, xlo, high, low, k):
    dve.wait_ge(high, k + 1)
    dve.tensor_tensor(xlo[:, k, :], x[:, k, 0:xhi.shape[2]], xhi[:, k, :].bitcast(F32), ALU.subtract
                      ).then_inc(low, 1)


def mixer_inputs(nc, io, sem, hT, cst, gains, rows, ps, cT, zT, vv, gate):
    with ExitStack() as ctx:
        def sb(name, shape, dt=F32):
            return ctx.enter_context(nc.sbuf_tensor("in_" + name, shape, dt))

        nT = sb("nT", [P, KT, NT])
        nhi = sb("nhi", [P, KT, NT], F32R)
        nlo = sb("nlo", [P, KT, NT], F32R)
        rstd = sb("rstd", [P, 2, NT])
        gw = sb("gw", [P, 4, 20])
        st = sb("st", [P, 3, 20])
        pre = sb("pre", [P, 2, 3 + SEQ + NB * (3 + DS)])
        wab = sb("wab", [P, KT, 8])
        cw = sb("cw", [P, QKV_TILES, CONV])
        stc = sb("stc", [P, QKV_TILES, NB, 3])
        scn_p = sb("scn_p", [P, QKV_TILES, 3])
        scn_s = sb("scn_s", [P, QKV_TILES, NB, 3])
        tiles = SplitTiles(nc, ctx, sem, "in_")

        h_loaded, loaded = sem("in_h_loaded"), sem("in_loaded")
        squares, sums, roots, normed = sem("in_squares"), sem("in_sums"), sem("in_roots"), sem("in_normed")
        high, low = sem("in_high"), sem("in_low")
        made, taken = sem("in_made"), sem("in_taken")
        edges, convolved, silus = sem("in_edges"), sem("in_convolved"), sem("in_silus")
        l2_done = sem("in_l2_done")
        gate_exp_in, gate_exps, gate_ln_in, gate_lns = (sem("in_gate_exp_in"), sem("in_gate_exps"),
                                                        sem("in_gate_ln_in"), sem("in_gate_lns"))
        ln_vars, ln_roots, ln_done = sem("in_ln_vars"), sem("in_ln_roots"), sem("in_ln_done")
        dve_seq, act_seq, stored, zeroed = sem("in_dve_seq"), sem("in_act_seq"), sem("in_stored"), sem("in_zeroed")

        COLS = [i * P for i in range(12)] + [2568 + i * P for i in range(4)] + [2056 + i * P for i in range(4)] \
            + [1536 + i * P for i in range(4)]
        GV, U, Z = 12, 16, 20
        ITEMS = [("tile", 0), ("ab", 0)] + [("tile", m) for m in range(1, 13)]
        for x in range(3):
            ITEMS += [("l2", x), ("tile", 13 + x)]
        ITEMS += [("turn", x) for x in range(3)]
        for x in range(5):
            ITEMS += [("l2", 3 + x), ("tile", 16 + x)]
        ITEMS += [("tile", m) for m in range(21, 24)]
        place = {item: i for i, item in enumerate(ITEMS)}
        w_in = io["w_in"].rearrange("(k p) c -> p k c", p=P)
        ident = cst[:, C_ID:C_ID + P]
        block = ctx.enter_context(nc.Block())

        @block.sync
        def _(sp):
            for k in range(KT):
                sp.dma_start(hT[:, k, :], io["xT"][:, k, :]).then_inc(h_loaded, 16)
            sp.dma_start(cst[:, :], io["consts"]).then_inc(loaded, 16)
            sp.dma_start(gains[:, :], io["gains"]).then_inc(loaded, 16)
            sp.dma_start(wab[:, :, :], w_in[:, :, 2048:2056]).then_inc(loaded, 16)
            for m in range(3):
                tiles.load(sp, m, w_in[:, :, COLS[m]:COLS[m] + P])
            sp.dma_start(cw[:, :, :], io["conv_w"]).then_inc(loaded, 16)
            sp.dma_start(stc[:, :, :, :], io["state_conv"]).then_inc(loaded, 16)
            sp.dma_start(rows[:, :], io["rows"].partition_broadcast(P)).then_inc(loaded, 16)
            for m in range(3, len(COLS)):
                tiles.load(sp, m, w_in[:, :, COLS[m]:COLS[m] + P])
            sp.wait_ge(edges, 2 + QKV_TILES)
            sp.dma_start(io["conv_prompt"], scn_p[:, :, :]).then_inc(stored, 16)
            sp.dma_start(io["conv_sample"], scn_s[:, :, :, :]).then_inc(stored, 16)
            sp.wait_ge(ln_done, 1)
            sp.dma_start(io["vrows"], vv[0:NS, 4, :]).then_inc(stored, 16)
            sp.wait_ge(stored, 48)

        @block.gpsimd
        def _(pool):
            for m in range(len(COLS)):
                tiles.split_low(pool, m)

        @block.tensor
        def _(pe):
            pe.wait_ge(loaded, 96)
            norm_sums(pe, cst, nT, ps, NT, squares, sums)
            for i, (kind, x) in enumerate(ITEMS):
                slot = i % 4
                if i >= 4:
                    pe.wait_ge(taken, i - 3)
                if kind == "ab":
                    for t, (t0, n) in enumerate(TILES):
                        for k in range(KT):
                            mm = pe.matmul(ps[0:n, 2 * slot, t * 8:t * 8 + 8], nT[:, k, t0:t0 + n], wab[:, k, :],
                                           start=(k == 0), stop=(k == KT - 1))
                    mm.then_inc(made, 1)
                elif kind == "tile":
                    tiles.products(pe, x, ps, slot, nhi, nlo, parts=low if x == 0 else None)
                elif kind == "l2":
                    pe.wait_ge(silus, x + 1)
                    for a in range(2):
                        mm = pe.matmul(ps[:, 2 * slot + a, 0:HALF], cst[:, C_ONES:C_ONES + P],
                                       nT[:, x, a * HALF:(a + 1) * HALF], start=True, stop=True)
                    mm.then_inc(made, 1)
                else:
                    pe.wait_ge(taken, place["tile", GV + 3] + 1)
                    for a, (t0, n) in enumerate(TILES[2 * x:2 * x + 2]):
                        for g in range(4):
                            mm = pe.transpose(ps[0:n, 2 * slot + a, g * P:g * P + P], zT[:, g, t0:t0 + n], ident)
                    mm.then_inc(made, 1)

        @block.scalar
        def _(act):
            chain = Chain(act, act_seq)
            act.wait_ge(h_loaded, 16 * KT)
            norm_squares(act, hT, nT, squares)
            act.wait_ge(loaded, 96)
            norm_root(act, cst, ps, NT, rstd[:, 0], sums, roots)
            tiles.split_high(act, 0)
            split_input_high(act, nT, nhi, normed, high)
            act.wait_ge(zeroed, 1)

            def silu(m):
                act.wait_ge(convolved, m + 1)
                chain.after(act.activation(cT[:, m, :], cT[:, m, :], ACT.Silu))
                if m < 8:
                    act.activation(nT[:, m, :], cT[:, m, :], ACT.Square).then_inc(silus, 1)

            others = 0
            for i, (kind, x) in enumerate(ITEMS):
                s = 2 * (i % 4)
                if kind == "tile":
                    if x + 1 < len(COLS):
                        tiles.split_high(act, x + 1)
                    act.wait_ge(tiles.used, x + 1)
                else:
                    others += 1
                    act.wait_ge(made, others)
                if kind == "ab":
                    act.copy(gate[:, 0:4, :], ps[:, s, 0:32].rearrange("p (i c) -> p i c", c=8))
                    act.copy(gate[0:NS, 4, :], ps[0:NS, s, 32:40]).then_inc(taken, 1)
                elif kind == "l2":
                    if x >= 2:
                        act.wait_ge(l2_done, x - 1)
                    act.activation(in2(rstd[:, x % 2, :]), ps[:, s:s + 2, 0:HALF], ACT.Sqrt,
                                   bias=cst[:, C_EPS:C_EPS + 1], scale=1.0).then_inc(taken, 1)
                elif kind == "turn":
                    for a, (t0, n) in enumerate(TILES[2 * x:2 * x + 2]):
                        ins = act.copy(vv[0:n, 2 * x + a, :], ps[0:n, s + a, :])
                    ins.then_inc(taken, 1)
                elif x < QKV_TILES:
                    act.wait_ge(edges, x + 1)
                    act.copy(pre[:, x % 2, 3:3 + HALF], ps[:, s, 0:HALF])
                    act.copy(pre[:, x % 2, 3 + HALF:3 + SEQ], ps[:, s + 1, 0:SEQ - HALF])
                    act.copy(pre[:, x % 2, 3 + SEQ:].rearrange("p (b t) -> p b t", t=3 + DS)[:, :, 3:],
                             ps[:, s + 1, SEQ - HALF:HALF].rearrange("p (b t) -> p b t", t=DS)).then_inc(taken, 1)
                else:
                    out, fn = {GV: (zT[:, x % 4], ACT.Gelu_apprx_tanh), U: (cT[:, 12 + x % 4], ACT.Gelu_apprx_tanh),
                               Z: (zT[:, x % 4], ACT.Silu)}[x // 4 * 4]
                    act.activation(in2(out), ps[:, s:s + 2, 0:HALF], fn).then_inc(taken, 1)
                if kind == "tile" and 1 <= x <= QKV_TILES:
                    silu(x - 1)
            act.wait_ge(ln_vars, 1)
            act.activation(st[:, 1, :], st[:, 1, :], ACT.Sqrt, bias=cst[:, C_EPS:C_EPS + 1],
                           scale=1.0 / P).then_inc(ln_roots, 1)
            act.wait_ge(gate_exp_in, 1)
            act.activation(gw[:, 1, :], gw[:, 1, :], ACT.Exp)
            act.activation(rows[:, R_ALOG:R_ALOG + 4], rows[:, R_ALOG:R_ALOG + 4], ACT.Exp)
            act.activation(gw[:, 3, :].rearrange("p (i h) -> p i h", h=4), gate[:, :, 0:4],
                           ACT.Sigmoid).then_inc(gate_exps, 1)
            act.wait_ge(gate_ln_in, 1)
            act.activation(gw[:, 2, :], gw[:, 2, :], ACT.Ln).then_inc(gate_lns, 1)

        @block.vector
        def _(dve):
            chain = Chain(dve, dve_seq)
            dve.memset(vv[:, 4, :], 0.0)
            dve.memset(pre[:, :, 0:3], 0.0)
            dve.memset(gate[:, 4, :], 0.0).then_inc(zeroed, 1)
            dve.wait_ge(h_loaded, 16 * KT)
            dve.wait_ge(loaded, 96)
            for b in range(2):
                dve.tensor_copy(pre[:, b, 3 + SEQ:].rearrange("p (b t) -> p b t", t=3 + DS)[:, :, 0:3],
                                stc[:, b]).then_inc(edges, 1)
            norm_scale(dve, chain, gains, G_MIX, hT, NT, rstd[:, 0], nT, roots, normed,
                       lambda k: split_input_low(dve, nT, nhi, nlo, high, low, k))
            for m in range(QKV_TILES):
                dve.wait_ge(taken, place["tile", m] + 1)
                pp = pre[:, m % 2, 0:3 + SEQ]
                sm = pre[:, m % 2, 3 + SEQ:].rearrange("p (b t) -> p b t", t=3 + DS)
                yp, ys = cT[:, m, 0:SEQ], cT[:, m, SEQ:].rearrange("p (b t) -> p b t", t=DS)
                dve.tensor_scalar(yp, pp[:, 0:SEQ], cw[:, m, 0:1], None, ALU.mult)
                chain.after(dve.tensor_scalar(ys, sm[:, :, 0:DS], cw[:, m, 0:1], None, ALU.mult))
                for j in range(1, CONV):
                    dve.scalar_tensor_tensor(out=yp, in0=pp[:, j:j + SEQ], scalar=cw[:, m, j:j + 1], in1=yp,
                                             op0=ALU.mult, op1=ALU.add)
                    ins = dve.scalar_tensor_tensor(out=ys, in0=sm[:, :, j:j + DS], scalar=cw[:, m, j:j + 1], in1=ys,
                                                   op0=ALU.mult, op1=ALU.add)
                    if j < CONV - 1:
                        chain.after(ins)
                ins.then_inc(convolved, 1)
                dve.tensor_copy(scn_p[:, m, :], pp[:, SEQ:SEQ + 3])
                ins = dve.tensor_copy(scn_s[:, m], sm[:, :, DS:DS + 3])
                if m + 2 < QKV_TILES:
                    chain.after(ins)
                    ins = dve.tensor_copy(sm[:, :, 0:3], stc[:, m + 2])
                ins.then_inc(edges, 1)
            g5 = lambda r: gw[:, r, :].rearrange("p (i h) -> p i h", h=4)
            chain.after(dve.tensor_tensor(g5(0), gate[:, :, 4:8], over(rows[:, R_DT:R_DT + 4], 1, 5), ALU.add))
            chain.after(dve.tensor_scalar(gw[:, 1, :], gw[:, 0, :], -1.0, None, ALU.mult))
            dve.tensor_tensor(gw[:, 1, :], gw[:, 0, :], gw[:, 1, :], ALU.min).then_inc(gate_exp_in, 1)
            for m in range(8):
                dve.wait_ge(taken, place["l2", m] + 1)
                chain.after(dve.reciprocal(rstd[:, m % 2, :], rstd[:, m % 2, :]))
                dve.scalar_tensor_tensor(out=cT[:, m, :], in0=cT[:, m, :], scalar=float(P) ** -0.5 if m < 4 else 1.0,
                                         in1=rstd[:, m % 2, :], op0=ALU.mult, op1=ALU.mult).then_inc(l2_done, 1)
            v3 = vv[:, :, :].rearrange("p i (g c) -> p (i g) c", g=4)
            sqv = nT[:, :, :].rearrange("p k n -> p (k n)")[:, 0:20 * P].rearrange("p (i c) -> p i c", i=20)
            chain.after(dve.tensor_reduce(st[:, 0, :], v3, AX, ALU.add))
            chain.after(dve.tensor_scalar(st[:, 0, :], st[:, 0, :], 1.0 / P, None, ALU.mult))
            chain.after(dve.tensor_tensor(v3, v3, last(st[:, 0, :].unsqueeze(2), P), ALU.subtract))
            chain.after(dve.tensor_tensor(sqv, v3, v3, ALU.mult))
            dve.tensor_reduce(st[:, 1, :], sqv, AX, ALU.add).then_inc(ln_vars, 1)
            dve.wait_ge(ln_roots, 1)
            chain.after(dve.reciprocal(st[:, 2, :], st[:, 1, :]))
            chain.after(dve.tensor_tensor(v3, v3, last(st[:, 2, :].unsqueeze(2), P), ALU.mult))
            chain.after(dve.tensor_tensor(vv[:, :, :], vv[:, :, :], over(rows[:, R_LNG:R_LNG + 512], 1, 5), ALU.mult))
            dve.tensor_tensor(vv[:, :, :], vv[:, :, :], over(rows[:, R_LNB:R_LNB + 512], 1, 5),
                              ALU.add).then_inc(ln_done, 1)
            dve.wait_ge(gate_exps, 1)
            dve.tensor_scalar(gw[:, 2, :], gw[:, 1, :], 1.0, None, ALU.add).then_inc(gate_ln_in, 1)
            dve.wait_ge(gate_lns, 1)
            dve.tensor_copy(gate[:, :, 4:8], g5(3))
            chain.after(dve.scalar_tensor_tensor(out=gw[:, 0, :], in0=gw[:, 0, :], scalar=0.0, in1=gw[:, 2, :],
                                                 op0=ALU.max, op1=ALU.add))
            chain.after(dve.scalar_tensor_tensor(out=gate[:, :, 0:4], in0=g5(0), scalar=-1.0,
                                                 in1=over(rows[:, R_ALOG:R_ALOG + 4], 1, 5),
                                                 op0=ALU.mult, op1=ALU.mult))


def mixer_core(nc, io, sem, cst, gains, rows, ps, cT, zT, vv, gate):
    NTILE = len(TILES)
    with ExitStack() as ctx:
        def sb(name, shape, dt=F32):
            return ctx.enter_context(nc.sbuf_tensor("dl_" + name, shape, dt))

        wT = sb("wT", [P, 4, P])
        wS = sb("wS", [NS, 4, NS])
        S0 = sb("S0", [P, H, NB, P])
        cols = sb("cols", [P, 5, 8])
        ecols = sb("ecols", [P, 5, 4, H])
        egr = sb("egr", [P, H, P])
        egl = sb("egl", [P, 4, H])
        egls = sb("egls", [P, H, NB])
        dec = sb("dec", [P, H, P])
        MT = sb("MT", [P, 5, H, P])
        QK = sb("QK", [P, 5, H, P])
        kd = sb("kd", [P, 5, H, P])
        bv = sb("bv", [P, 5, H, P])
        Dm = sb("Dm", [P, 5, H, P])
        Em = sb("Em", [P, 5, H, P])
        Mb = sb("Mb", [P, 3, H, P])
        X = sb("X", [P, 2, H, P])
        R = sb("R", [P, H, P])
        vn = sb("vn", [P, 2, H, P])
        S = sb("S", [P, 2, H, P])
        km = Dm[:, 0:4].rearrange("p a h c -> p (a h c)")[:, 0:2 * NB * NS].rearrange("p (a b t) -> p a b t", a=2, b=NB)
        vm = MT[0:NS, 0:4].rearrange("p a h c -> p (a h c)").rearrange("p (a b v) -> p a b v", a=2, b=NB)
        tmp = sb("tmp", [P, 2, 512])
        rstd = sb("rstd", [P, 2, NT])

        loaded, wS_zero, wS_loaded, states = (sem("dl_loaded"), sem("dl_wS_zero"), sem("dl_wS_loaded"),
                                              sem("dl_states"))
        prep_mm, act_a, dve_a, act_b, prep_done = (sem("dl_prep_mm"), sem("dl_act_a"), sem("dl_dve_a"),
                                                   sem("dl_act_b"), sem("dl_prep_done"))
        masked, x_mm, x_out, de_mm, de_done = (sem("dl_masked"), sem("dl_x_mm"), sem("dl_x_out"), sem("dl_de_mm"),
                                               sem("dl_de_done"))
        sg_masked, sg_mm, sg_done = sem("dl_sg_masked"), sem("dl_sg_mm"), sem("dl_sg_done")
        ks_mm, r_ready, vn_mm, vn_ready, o_mm, o_out, ds_mm, s_ready = (
            sem("dl_ks_mm"), sem("dl_r_ready"), sem("dl_vn_mm"), sem("dl_vn_ready"), sem("dl_o_mm"), sem("dl_o_out"),
            sem("dl_ds_mm"), sem("dl_s_ready"))
        km_ready, ks_done, vm_ready, ss_mm, ss_done = (sem("dl_km_ready"), sem("dl_ks_done"), sem("dl_vm_ready"),
                                                       sem("dl_ss_mm"), sem("dl_ss_done"))
        o_sq, o_sum, o_root, o_done = sem("dl_o_sq"), sem("dl_o_sum"), sem("dl_o_root"), sem("dl_o_done")
        dve_seq, act_seq, stored = sem("dl_dve_seq"), sem("dl_act_seq"), sem("dl_stored")
        ident_ready = sem("dl_ident_ready")

        STEPS = [(l, i) for l in range(LEVELS) for i in range(NTILE) if l < SAMPLE_LEVELS or i < 4]

        def previous(j):
            l, i = STEPS[j]
            return STEPS.index((l - 1, i)) if l else None

        lvl = lambda l, n: cst[0:n, C_LVL + l * P:C_LVL + l * P + n]
        ident = cst[:, C_ID:C_ID + P]
        block = ctx.enter_context(nc.Block())

        @block.sync
        def _(sp):
            sp.dma_start(wT[:, :, :], io["sg_wT"].rearrange("g s t -> s g t")).then_inc(loaded, 16)
            sp.wait_ge(wS_zero, 1)
            for b in range(NB):
                sp.dma_start(wS[b * DS:(b + 1) * DS, :, b * DS:(b + 1) * DS],
                             io["sg_wT"][:, 0:DS, 0:DS].rearrange("g s t -> s g t")).then_inc(wS_loaded, 16)
            for h in range(H):
                sp.dma_start(S0[:, h], io["state_delta"][:, h].rearrange("b k v -> k b v")).then_inc(states, 16)
            sp.wait_ge(s_ready, 4)
            sp.dma_start(io["delta_prompt"], S[:, 1]).then_inc(stored, 16)
            for h in range(H):
                sp.wait_ge(ss_done, 2 * h + 2)
                sp.dma_start(io["delta_sample"][:, h], S0[:, h]).then_inc(stored, 16)
            sp.wait_ge(stored, 16 * 5)

        @block.gpsimd
        def _(pool):
            pool.memset(wS[:, :, :], 0.0).then_inc(wS_zero, 1)
            for i, (t0, n) in enumerate(TILES):
                pool.tensor_copy(Dm[0:n, i, :, 0:n], over(ident[0:n, 0:n], 1, H))
                ins = pool.tensor_copy(Em[0:n, i, :, 0:n], over(ident[0:n, 0:n], 1, H))
            ins.then_inc(ident_ready, 1)
            for j, (l, i) in enumerate(STEPS):
                n = TILES[i][1]
                if l == 0:
                    pool.wait_ge(prep_done, i + 1)
                if j >= 3:
                    pool.wait_ge(x_mm, j - 2)
                pool.tensor_tensor(Mb[0:n, j % 3, :, 0:n], MT[0:n, i, :, 0:n], over(lvl(l, n), 1, H),
                                   ALU.mult).then_inc(masked, 1)

        @block.tensor
        def _(pe):
            for i, (t0, n) in enumerate(TILES):
                incl = cst[0:n, C_INCL:C_INCL + n] if n == P else cst[0:n, C_INCLS:C_INCLS + n]
                blk = cst[0:n, C_ONES:C_ONES + n] if n == P else cst[0:n, C_BLKS:C_BLKS + n]
                if i:
                    pe.wait_ge(prep_done, i)
                for h in range(H):
                    pe.matmul(ps[:, 0, h * n:h * n + n], gate[0:n, i, h:h + 1].broadcast_to([n, P]), incl,
                              start=True, stop=True)
                    pe.matmul(ps[:, 1, h * n:h * n + n], gate[0:n, i, 4 + h:5 + h].broadcast_to([n, P]),
                              ident[0:n, 0:n], start=True, stop=True)
                pe.matmul(ps[0:n, 2, 0:4], incl, gate[0:n, i, 0:4], start=True, stop=True)
                pe.matmul(ps[0:n, 2, 4:8], blk, gate[0:n, i, 0:4], start=True, stop=True)
                for h in range(H):
                    q, k, v = (cT[:, 4 * x + h, t0:t0 + n] for x in range(3))
                    pe.matmul(ps[0:n, 3, h * n:h * n + n], k, k, start=True, stop=True)
                    pe.matmul(ps[0:n, 4, h * n:h * n + n], k, q, start=True, stop=True)
                    pe.transpose(ps[0:n, 5, h * P:h * P + P], v, ident)
                    mm = pe.transpose(ps[0:n, 6, h * P:h * P + P], k, ident)
                mm.then_inc(prep_mm, 1)
            pe.wait_ge(prep_done, NTILE)
            pe.wait_ge(sg_masked, 1)
            for i, (t0, n) in enumerate(TILES):
                w = wT if n == P else wS
                if i >= 2:
                    pe.wait_ge(sg_done, i - 1)
                for g in range(4):
                    mm = pe.matmul(ps[:, 6 + i % 2, g * n:g * n + n], vv[0:n, i, g * P:g * P + P], w[0:n, g, 0:n],
                                   start=True, stop=True)
                mm.then_inc(sg_mm, 1)

            def x_step(j):
                l, i = STEPS[j]
                n = TILES[i][1]
                pe.wait_ge(masked, j + 1)
                if l == 0:
                    pe.wait_ge(ident_ready, 1)
                else:
                    pe.wait_ge(de_done, previous(j) + 1)
                if j >= 2:
                    pe.wait_ge(x_out, j - 1)
                for h in range(H):
                    mm = pe.matmul(ps[0:n, j % 2, h * n:h * n + n], Mb[0:n, j % 3, h, 0:n], Dm[0:n, i, h, 0:n],
                                   start=True, stop=True)
                mm.then_inc(x_mm, 1)

            def de_step(j):
                l, i = STEPS[j]
                n = TILES[i][1]
                pe.wait_ge(x_out, j + 1)
                if j >= 2:
                    pe.wait_ge(de_done, j - 1)
                for h in range(H):
                    pe.matmul(ps[0:n, 2 + j % 2, h * n:h * n + n], Em[0:n, i, h, 0:n], X[0:n, j % 2, h, 0:n],
                              start=True, stop=True)
                    mm = pe.matmul(ps[0:n, 4 + j % 2, h * n:h * n + n], X[0:n, j % 2, h, 0:n], Em[0:n, i, h, 0:n],
                                   start=True, stop=True)
                mm.then_inc(de_mm, 1)

            for j in range(len(STEPS) + 1):
                if j < len(STEPS):
                    x_step(j)
                if j:
                    de_step(j - 1)
            pe.wait_ge(de_done, len(STEPS))
            pe.wait_ge(sg_done, NTILE)

            for i in range(4):
                t0 = i * P
                if i:
                    pe.wait_ge(s_ready, i)
                    for h in range(H):
                        mm = pe.matmul(ps[:, 0, h * P:h * P + P], cT[:, 4 + h, t0:t0 + P], S[:, (i - 1) % 2, h],
                                       start=True, stop=True)
                    mm.then_inc(ks_mm, 1)
                pe.wait_ge(r_ready, i + 1)
                for h in range(H):
                    mm = pe.matmul(ps[:, 1, h * P:h * P + P], Em[:, i, h], R[:, h] if i else bv[:, 0, h],
                                   start=True, stop=True)
                mm.then_inc(vn_mm, 1)
                pe.wait_ge(vn_ready, i + 1)
                for h in range(H):
                    mm = pe.matmul(ps[:, 3, h * P:h * P + P], kd[:, i, h], vn[:, i % 2, h], start=True, stop=True)
                mm.then_inc(ds_mm, 1)
                if i:
                    pe.wait_ge(o_out, i)
                for h in range(H):
                    mm = pe.matmul(ps[:, 2, h * P:h * P + P], vn[:, i % 2, h], QK[:, i, h], start=True, stop=(i == 0))
                    if i:
                        mm = pe.matmul(ps[:, 2, h * P:h * P + P], S[:, (i - 1) % 2, h], cT[:, h, t0:t0 + P],
                                       start=False, stop=True)
                mm.then_inc(o_mm, 1)

            pe.wait_ge(states, 16 * H)
            for h in range(H):
                pe.wait_ge(km_ready, h + 1)
                for b in range(NB):
                    mm = pe.matmul(ps[0:NS, 0, h * P:h * P + P], km[:, h % 2, b], S0[:, h, b],
                                   start=(b == 0), stop=(b == NB - 1))
                mm.then_inc(ks_done, 1)
            pe.wait_ge(r_ready, 5)
            for h in range(H):
                mm = pe.matmul(ps[0:NS, 1, h * P:h * P + P], Em[0:NS, 4, h, 0:NS], R[0:NS, h], start=True, stop=True)
            mm.then_inc(vn_mm, 1)
            pe.wait_ge(vn_ready, 5)
            pe.wait_ge(o_out, 4)
            for h in range(H):
                pe.matmul(ps[:, 2, h * NS:h * NS + NS], vn[0:NS, 0, h], QK[0:NS, 4, h, 0:NS], start=True, stop=False)
                for b in range(NB):
                    c = b * DS
                    mm = pe.matmul(ps[:, 2, h * NS + c:h * NS + c + DS], S0[:, h, b], cT[:, h, SEQ + c:SEQ + c + DS],
                                   start=False, stop=(b == NB - 1))
            mm.then_inc(o_mm, 1)
            for h in range(H):
                pe.wait_ge(vm_ready, h + 1)
                for a in range(2):
                    if h >= 2:
                        pe.wait_ge(ss_done, 2 * (h - 2) + 2)
                    mm = pe.matmul(ps[:, 4 + 2 * (h % 2) + a, 0:512], kd[0:NS, 4, h],
                                   vm[:, h % 2, 4 * a:4 * a + 4].rearrange("p b v -> p (b v)"), start=True, stop=True)
                mm.then_inc(ss_mm, 1)
            for h in range(H):
                pe.wait_ge(o_sq, h + 1)
                if h == 0:
                    pe.wait_ge(o_out, 5)
                    pe.wait_ge(r_ready, 5)
                    pe.wait_ge(ss_done, 2 * H)
                for a in range(2):
                    mm = pe.matmul(ps[:, 2 * h + a, 0:HALF], cst[:, C_ONES:C_ONES + P],
                                   cT[:, h, a * HALF:(a + 1) * HALF], start=True, stop=True)
                mm.then_inc(o_sum, 1)

        @block.scalar
        def _(act):
            for i, (t0, n) in enumerate(TILES):
                act.wait_ge(prep_mm, i + 1)
                if i:
                    act.wait_ge(prep_done, i)
                act.copy(cols[0:n, i, :], ps[0:n, 2, 0:8])
                act.activation(ecols[0:n, i, 0, :], ps[0:n, 2, 0:4], ACT.Exp)
                act.activation(egr[:, :, 0:n], ps[:, 0, 0:H * n].rearrange("p (h n) -> p h n", h=H),
                               ACT.Exp).then_inc(act_a, 1)
                act.wait_ge(dve_a, i + 1)
                act.activation(dec[0:n, :, 0:n], dec[0:n, :, 0:n], ACT.Exp)
                act.activation(ecols[0:n, i, 2, :], ecols[0:n, i, 1, :], ACT.Exp).then_inc(act_b, 1)
            for j, (l, i) in enumerate(STEPS):
                n = TILES[i][1]
                act.wait_ge(x_mm, j + 1)
                if j >= 2:
                    act.wait_ge(de_mm, j - 1)
                act.copy(X[0:n, j % 2, :, 0:n], ps[0:n, j % 2, 0:H * n].rearrange("p (h n) -> p h n", h=H)
                         ).then_inc(x_out, 1)
            for i in range(5):
                t0, n = TILES[i]
                act.wait_ge(vn_mm, i + 1)
                if i >= 2:
                    act.wait_ge(o_mm, i - 1)
                act.copy(vn[0:n, i % 2, :, :], ps[0:n, 1, 0:512].rearrange("p (h v) -> p h v", h=H)
                         ).then_inc(vn_ready, 1)
                act.wait_ge(o_mm, i + 1)
                act.copy(cT[:, 8:12, t0:t0 + n], ps[:, 2, 0:H * n].rearrange("p (h n) -> p h n", h=H)
                         ).then_inc(o_out, 1)
            act.wait_ge(o_out, 5)
            for h in range(H):
                act.activation(cT[:, h], cT[:, 8 + h], ACT.Square).then_inc(o_sq, 1)
            for h in range(H):
                act.wait_ge(o_sum, h + 1)
                if h >= 2:
                    act.wait_ge(o_done, h - 1)
                act.activation(in2(rstd[:, h % 2]), pair(ps, h, NT), ACT.Sqrt, bias=cst[:, C_EPS:C_EPS + 1],
                               scale=1.0 / P).then_inc(o_root, 1)

        @block.vector
        def _(dve):
            chain = Chain(dve, dve_seq)
            hn = lambda bank, n, p=P: ps[0:p, bank, 0:H * n].rearrange("p (h n) -> p h n", h=H)
            for i, (t0, n) in enumerate(TILES):
                beta, gc = gate[0:n, i, 4:8], cols[0:n, i, 0:4]
                dve.wait_ge(act_a, i + 1)
                for h in range(H):
                    dve.tensor_scalar(dec[0:n, h, 0:n], ps[0:n, 0, h * n:h * n + n], cols[0:n, i, h:h + 1], 0.0,
                                      ALU.subtract, ALU.min)
                dve.tensor_tensor(ecols[0:n, i, 1, :], cols[0:n, i, 4:8], gc, ALU.subtract).then_inc(dve_a, 1)
                dve.tensor_tensor(bv[0:n, i], hn(5, P, n), last(beta.unsqueeze(2), P), ALU.mult)
                dve.tensor_tensor(cT[:, 0:4, t0:t0 + n], cT[:, 0:4, t0:t0 + n], egr[:, :, 0:n], ALU.mult)
                dve.tensor_tensor(ecols[0:n, i, 3, :], beta, ecols[0:n, i, 0, :], ALU.mult)
                if n == P:
                    dve.tensor_copy(egl[:, i, :], egr[:, :, P - 1])
                else:
                    dve.tensor_copy(egls[:, :, :], egr[:, :, DS - 1:NS:DS])
                dve.wait_ge(act_b, i + 1)
                d = dec[0:n, :, 0:n]
                m = cst[0:n, C_INCL:C_INCL + n] if n == P else cst[0:n, C_INCLS:C_INCLS + n]
                chain.after(dve.tensor_tensor(d, d, over(m, 1, H), ALU.mult))
                dve.tensor_tensor(QK[0:n, i, :, 0:n], hn(4, n, n), d, ALU.mult)
                chain.after(dve.tensor_tensor(MT[0:n, i, :, 0:n], hn(3, n, n), d, ALU.mult))
                dve.tensor_tensor(MT[0:n, i, :, 0:n], MT[0:n, i, :, 0:n], hn(1, n, n), ALU.mult)
                dve.tensor_tensor(kd[0:n, i], hn(6, P, n), last(ecols[0:n, i, 2, :].unsqueeze(2), P),
                                  ALU.mult).then_inc(prep_done, 1)
            dve.wait_ge(loaded, 16)
            dve.wait_ge(wS_loaded, 16 * NB)
            dve.tensor_tensor(wT[:, :, :], wT[:, :, :], over(cst[:, C_INCL:C_INCL + P], 1, 4), ALU.mult)
            dve.tensor_tensor(wS[:, :, :], wS[:, :, :], over(cst[0:NS, C_INCLS:C_INCLS + NS], 1, 4),
                              ALU.mult).then_inc(sg_masked, 1)
            bias = rows[:, R_SGB:R_SGB + 512].rearrange("p (g t) -> p g t", g=4)
            for i, (t0, n) in enumerate(TILES):
                dve.wait_ge(sg_mm, i + 1)
                if n == P:
                    t3 = tmp[:, i % 2, 0:4 * n].rearrange("p (g t) -> p g t", g=4)
                    chain.after(dve.tensor_tensor(t3, hn(6 + i % 2, n), bias, ALU.add))
                else:
                    t3 = tmp[:, i % 2, 0:4 * n].rearrange("p (g t) -> p g t", g=4)
                    t4 = tmp[:, i % 2, 0:4 * n].rearrange("p (g b t) -> p g b t", g=4, b=NB)
                    s4 = ps[:, 6 + i % 2, 0:4 * n].rearrange("p (g b t) -> p g b t", g=4, b=NB)
                    chain.after(dve.tensor_tensor(t4, s4, over(bias[:, :, 0:DS], 2, NB), ALU.add))
                dve.tensor_tensor(cT[:, 12:16, t0:t0 + n], t3, cT[:, 12:16, t0:t0 + n], ALU.mult).then_inc(sg_done, 1)
            for j, (l, i) in enumerate(STEPS):
                n = TILES[i][1]
                dve.wait_ge(de_mm, j + 1)
                if l:
                    dve.wait_ge(de_done, previous(j) + 1)
                dve.tensor_tensor(Dm[0:n, i, :, 0:n], Dm[0:n, i, :, 0:n], hn(2 + j % 2, n, n), ALU.subtract)
                dve.tensor_tensor(Em[0:n, i, :, 0:n], Em[0:n, i, :, 0:n], hn(4 + j % 2, n, n),
                                  ALU.subtract).then_inc(de_done, 1)
            dve.wait_ge(de_done, len(STEPS))
            for i in range(4):
                if i:
                    dve.wait_ge(ks_mm, i)
                    t3 = tmp[:, 0, :].rearrange("p (h v) -> p h v", h=H)
                    chain.after(dve.tensor_tensor(t3, hn(0, P), last(ecols[:, i, 3, :].unsqueeze(2), P), ALU.mult))
                    dve.tensor_tensor(R[:, :, :], bv[:, i], t3, ALU.subtract).then_inc(r_ready, 1)
                else:
                    dve.tensor_copy(tmp[:, 0, 0:1], ecols[:, 0, 3, 0:1]).then_inc(r_ready, 1)
                dve.wait_ge(ds_mm, i + 1)
                if i >= 2:
                    dve.wait_ge(o_mm, i)
                if i == 0:
                    dve.tensor_copy(S[:, 0], hn(3, P)).then_inc(s_ready, 1)
                else:
                    for h in range(H):
                        ins = dve.scalar_tensor_tensor(out=S[:, i % 2, h], in0=S[:, (i - 1) % 2, h],
                                                       scalar=egl[:, i, h:h + 1], in1=ps[:, 3, h * P:h * P + P],
                                                       op0=ALU.mult, op1=ALU.add)
                    ins.then_inc(s_ready, 1)
            colb = cst[:, C_COLB:C_COLB + NB * NS].rearrange("p (b t) -> p b t", b=NB)
            for h in range(H):
                if h >= 2:
                    dve.wait_ge(ks_done, h - 1)
                dve.tensor_tensor(km[:, h % 2], over(cT[:, 4 + h, SEQ:NT], 1, NB), colb, ALU.mult).then_inc(km_ready, 1)
            dve.wait_ge(ks_done, H)
            t3 = tmp[0:NS, 0, :].rearrange("p (h v) -> p h v", h=H)
            chain.after(dve.tensor_tensor(t3, hn(0, P, NS), last(ecols[0:NS, 4, 3, :].unsqueeze(2), P), ALU.mult))
            dve.tensor_tensor(R[0:NS], bv[0:NS, 4], t3, ALU.subtract).then_inc(r_ready, 1)
            dve.wait_ge(vn_ready, 5)
            for h in range(H):
                if h >= 2:
                    dve.wait_ge(ss_mm, h - 1)
                dve.tensor_tensor(vm[:, h % 2], over(vn[0:NS, 0, h], 1, NB),
                                  last(cst[0:NS, C_ROWB:C_ROWB + NB].unsqueeze(2), P), ALU.mult).then_inc(vm_ready, 1)
                if h >= 1:
                    sample_state(dve, chain, h - 1, ss_mm, ss_done, S0, egls, ps)
            sample_state(dve, chain, H - 1, ss_mm, ss_done, S0, egls, ps)
            for h in range(H):
                dve.wait_ge(o_root, h + 1)
                chain.after(dve.reciprocal(rstd[:, h % 2], rstd[:, h % 2]))
                chain.after(dve.scalar_tensor_tensor(out=cT[:, 8 + h], in0=cT[:, 8 + h], scalar=gains[:, G_O:G_O + 1],
                                                     in1=rstd[:, h % 2], op0=ALU.mult, op1=ALU.mult))
                dve.tensor_tensor(cT[:, 8 + h], cT[:, 8 + h], zT[:, h], ALU.mult).then_inc(o_done, 1)


def sample_state(dve, chain, h, ss_mm, ss_done, S0, egls, ps):
    dve.wait_ge(ss_mm, h + 1)
    chain.after(dve.tensor_tensor(S0[:, h], S0[:, h], last(egls[:, h, :].unsqueeze(2), P), ALU.mult))
    for a in range(2):
        dve.tensor_tensor(S0[:, h, 4 * a:4 * a + 4], S0[:, h, 4 * a:4 * a + 4],
                          ps[:, 4 + 2 * (h % 2) + a, 0:512].rearrange("p (b v) -> p b v", b=4), ALU.add
                          ).then_inc(ss_done, 1)


def mixer_output(nc, io, sem, hT, ps, cT):
    with ExitStack() as ctx:
        ohi = ctx.enter_context(nc.sbuf_tensor("ou_ohi", [P, KT, NT], F32R))
        olo = ctx.enter_context(nc.sbuf_tensor("ou_olo", [P, KT, NT], F32R))
        tiles = SplitTiles(nc, ctx, sem, "ou_")
        high, low, added = sem("ou_high"), sem("ou_low"), sem("ou_added")
        w = io["w_out"].rearrange("(k p) c -> p k c", p=P)
        block = ctx.enter_context(nc.Block())

        @block.sync
        def _(sp):
            for m in range(KT):
                tiles.load(sp, m, w[:, :, m * P:(m + 1) * P])

        @block.gpsimd
        def _(pool):
            for m in range(KT):
                tiles.split_low(pool, m)

        @block.scalar
        def _(act):
            for k in range(KT):
                act.copy(ohi[:, k, :], cT[:, 8 + k, :]).then_inc(high, 1)
                if k == 3:
                    tiles.split_high(act, 0)
            for m in range(1, KT):
                tiles.split_high(act, m)

        @block.tensor
        def _(pe):
            for m in range(KT):
                if m >= 4:
                    pe.wait_ge(added, m - 3)
                tiles.products(pe, m, ps, m % 4, ohi, olo, parts=None if m else low)

        @block.vector
        def _(dve):
            for k in range(KT):
                dve.wait_ge(high, k + 1)
                dve.tensor_tensor(olo[:, k, :], cT[:, 8 + k, :], ohi[:, k, :].bitcast(F32), ALU.subtract
                                  ).then_inc(low, 1)
            for m in range(KT):
                dve.wait_ge(tiles.used, m + 1)
                dve.tensor_tensor(in2(hT[:, m]), in2(hT[:, m]), pair(ps, m, NT), ALU.add).then_inc(added, 1)


def memory_attention(nc, io, sem, hT, cst, gains, ps):
    SCALE = float(2 * P) ** -0.5
    ident = cst[:, C_ID:C_ID + P]
    MEMORY = 2 * KT
    QUERY = 3 * KT
    RING = 7
    LAST = len(TILES) - 1
    with ExitStack() as ctx:
        def sb(name, shape, dt=F32):
            return ctx.enter_context(nc.sbuf_tensor("at_" + name, shape, dt))

        memT = sb("memT", [P, KT, MEM])
        mvT = sb("mvT", [P, KT, MEM])
        cache = sb("cache", [P, 5, KT, MEM])
        slots = [cache[:, i] for i in range(5)] + [memT[:, :, :], mvT[:, :, :]]
        mkT = sb("mkT", [P, KT, MEM])
        mv = sb("mv", [P, 2, D])
        qT = sb("qT", [P, KT, NT])
        nhi = sb("nhi", [P, KT, NT], F32R)
        nlo = sb("nlo", [P, KT, NT], F32R)
        nlo_flat = nlo[:, :, :].rearrange("p k n -> p (k n)")
        mhi, mlo = (nlo_flat[:, i * KT * MEM:(i + 1) * KT * MEM].rearrange("p (k m) -> p k m", k=KT) for i in range(2))
        qm = sb("qm", [P, 2, KT, NS])
        prob = sb("prob", [P, 2, 4, MEM])
        rstd, rstd_m = prob[:, 0].rearrange("p h m -> p (h m)"), prob[:, 1, 0]
        probT = sb("probT", [P, 2, 8, P])
        small = sb("small", [P, 2, 4, 4])
        mixed_s = prob[0:NS, LAST % 2].rearrange("p h m -> p (h m)")
        tiles = SplitTiles(nc, ctx, sem, "at_")

        mem_loaded = [sem(f"at_mem_loaded{i}") for i in range(2)]
        squares_m, sums_m, roots_m, normed_m = (sem("at_squares_m"), sem("at_sums_m"), sem("at_roots_m"),
                                                sem("at_normed_m"))
        high_m, low_m = sem("at_high_m"), sem("at_low_m")
        squares, sums, roots, normed = sem("at_squares"), sem("at_sums"), sem("at_roots"), sem("at_normed")
        high, low = sem("at_high"), sem("at_low")
        taken, mv_turned, mv_taken = sem("at_taken"), sem("at_mv_turned"), sem("at_mv_taken")
        cache_loaded = [sem(f"at_cache_loaded{i}") for i in range(RING)]
        cache_used = sem("at_cache_used")
        scores, maxed, exped, scaled = sem("at_scores"), sem("at_maxed"), sem("at_exped"), sem("at_scaled")
        turned, turned_out, mixed = sem("at_turned"), sem("at_turned_out"), sem("at_mixed")
        sample_out = sem("at_sample_out")
        mixed_high, mixed_low = sem("at_mixed_high"), sem("at_mixed_low")
        qm_ready, added, dve_seq, stored = sem("at_qm_ready"), sem("at_added"), sem("at_dve_seq"), sem("at_stored")
        weights = [io[n].rearrange("(k p) c -> p k c", p=P) for n in ("w_mk", "w_mv", "w_mq", "w_mo")]
        block = ctx.enter_context(nc.Block())

        @block.sync
        def _(sp):
            def load_tile(m):
                tiles.load(sp, m, weights[m // KT][:, :, (m % KT) * P:(m % KT + 1) * P])

            def load_cache(i):
                if i >= RING:
                    sp.wait_ge(cache_used, i - RING + 1)
                elif i == 6:
                    sp.wait_ge(mv_turned, 4)
                elif i == 5:
                    sp.wait_ge(low_m, KT)
                if i < NB:
                    dst, src = slots[i % RING], io["cacheT"][i]
                else:
                    dst = slots[i % RING].rearrange("p k m -> p (k m)").rearrange("p (m d) -> p m d", m=2)
                    src = io["cache_v"][i - NB]
                sp.dma_start(dst, src).then_inc(cache_loaded[i % RING], 16)

            for k in range(2):
                sp.dma_start(memT[:, 4 * k:4 * k + 4], io["memT"][:, 4 * k:4 * k + 4]).then_inc(mem_loaded[k], 16)
            for m in range(QUERY + 3):
                load_tile(m)
                if MEMORY + 1 <= m <= MEMORY + 6:
                    load_cache(m - MEMORY - 1)
                if m == KT + 4:
                    sp.wait_ge(taken, KT)
                    sp.dma_start(io["mem_k"], mkT[:, :, :]).then_inc(stored, 16)
            for i in range(6, 2 * NB):
                load_cache(i)
                if i == 6:
                    sp.wait_ge(mv_taken, 4)
                    sp.dma_start(io["mem_v"], mv[:, :, :]).then_inc(stored, 16)
            for m in range(QUERY + 3, 4 * KT):
                load_tile(m)
            sp.wait_ge(stored, 32)

        @block.gpsimd
        def _(pool):
            for m in range(4 * KT):
                tiles.split_low(pool, m)

        @block.tensor
        def _(pe):
            norm_sums(pe, cst, mvT, ps, MEM, squares_m, sums_m)
            for m in range(MEMORY):
                if m >= 4:
                    pe.wait_ge(taken, m - 3)
                tiles.products(pe, m, ps, (m % 4) // 2, mhi, mlo, [(m % 2, 0, MEM)],
                               None if m else low_m)
                if m == KT:
                    norm_sums(pe, cst, qT, ps, NT, squares, sums, 4)

            def turn_values(half, bank):
                pe.wait_ge(taken, KT + 4 * half + 4)
                for i in range(2):
                    for k in range(4):
                        mm = pe.transpose(ps[:, bank + i, k * P:(k + 1) * P],
                                          mvT[:, 4 * half + k, i * P:(i + 1) * P], ident)
                    mm.then_inc(mv_turned, 1)

            turn_values(0, 6)
            for m in range(MEMORY, QUERY):
                if m < MEMORY + 2:
                    pe.wait_ge(taken, 2 * (m - MEMORY) + MEMORY - 2)
                elif m == MEMORY + 2:
                    pe.wait_ge(mv_taken, 4)
                elif m >= MEMORY + 4:
                    pe.wait_ge(taken, m - 3)
                tiles.products(pe, m, ps, m % 4, nhi, nlo, parts=low if m == MEMORY else None)
                if m == MEMORY:
                    turn_values(1, 4)

            pe.wait_ge(taken, QUERY)

            def score(i):
                t0, n = TILES[i]
                if i:
                    pe.wait_ge(exped, i)
                if i < LAST:
                    for h in range(4):
                        for e in range(2):
                            mm = pe.matmul(ps[:, h // 2, (h % 2) * MEM:(h % 2 + 1) * MEM], qT[:, 2 * h + e, t0:t0 + P],
                                           mkT[:, 2 * h + e, :], start=(e == 0), stop=(e == 1))
                    mm.then_inc(scores, 1)
                    return
                for b in range(NB):
                    pe.wait_ge(qm_ready, b + 1)
                    pe.wait_ge(cache_loaded[b % RING], 16 * (b // RING + 1))
                    for h in range(4):
                        for e in range(2):
                            mm = pe.matmul(ps[0:n, h // 2, (h % 2) * MEM:(h % 2 + 1) * MEM], qm[:, b % 2, 2 * h + e],
                                           slots[b % RING][:, 2 * h + e, :], start=(b == 0 and h % 2 == 0 and e == 0),
                                           stop=(b == NB - 1 and e == 1), skip_group_check=True)
                    mm.then_inc(cache_used, 1)

            def turn(i):
                n = TILES[i][1]
                pe.wait_ge(scaled, i + 1)
                if i:
                    pe.wait_ge(turned_out, i)
                for j in range(8):
                    h, m = j // 2, j % 2
                    mm = pe.transpose(ps[:, 2 + j // 4, (j % 4) * P:(j % 4) * P + n],
                                      prob[0:n, i % 2, h, m * P:(m + 1) * P], ident[0:n, 0:n])
                mm.then_inc(turned, 1)

            def mix(i):
                pe.wait_ge(turned_out, i + 1)
                if i:
                    pe.wait_ge(mixed_low, i)
                if i < LAST:
                    for j in range(8):
                        h = j // 2
                        for m in range(2):
                            mm = pe.matmul(ps[:, 4 + j // 4, (j % 4) * P:(j % 4 + 1) * P], mv[:, m, j * P:(j + 1) * P],
                                           probT[:, i % 2, 2 * h + m, :], start=(m == 0), stop=(m == 1))
                    mm.then_inc(mixed, 1)
                    return
                for b in range(NB):
                    s = (NB + b) % RING
                    pe.wait_ge(qm_ready, NB + b + 1)
                    pe.wait_ge(cache_loaded[s], 16 * ((NB + b) // RING + 1))
                    vc = slots[s].rearrange("p k m -> p (k m)")
                    for h in range(4):
                        for m in range(2):
                            mm = pe.matmul(ps[0:NS, 4 + h // 2, (h % 2) * 256:(h % 2 + 1) * 256],
                                           qm[:, b % 2, 2 * h + m], vc[:, m * D + h * 256:m * D + (h + 1) * 256],
                                           start=(b == 0 and h % 2 == 0 and m == 0), stop=(b == NB - 1 and m == 1),
                                           skip_group_check=True)
                    mm.then_inc(cache_used, 1)
                pe.wait_ge(sample_out, 1)
                for j in range(8):
                    mm = pe.transpose(ps[:, 6 + j // 4, (j % 4) * P:(j % 4) * P + NS],
                                      mixed_s[:, j * P:(j + 1) * P], ident[0:NS, 0:NS])
                mm.then_inc(mixed, 1)

            for i in range(len(TILES) + 2):
                if i < len(TILES):
                    score(i)
                if 1 <= i <= len(TILES):
                    turn(i - 1)
                if i >= 2:
                    mix(i - 2)
            pe.wait_ge(mixed_low, len(TILES))
            for m in range(QUERY, 4 * KT):
                if m >= QUERY + 4:
                    pe.wait_ge(added, m - QUERY - 3)
                tiles.products(pe, m, ps, m % 4, nhi, nlo)

        @block.scalar
        def _(act):
            for k in range(KT):
                act.wait_ge(mem_loaded[k // 4], 16)
                act.activation(mvT[:, k, :], memT[:, k, :], ACT.Square).then_inc(squares_m, 1)
            tiles.split_high(act, 0)
            norm_root(act, cst, ps, MEM, rstd_m, sums_m, roots_m)
            tiles.split_high(act, 1)
            split_input_high(act, memT, mhi, normed_m, high_m)
            for m in range(QUERY):
                tiles.split_high(act, m + 2)
                act.wait_ge(tiles.used, m + 1)
                if m < MEMORY:
                    dst = mkT if m < KT else mvT
                    act.copy(dst[:, m % KT], ps[:, m % 4, 0:MEM]).then_inc(taken, 1)
                else:
                    act.copy(in2(qT[:, m - MEMORY]), pair(ps, m, NT)).then_inc(taken, 1)
                if m < KT:
                    act.activation(qT[:, m, :], hT[:, m, :], ACT.Square).then_inc(squares, 1)
                elif m < MEMORY:
                    if m == KT:
                        norm_root(act, cst, ps, NT, rstd, sums, roots, 4)
                    elif KT + 2 <= m < KT + 6:
                        for k in range(2 * (m - KT - 2), 2 * (m - KT - 1)):
                            act.wait_ge(normed, k + 1)
                            act.copy(nhi[:, k, :], qT[:, k, :]).then_inc(high, 1)

            def turn_out(i):
                n = TILES[i][1]
                act.wait_ge(turned, i + 1)
                if i >= 2:
                    act.wait_ge(mixed, i - 1)
                act.copy(probT[:, i % 2, :, 0:n].rearrange("p (a j) n -> p a j n", a=2),
                         ps[:, 2:4, :].rearrange("p a (j n) -> p a j n", j=4)[:, :, :, 0:n]).then_inc(turned_out, 1)

            def mix_high(i):
                t0, n = TILES[i]
                bank = 4 if i < LAST else 6
                if i == LAST:
                    act.wait_ge(cache_used, 2 * NB)
                    act.copy(mixed_s.rearrange("p (a n) -> p a n", a=2), ps[0:NS, 4:6, :]).then_inc(sample_out, 1)
                act.wait_ge(mixed, i + 1)
                act.copy(nhi[:, :, t0:t0 + n].rearrange("p (a j) n -> p a j n", a=2),
                         ps[:, bank:bank + 2, :].rearrange("p a (j n) -> p a j n", j=4)[:, :, :, 0:n]).then_inc(mixed_high, 1)

            for i in range(len(TILES) + 2):
                if i < len(TILES):
                    n = TILES[i][1]
                    act.wait_ge(maxed, i + 1)
                    if i >= 2:
                        act.wait_ge(turned, i - 1)
                    for h in range(4):
                        ins = act.activation(prob[0:n, i % 2, h, :], ps[0:n, h // 2, (h % 2) * MEM:(h % 2 + 1) * MEM],
                                             ACT.Exp, bias=small[0:n, i % 2, 1, h:h + 1], scale=SCALE,
                                             accum_out=small[0:n, i % 2, 2, h:h + 1])
                    ins.then_inc(exped, 1)
                if 1 <= i <= len(TILES):
                    turn_out(i - 1)
                if i >= 2:
                    mix_high(i - 2)
            for m in range(QUERY + 2, 4 * KT):
                tiles.split_high(act, m)

        @block.vector
        def _(dve):
            chain = Chain(dve, dve_seq)
            norm_scale(dve, chain, gains, G_MEMKV, memT, MEM, rstd_m, memT, roots_m, normed_m,
                       lambda k: split_input_low(dve, memT, mhi, mlo, high_m, low_m, k))
            norm_scale(dve, chain, gains, G_MEM, hT, NT, rstd, qT, roots, normed)

            def take_values(half, bank):
                for i in range(2):
                    dve.wait_ge(mv_turned, 2 * half + i + 1)
                    dve.tensor_copy(mv[:, i, 512 * half:512 * half + 512], ps[:, bank + i, :]).then_inc(mv_taken, 1)

            take_values(0, 6)
            dve.wait_ge(tiles.used, MEMORY)
            for k in range(KT):
                split_input_low(dve, qT, nhi, nlo, high, low, k)
            take_values(1, 4)
            colb = cst[:, C_COLB:C_COLB + NB * NS].rearrange("p (b t) -> p b t", b=NB)

            def mask(b, src):
                dve.tensor_tensor(qm[:, b % 2], src, over(colb[:, b], 1, KT), ALU.mult).then_inc(qm_ready, 1)

            def mix_low(i):
                t0, n = TILES[i]
                bank = 4 if i < LAST else 6
                dve.wait_ge(mixed_high, i + 1)
                view = lambda x: x[:, :, t0:t0 + n].rearrange("p (a j) n -> p a j n", a=2)
                dve.tensor_tensor(view(nlo), ps[:, bank:bank + 2, :].rearrange("p a (j n) -> p a j n", j=4)[:, :, :, 0:n],
                                  view(nhi).bitcast(F32), ALU.subtract).then_inc(mixed_low, 1)

            dve.wait_ge(taken, QUERY)
            for b in range(2):
                mask(b, qT[:, :, SEQ:NT])
            for i in range(len(TILES) + 2):
                if i == LAST:
                    for b in range(2, NB):
                        dve.wait_ge(cache_used, b - 1)
                        mask(b, qT[:, :, SEQ:NT])
                if i < len(TILES):
                    n = TILES[i][1]
                    s = small[0:n, i % 2]
                    if i < LAST:
                        dve.wait_ge(scores, i + 1)
                    else:
                        dve.wait_ge(cache_used, NB)
                    if i >= 2:
                        dve.wait_ge(exped, i - 1)
                    chain.after(dve.tensor_reduce(s[:, 0, :].rearrange("p (a h) -> p a h", a=2),
                                                  ps[0:n, 0:2, :].rearrange("p a (h m) -> p a h m", h=2), AX, ALU.max))
                    dve.tensor_scalar(s[:, 1, :], s[:, 0, :], -SCALE, None, ALU.mult).then_inc(maxed, 1)
                    dve.wait_ge(exped, i + 1)
                    chain.after(dve.reciprocal(s[:, 3, :], s[:, 2, :]))
                    dve.tensor_tensor(prob[0:n, i % 2], prob[0:n, i % 2], last(s[:, 3, :].unsqueeze(2), MEM),
                                      ALU.mult).then_inc(scaled, 1)
                if i == LAST + 2:
                    dve.wait_ge(turned_out, LAST + 1)
                    for b in range(NB):
                        dve.wait_ge(cache_used, NB + b - 1)
                        mask(b, probT[:, LAST % 2, :, 0:NS])
                if i >= 2:
                    mix_low(i - 2)
            for m in range(KT):
                dve.wait_ge(tiles.used, QUERY + m + 1)
                dve.tensor_tensor(in2(hT[:, m]), in2(hT[:, m]), pair(ps, m, NT), ALU.add).then_inc(added, 1)


def peer_scores(nc, io, sem, hT, cst, gains, ps, xhi, xlo, scores_sb):
    with ExitStack() as ctx:
        def sb(name, shape, dt=F32):
            return ctx.enter_context(nc.sbuf_tensor("ps_" + name, shape, dt))

        nT = qT = sb("nT", [P, KT, NT])
        rstd = sb("rstd", [P, NT])
        tiles = SplitTiles(nc, ctx, sem, "ps_")
        kbd = sb("kbd", [P, PH, 2 * NKEY])
        squares, sums, roots, normed = sem("ps_squares"), sem("ps_sums"), sem("ps_roots"), sem("ps_normed")
        taken, low = sem("ps_taken"), sem("ps_low")
        keys_zero, keys_loaded = sem("ps_keys_zero"), sem("ps_keys_loaded")
        score_mm, score_out, high, dve_seq, zeroed = (sem("ps_score_mm"), sem("ps_score_out"), sem("ps_high"),
                                                      sem("ps_dve_seq"), sem("ps_zeroed"))
        block = ctx.enter_context(nc.Block())

        @block.sync
        def _(sp):
            w = io["peer_wq"].rearrange("(k p) c -> p k c", p=P)
            for m in range(KT):
                tiles.load(sp, m, w[:, :, m * P:(m + 1) * P])
                if m == 3:
                    sp.wait_ge(keys_zero, 1)
                    sp.dma_start(kbd[0:64, :, 0:NKEY], io["keysT"][0:64]).then_inc(keys_loaded, 16)
                    sp.dma_start(kbd[64:P, :, NKEY:2 * NKEY], io["keysT"][64:P]).then_inc(keys_loaded, 16)

        @block.gpsimd
        def _(pool):
            pool.memset(kbd[:, :, :], 0.0).then_inc(keys_zero, 1)
            pool.memset(scores_sb[:, 4], 0.0).then_inc(zeroed, 1)
            for m in range(KT):
                tiles.split_low(pool, m)

        @block.tensor
        def _(pe):
            norm_sums(pe, cst, nT, ps, NT, squares, sums)
            for m in range(KT):
                if m >= 4:
                    pe.wait_ge(taken, m - 3)
                tiles.products(pe, m, ps, m % 4, xhi, xlo, parts=None if m else low)
            pe.wait_ge(taken, KT)
            pe.wait_ge(keys_loaded, 32)
            for c in range(2 * len(TILES)):
                t0, n = TILES[c // 2]
                if c >= 4:
                    pe.wait_ge(score_out, c - 3)
                for x in range(4):
                    h = 4 * (c % 2) + x
                    mm = pe.matmul(ps[0:n, 2 * (c % 4) + x // 2, (x % 2) * 256:(x % 2 + 1) * 256],
                                   qT[:, h, t0:t0 + n], kbd[:, h, :], start=True, stop=True)
                mm.then_inc(score_mm, 1)

        @block.scalar
        def _(act):
            norm_squares(act, hT, nT, squares)
            tiles.split_high(act, 0)
            norm_root(act, cst, ps, NT, rstd, sums, roots)
            tiles.split_high(act, 1)
            split_input_high(act, nT, xhi, normed, high)
            for m in range(KT):
                if m + 2 < KT:
                    tiles.split_high(act, m + 2)
                act.wait_ge(tiles.used, m + 1)
                act.copy(in2(qT[:, m]), pair(ps, m, NT)).then_inc(taken, 1)
            act.wait_ge(zeroed, 1)
            for c in range(2 * len(TILES)):
                n = TILES[c // 2][1]
                act.wait_ge(score_mm, c + 1)
                act.copy(scores_sb[0:n, c // 2, 8 * (c % 2):8 * (c % 2) + 8, :].rearrange("p (a x) k -> p a (x k)", a=2),
                         ps[0:n, 2 * (c % 4):2 * (c % 4) + 2, :]).then_inc(score_out, 1)

        @block.vector
        def _(dve):
            chain = Chain(dve, dve_seq)
            norm_scale(dve, chain, gains, G_FFN, hT, NT, rstd, nT, roots, normed,
                       lambda k: split_input_low(dve, nT, xhi, xlo, high, low, k))


class ExpertLoop:

    def __init__(self, nc, ctx, sem, name, io, j0, count, ps, xhi, xlo):
        sb = lambda n, s, dt=F32: ctx.enter_context(nc.sbuf_tensor(name + n, s, dt))
        self.u = sb("u", [P, 4, KT, P])
        self.uhi = sb("uhi", [P, 2, KT, P], F32R)
        self.ulo = sb("ulo", [P, 2, KT, P], F32R)
        self.h = sb("h", [P, 2, 2, NT])
        self.u_loaded = [sem(f"{name}u_loaded{i}") for i in range(4)]
        self.high, self.low, self.products, self.gelus = (sem(name + "high"), sem(name + "low"),
                                                          sem(name + "products"), sem(name + "gelus"))
        self.h_stored = [sem(f"{name}h_stored{i}") for i in range(2)]
        self.io, self.j0, self.count, self.ps, self.x = io, j0, count, ps, (xhi, xlo)

    def load(self, sp, j, slot):
        sp.dma_start(self.u[:, slot], self.io["uT"][self.j0 + j]).then_inc(self.u_loaded[slot], 16)

    def store(self, sp, group, c):
        sp.dma_start(self.io["acts"][self.j0 // 4 + group, :, 2 * c:2 * c + 2, :], self.h[:, c]
                     ).then_inc(self.h_stored[c], 16)

    def sync_step(self, sp, g, first=False, last=False):
        for b in range(4):
            j = 4 * g + b
            if not (last and b):
                if not (first and b == 0):
                    sp.wait_ge(self.low, j)
                self.load(sp, j + 3, (b + 3) % 4)
            if b % 2 == 0 and not (first and b == 0):
                sp.wait_ge(self.gelus, j)
                self.store(sp, g if b else g - 1, 0 if b else 1)

    def scalar_high(self, act, j, b, g, wait_products=True):
        act.wait_ge(self.u_loaded[b], 16 * g + 16)
        if wait_products:
            act.wait_ge(self.products, j - 1)
        act.copy(self.uhi[:, b % 2], self.u[:, b]).then_inc(self.high, 1)

    def scalar_tile(self, act, g, b, first=False, last=False):
        j = 4 * g + b
        if not (last and b == 3):
            self.scalar_high(act, j + 1, (b + 1) % 4, g + (b + 1) // 4, not (first and b == 0))
        act.wait_ge(self.products, j + 1)
        if b % 2 == 0 and not first:
            act.wait_ge(self.h_stored[b // 2], 16 * g)
        act.activation(in2(self.h[:, b // 2, b % 2]), self.ps[:, 2 * (b % 2):2 * (b % 2) + 2, 0:HALF],
                       ACT.Gelu_apprx_tanh).then_inc(self.gelus, 1)

    def pool_step(self, pool, g, first=False):
        for b in range(4):
            j = 4 * g + b
            pool.wait_ge(self.high, j + 1)
            if not (first and b < 2):
                pool.wait_ge(self.products, j - 1)
            pool.tensor_tensor(self.ulo[:, b % 2], self.u[:, b], self.uhi[:, b % 2].bitcast(F32), ALU.subtract
                               ).then_inc(self.low, 1)

    def tensor_tile(self, pe, g, b, first=False):
        j = 4 * g + b
        pe.wait_ge(self.low, j + 1)
        if not (first and b < 2):
            pe.wait_ge(self.gelus, j - 1)
        xhi, xlo = self.x
        for k in range(KT):
            for n, (w, x) in enumerate(((self.uhi, xhi), (self.uhi, xlo), (self.ulo, xhi))):
                for a in range(2):
                    mm = pe.matmul(self.ps[:, 2 * (b % 2) + a, 0:HALF], w[:, b % 2, k, :],
                                   x[:, k, a * HALF:(a + 1) * HALF], start=(k == 0 and n == 0),
                                   stop=(k == KT - 1 and n == 2))
        mm.then_inc(self.products, 1)

    def run(self, eng, step):
        n = self.count // 4
        step(0, first=True)
        with eng.Fori(1, n - 1) as g:
            step(g)
        step(n - 1, last=True)

    def finish_sync(self, sp):
        n = self.count // 4
        sp.wait_ge(self.gelus, self.count)
        self.store(sp, n - 1, 1)
        for c in range(2):
            sp.wait_ge(self.h_stored[c], 16 * n)


LOWEST = -3.0e38


def peer_select(nc, io, sem, cst, ps, xhi, xlo, scores_sb, picks, drops):
    COUNT = 56
    with ExitStack() as ctx:
        def sb(name, shape, dt=F32):
            return ctx.enter_context(nc.sbuf_tensor("se_" + name, shape, dt))

        loop = ExpertLoop(nc, ctx, sem, "se_", io, 0, COUNT, ps, xhi, xlo)
        s = sb("s", [P, 16, NKEY])
        r = sb("r", [P, 16, NKEY])
        best = sb("best", [P, 16, TOPK])
        where = sb("where", [P, 16, TOPK], U32)
        wheref = sb("wheref", [P, PH, 2, TOPK])
        cand = sb("cand", [P, PH, TOPK * TOPK])
        top = sb("top", [P, PH, TOPK])
        topi = sb("topi", [P, PH, TOPK], U32)
        parts = sb("parts", [P, 2, PH * TOPK], U32)
        partsf = sb("partsf", [P, 2, PH * TOPK])
        idle = sb("idle", [P, 2])
        seq = sem("se_seq")
        block = ctx.enter_context(nc.Block())

        @block.sync
        def _(sp):
            for j in range(3):
                loop.load(sp, j, j)
            loop.run(sp, lambda g, first=False, last=False: loop.sync_step(sp, g, first, last))
            loop.finish_sync(sp)

        @block.scalar
        def _(act):
            loop.scalar_high(act, 0, 0, 0, False)

            def step(g, first=False, last=False):
                for b in range(4):
                    loop.scalar_tile(act, g, b, first, last)

            loop.run(act, step)

        @block.gpsimd
        def _(pool):
            loop.run(pool, lambda g, first=False, last=False: loop.pool_step(pool, g, first))

        @block.tensor
        def _(pe):
            def step(g, first=False, last=False):
                for b in range(4):
                    loop.tensor_tile(pe, g, b, first)

            loop.run(pe, step)

        @block.vector
        def _(dve):
            STEPS = 19
            iota16 = cst[:, C_IOTA:C_IOTA + TOPK]
            dve.memset(idle[:, :], 0.0)
            with dve.Fori(0, len(TILES)) as i:
                done = 0

                def after(ins, search=False):
                    nonlocal done
                    done += 1
                    ins.then_inc(seq, 1)
                    dve.wait_ge(seq, i * STEPS + done)
                    if search:
                        dve.tensor_copy(idle[:, 0:1], idle[:, 1:2])

                after(dve.tensor_copy(s[:, :, :], scores_sb[:, bass.ds(i, 1)].rearrange("p o c k -> p (o c) k")), True)
                for c in range(16):
                    ins = dve.max(best[:, c, 0:8], s[:, c, :])
                after(ins, True)
                for c in range(16):
                    dve.max_index(where[:, c, 0:8], best[:, c, 0:8], s[:, c, :])
                    ins = dve.match_replace(r[:, c, :], best[:, c, 0:8], s[:, c, :], LOWEST)
                after(ins, True)
                for c in range(16):
                    ins = dve.max(best[:, c, 8:16], r[:, c, :])
                after(ins, True)
                for c in range(16):
                    ins = dve.max_index(where[:, c, 8:16], best[:, c, 8:16], r[:, c, :])
                b4 = best[:, :, :].rearrange("p (h q) a -> p h q a", q=2)
                after(dve.tensor_tensor(cand[:, :, :].rearrange("p h (a b) -> p h a b", a=TOPK),
                                        last(b4[:, :, 0, :].unsqueeze(3), TOPK), over(b4[:, :, 1, :], 2, TOPK), ALU.add))
                dve.tensor_copy(wheref[:, :, :, :], where[:, :, :].rearrange("p (h q) a -> p h q a", q=2))
                for h in range(PH):
                    ins = dve.max(top[:, h, 0:8], cand[:, h, :])
                after(ins, True)
                rc = r[:, :, :].rearrange("p (h q) k -> p h (q k)", q=2)
                for h in range(PH):
                    dve.max_index(topi[:, h, 0:8], top[:, h, 0:8], cand[:, h, :])
                    ins = dve.match_replace(rc[:, h], top[:, h, 0:8], cand[:, h, :], LOWEST)
                after(ins, True)
                for h in range(PH):
                    ins = dve.max(top[:, h, 8:16], rc[:, h])
                after(ins, True)
                for h in range(PH):
                    ins = dve.max_index(topi[:, h, 8:16], top[:, h, 8:16], rc[:, h])
                after(ins, True)
                dve.tensor_tensor(drops[:, bass.ds(i, 1)].rearrange("p o (h a) -> p (o h) a", h=PH), top[:, :, :],
                                  last(top[:, :, 0:1], TOPK), ALU.subtract)
                flat = topi[:, :, :].rearrange("p h a -> p (h a)")
                dve.tensor_scalar(parts[:, 0], flat, 4, None, ALU.logical_shift_right)
                after(dve.tensor_scalar(parts[:, 1], flat, TOPK - 1, None, ALU.bitwise_and))
                after(dve.tensor_copy(partsf[:, :, :], parts[:, :, :]))
                eq = s[:, :, :].rearrange("p c k -> p (c k)").rearrange("p (j a) -> p j a", a=TOPK)
                for q in range(2):
                    after(dve.tensor_tensor(eq, last(partsf[:, q].unsqueeze(2), TOPK), over(iota16, 1, PH * TOPK),
                                            ALU.is_equal))
                    e4 = eq.rearrange("p (h j) a -> p h j a", h=PH)
                    after(dve.tensor_tensor(e4, e4, over(wheref[:, :, q, :], 2, TOPK), ALU.mult))
                    after(dve.tensor_reduce(picks[:, bass.ds(i, 1), q].rearrange("p o j -> p (o j)"), eq, AX, ALU.add))
                for _ in range(STEPS - done):
                    after(dve.tensor_copy(partsf[:, 0, 0:1], parts[:, 0, 0:1]))
                assert done == STEPS


def peer_spread(nc, io, sem, cst, ps, xhi, xlo, picks, drops):
    COUNT = 72
    PARTS = 3
    with ExitStack() as ctx:
        def sb(name, shape, dt=F32):
            return ctx.enter_context(nc.sbuf_tensor("sp_" + name, shape, dt))

        loop = ExpertLoop(nc, ctx, sem, "sp_", io, 56, COUNT, ps, xhi, xlo)
        pickT = sb("pickT", [P, 2 + PARTS, NT])
        part = sb("part", [P, NT], BF16)
        cur = sb("cur", [P, 2 + PARTS, 32])
        iota = sb("iota", [P, P], BF16)
        hot1 = sb("hot1", [P, 2, 8, P], BF16)
        hot2 = sb("hot2", [P, 2, PARTS, 8, P], BF16)
        spread = sb("spread", [P, P, 32])
        total = sb("total", [P, 2, 5 * PH])
        exps, gates, turned, turned_out = sem("sp_exps"), sem("sp_gates"), sem("sp_turned"), sem("sp_turned_out")
        hots, spread_mm, spread_out, seq, cur_seq = (sem("sp_hots"), sem("sp_spread_mm"), sem("sp_spread_out"),
                                                     sem("sp_seq"), sem("sp_cur_seq"))
        spread_stored = sem("sp_spread_stored")
        ident = cst[:, C_ID:C_ID + P]
        block = ctx.enter_context(nc.Block())

        @block.sync
        def _(sp):
            for j in range(3):
                loop.load(sp, j, j)

            def store_spread(g):
                sp.wait_ge(spread_out, 4 * g + 4)
                sp.dma_start(io["gates"][g], spread[:, :, :]).then_inc(spread_stored, 16)

            def step(g, first=False, last=False):
                loop.sync_step(sp, g, first, last)
                if not last:
                    store_spread(g)

            loop.run(sp, step)
            loop.finish_sync(sp)
            store_spread(COUNT // 4 - 1)
            sp.wait_ge(spread_stored, 16 * (COUNT // 4))

        @block.scalar
        def _(act):
            act.activation(drops[:, :, :], drops[:, :, :], ACT.Exp).then_inc(exps, 1)
            loop.scalar_high(act, 0, 0, 0, False)

            def take(g, b, fresh=False):
                act.wait_ge(spread_mm, 4 * g + b + 1)
                if b == 0 and not fresh:
                    act.wait_ge(spread_stored, 16 * g)
                for x in range(2):
                    ins = act.copy(spread[:, :, 8 * b + 4 * x:8 * b + 4 * x + 4],
                                   ps[:, 4 + 2 * (b % 2) + x, :].rearrange("p (t e) -> p e t", t=4))
                ins.then_inc(spread_out, 1)

            def step(g, first=False, last=False):
                for b in range(4):
                    loop.scalar_tile(act, g, b, first, last)
                    if b:
                        take(g, b - 1, first)
                    elif not first:
                        take(g - 1, 3)

            loop.run(act, step)
            take(COUNT // 4 - 1, 3)

        @block.gpsimd
        def _(pool):
            loop.run(pool, lambda g, first=False, last=False: loop.pool_step(pool, g, first))

        @block.tensor
        def _(pe):
            pe.wait_ge(gates, 1)
            for i, (t0, n) in enumerate(TILES):
                if i >= 2:
                    pe.wait_ge(turned_out, i - 1)
                for q in range(3):
                    mm = pe.transpose(ps[:, 4 + i % 2, q * P:q * P + n], picks[0:n, i, q, :], ident[0:n, 0:n])
                mm.then_inc(turned, 1)
            pe.wait_ge(turned_out, len(TILES))

            def step(g, first=False, last=False):
                for b in range(4):
                    loop.tensor_tile(pe, g, b, first)
                    j = 4 * g + b
                    pe.wait_ge(hots, j + 1)
                    if not (first and b < 2):
                        pe.wait_ge(spread_out, j - 1)
                    for t in range(8):
                        for x in range(PARTS):
                            mm = pe.matmul(ps[:, 4 + 2 * (b % 2) + t // 4, (t % 4) * P:(t % 4 + 1) * P],
                                           hot1[:, b % 2, t], hot2[:, b % 2, x, t], start=(x == 0),
                                           stop=(x == PARTS - 1))
                    mm.then_inc(spread_mm, 1)

            loop.run(pe, step)

        @block.vector
        def _(dve):
            chain = Chain(dve, seq)
            dve.wait_ge(exps, 1)
            d3 = drops[:, :, :].rearrange("p i (h a) -> p (i h) a", a=TOPK)
            chain.after(dve.tensor_reduce(total[:, 0], d3, AX, ALU.add))
            chain.after(dve.reciprocal(total[:, 1], total[:, 0]))
            dve.tensor_tensor(picks[:, :, 2, :].rearrange("p i (h a) -> p i h a", a=TOPK),
                              drops[:, :, :].rearrange("p i (h a) -> p i h a", a=TOPK),
                              last(total[:, 1].rearrange("p (i h) -> p i h", h=PH).unsqueeze(3), TOPK),
                              ALU.mult).then_inc(gates, 1)
            for i, (t0, n) in enumerate(TILES):
                dve.wait_ge(turned, i + 1)
                dve.tensor_copy(pickT[:, 0:3, t0:t0 + n],
                                ps[:, 4 + i % 2, 0:3 * P].rearrange("p (q t) -> p q t", q=3)[:, :, 0:n]
                                ).then_inc(turned_out, 1)
            dve.wait_ge(turned_out, len(TILES))
            dve.tensor_copy(iota[:, :], cst[:, C_IOTA:C_IOTA + P])
            for x in range(PARTS - 1):
                chain.after(dve.tensor_copy(part[:, :], pickT[:, 2 + x, :]))
                chain.after(dve.tensor_tensor(pickT[:, 3 + x, :], pickT[:, 2 + x, :], part[:, :], ALU.subtract))
                chain.after(dve.tensor_copy(pickT[:, 2 + x, :], part[:, :]))

            def step(g, first=False, last=False):
                if not first:
                    dve.wait_ge(hots, 4 * g)
                dve.tensor_copy(cur[:, :, :], pickT[:, :, bass.ds(32 * g, 32)]).then_inc(cur_seq, 1)
                dve.wait_ge(cur_seq, g + 1)
                for b in range(4):
                    j = 4 * g + b
                    if not (first and b < 2):
                        dve.wait_ge(spread_mm, j - 1)
                    for t in range(8):
                        c = 8 * b + t
                        dve.tensor_scalar(hot1[:, b % 2, t], iota[:, :], cur[:, 0, c:c + 1], None, ALU.is_equal)
                        for x in range(PARTS):
                            ins = dve.tensor_scalar(hot2[:, b % 2, x, t], iota[:, :], cur[:, 1, c:c + 1],
                                                    cur[:, 2 + x, c:c + 1], ALU.is_equal, ALU.mult)
                    ins.then_inc(hots, 1)

            loop.run(dve, step)


def peer_output(nc, io, sem, hT, ps):
    GROUPS = NKEY // 4
    with ExitStack() as ctx:
        def sb(name, shape, dt=F32):
            return ctx.enter_context(nc.sbuf_tensor("po_" + name, shape, dt))

        v = sb("v", [P, 2, 2, D])
        w = sb("w", [P, 2, 4, NT])
        g_sb = sb("g", [P, 2, NT // 32, 4, 32])
        whi = sb("whi", [P, 2, 4, NT], F32R)
        wlo = sb("wlo", [P, 2, 4, NT], F32R)
        vhi = sb("vhi", [P, 2, 4, D], F32R)
        vlo = sb("vlo", [P, 2, 4, D], F32R)
        v_loaded = [sem(f"po_v_loaded{i}") for i in range(2)]
        hg_loaded = [sem(f"po_hg_loaded{i}") for i in range(2)]
        gg_loaded = [sem(f"po_gg_loaded{i}") for i in range(2)]
        v_high, v_low, weighted, w_high, w_low = (sem("po_v_high"), sem("po_v_low"), sem("po_weighted"),
                                                  sem("po_w_high"), sem("po_w_low"))
        products, added = sem("po_products"), sem("po_added")
        block = ctx.enter_context(nc.Block())
        v_dram = io["peer_v"].rearrange("(p e) d -> p e d", p=P)
        g_dram = io["gates"].rearrange("k p e t -> p k e t")

        def run(eng, step):
            step(0, first=True)
            with eng.Fori(1, GROUPS // 2 - 1) as u:
                step(u)
            step(GROUPS // 2 - 1, last=True)

        @block.sync
        def _(sp):
            def load(q, s, waits=True):
                for c in range(2):
                    if waits:
                        sp.wait_ge(v_low, 4 * q - 2 + 2 * c)
                    sp.dma_start(v[:, c], v_dram[:, bass.ds(4 * q + 2 * c, 2), :]).then_inc(v_loaded[c], 16)

            def load_w(q, s, waits=True):
                if waits:
                    sp.wait_ge(w_low, q - 1)
                sp.dma_start(w[:, s], io["acts"][q]).then_inc(hg_loaded[s], 16)
                sp.dma_start(g_sb[:, s], g_dram[:, :, bass.ds(4 * q, 4), :]).then_inc(gg_loaded[s], 16)

            load_w(0, 0, False)
            load(0, 0, False)
            load_w(1, 1, False)

            def step(u, first=False, last=False):
                load(2 * u + 1, 1)
                if not last:
                    load_w(2 * u + 2, 0)
                    load(2 * u + 2, 0)
                    load_w(2 * u + 3, 1)

            run(sp, step)

        @block.scalar
        def _(act):
            def split(q, u, s, free):
                if free:
                    act.wait_ge(products, 8 * q - 8)
                for b in range(4):
                    if b % 2 == 0:
                        act.wait_ge(v_loaded[b // 2], 16 * q + 16)
                    act.copy(vhi[:, s, b], v[:, b // 2, b % 2]).then_inc(v_high, 1)
                act.wait_ge(weighted, q + 1)
                act.copy(whi[:, s], w[:, s]).then_inc(w_high, 1)

            split(0, 0, 0, False)

            def step(u, first=False, last=False):
                split(2 * u + 1, u, 1, not first)
                if not last:
                    split(2 * u + 2, u + 1, 0, True)

            run(act, step)

        @block.gpsimd
        def _(pool):
            def split(q, s, free):
                if free:
                    pool.wait_ge(products, 8 * q - 8)
                for b in range(4):
                    pool.wait_ge(v_high, 4 * q + b + 1)
                    pool.tensor_tensor(vlo[:, s, b], v[:, b // 2, b % 2], vhi[:, s, b].bitcast(F32), ALU.subtract
                                       ).then_inc(v_low, 1)

            split(0, 0, False)

            def step(u, first=False, last=False):
                split(2 * u + 1, 1, not first)
                if not last:
                    split(2 * u + 2, 0, True)

            run(pool, step)

        @block.tensor
        def _(pe):
            def group(q, s, first=False):
                pe.wait_ge(v_low, 4 * q + 4)
                pe.wait_ge(w_low, q + 1)
                for m in range(KT):
                    if not (first and m < 4):
                        pe.wait_ge(added, 8 * q + m - 3)
                    for b in range(4):
                        for n, (x, y) in enumerate(((vhi, whi), (vhi, wlo), (vlo, whi))):
                            for a in range(2):
                                mm = pe.matmul(ps[:, 2 * (m % 4) + a, 0:HALF], x[:, s, b, m * P:(m + 1) * P],
                                               y[:, s, b, a * HALF:(a + 1) * HALF], start=(b == 0 and n == 0),
                                               stop=(b == 3 and n == 2))
                    mm.then_inc(products, 1)

            def step(u, first=False, last=False):
                group(2 * u, 0, first)
                group(2 * u + 1, 1)

            run(pe, step)

        @block.vector
        def _(dve):
            def weigh(q, u, s):
                dve.wait_ge(hg_loaded[s], 16 * u + 16)
                dve.wait_ge(gg_loaded[s], 16 * u + 16)
                for b in range(4):
                    x = w[:, s, b].rearrange("p (k t) -> p k t", t=32)
                    ins = dve.tensor_tensor(x, x, g_sb[:, s, :, b, :], ALU.mult)
                ins.then_inc(weighted, 1)

            def rest(q, s):
                dve.wait_ge(w_high, q + 1)
                dve.tensor_tensor(wlo[:, s], w[:, s], whi[:, s].bitcast(F32), ALU.subtract).then_inc(w_low, 1)

            def add(q, m):
                dve.wait_ge(products, 8 * q + m + 1)
                dve.tensor_tensor(in2(hT[:, m]), in2(hT[:, m]), pair(ps, m, NT), ALU.add).then_inc(added, 1)

            def group(q, after, u, s, prepare=True):
                if prepare:
                    weigh(after, u, s)
                for m in range(4):
                    add(q, m)
                if prepare:
                    rest(after, s)
                for m in range(4, KT):
                    add(q, m)

            weigh(0, 0, 0)
            rest(0, 0)

            def step(u, first=False, last=False):
                group(2 * u, 2 * u + 1, u, 1)
                group(2 * u + 1, 2 * u + 2, u + 1, 0, not last)

            run(dve, step)


def final_norm(nc, io, sem, hT, cst, gains, ps):
    with ExitStack() as ctx:
        nT = ctx.enter_context(nc.sbuf_tensor("fn_nT", [P, KT, NT], F32))
        rstd = ctx.enter_context(nc.sbuf_tensor("fn_rstd", [P, NT], F32))
        squares, sums, roots, normed = sem("fn_squares"), sem("fn_sums"), sem("fn_roots"), sem("fn_normed")
        dve_seq, stored = sem("fn_dve_seq"), sem("fn_stored")
        block = ctx.enter_context(nc.Block())

        @block.sync
        def _(sp):
            for k in range(2):
                sp.wait_ge(normed, 4 * k + 4)
                sp.dma_start(io["y"][:, 4 * k:4 * k + 4], nT[:, 4 * k:4 * k + 4]).then_inc(stored, 16)
            sp.wait_ge(stored, 32)

        @block.tensor
        def _(pe):
            norm_sums(pe, cst, nT, ps, NT, squares, sums)

        @block.scalar
        def _(act):
            norm_squares(act, hT, nT, squares)
            norm_root(act, cst, ps, NT, rstd, sums, roots)

        @block.vector
        def _(dve):
            norm_scale(dve, Chain(dve, dve_seq), gains, G_FINAL, hT, NT, rstd, nT, roots, normed)


def build(nc, io):
    with ExitStack() as ctx:
        def sb(name, shape, dt=F32):
            return ctx.enter_context(nc.sbuf_tensor(name, shape, dt))

        held = []

        def sem(name):
            held.append(nc.alloc_semaphore(name=name))
            return held[-1]

        def free_semaphores():
            nc.clear_and_free_semaphores(list(held))
            held.clear()
            nc.all_engine_barrier()

        ps = ctx.enter_context(nc.psum_tensor("ps", [P, 8, 512], F32))
        hT = sb("hT", [P, KT, NT])
        cst = sb("cst", [P, C_N])
        gains = sb("gains", [P, G_N])
        rows = sb("rows", [P, R_N])
        with ExitStack() as mixer:
            cT = mixer.enter_context(nc.sbuf_tensor("cT", [P, 16, NT], F32))
            zT = mixer.enter_context(nc.sbuf_tensor("zT", [P, H, NT], F32))
            vv = mixer.enter_context(nc.sbuf_tensor("vv", [P, 5, 512], F32))
            gate = mixer.enter_context(nc.sbuf_tensor("gate", [P, 5, 8], F32))
            mixer_inputs(nc, io, sem, hT, cst, gains, rows, ps, cT, zT, vv, gate)
            mixer_core(nc, io, sem, cst, gains, rows, ps, cT, zT, vv, gate)
            mixer_output(nc, io, sem, hT, ps, cT)
        free_semaphores()
        memory_attention(nc, io, sem, hT, cst, gains, ps)
        free_semaphores()
        with ExitStack() as peer:
            picks = peer.enter_context(nc.sbuf_tensor("picks", [P, 5, 3, P], F32))
            drops = peer.enter_context(nc.sbuf_tensor("drops", [P, 5, P], F32))
            xhi = peer.enter_context(nc.sbuf_tensor("xhi", [P, KT, NT], F32R))
            xlo = peer.enter_context(nc.sbuf_tensor("xlo", [P, KT, NT], F32R))
            with ExitStack() as select:
                scores_sb = select.enter_context(nc.sbuf_tensor("scores", [P, 5, 16, NKEY], F32))
                peer_scores(nc, io, sem, hT, cst, gains, ps, xhi, xlo, scores_sb)
                peer_select(nc, io, sem, cst, ps, xhi, xlo, scores_sb, picks, drops)
            peer_spread(nc, io, sem, cst, ps, xhi, xlo, picks, drops)
        peer_output(nc, io, sem, hT, ps)
        final_norm(nc, io, sem, hT, cst, gains, ps)


def feature_major(a):
    a = np.asarray(a)
    return np.ascontiguousarray(a.T.reshape(-1, P, a.shape[0]).transpose(1, 0, 2))


def token_major(a):
    return np.ascontiguousarray(a.transpose(2, 1, 0).reshape(a.shape[2], -1))


def layouts(x):
    g = lambda a: np.asarray(a).reshape(-1, P).T
    return {
        "xT": feature_major(np.concatenate([np.asarray(x["x_prompt"]).reshape(SEQ, D),
                                            np.asarray(x["x_sample"]).reshape(NS, D)])),
        "consts": constant_table(),
        "gains": np.ascontiguousarray(np.concatenate(
            [g(x[k]) for k in ("norm_mix_g", "norm_mem_g", "mem_norm_g", "norm_ffn_g", "final_norm_g", "o_norm_g")], 1)),
        "rows": np.concatenate([np.asarray(x[k]).reshape(-1) for k in
                                ("a_log", "dt_bias", "sg_ln_g", "sg_ln_b", "sg_b")]),
        "w_in": np.asarray(x["w_in"])[0],
        "w_out": np.asarray(x["w_out"])[0],
        "conv_w": np.ascontiguousarray(np.asarray(x["conv_w"])[0].T.reshape(QKV_TILES, P, CONV).transpose(1, 0, 2)),
        "state_conv": np.ascontiguousarray(np.asarray(x["state_conv"])[0].transpose(2, 0, 1)
                                           .reshape(QKV_TILES, P, NB, 3).transpose(1, 0, 2, 3)),
        "sg_wT": np.ascontiguousarray(np.asarray(x["sg_w"])[0].transpose(0, 2, 1)),
        "state_delta": np.asarray(x["state_delta"])[0],
        "memT": feature_major(np.asarray(x["mem_prompt"])[0]),
        **{k: np.asarray(x[k])[0] for k in ("w_mq", "w_mk", "w_mv", "w_mo")},
        "cacheT": np.ascontiguousarray(np.asarray(x["cache_mem_k"])[0].reshape(NB, MEM, KT, P).transpose(0, 3, 2, 1)),
        "cache_v": np.ascontiguousarray(np.asarray(x["cache_mem_v"])[0].reshape(NB, 2, P, D).transpose(0, 2, 1, 3)),
        "peer_wq": np.asarray(x["peer_wq"])[0],
        "keysT": np.ascontiguousarray(np.asarray(x["peer_keys"])[0].transpose(1, 3, 0, 2).reshape(P, PH, NKEY)),
        "uT": np.ascontiguousarray(np.asarray(x["peer_u"])[0].reshape(NKEY, NKEY, KT, P).transpose(1, 3, 2, 0)),
        "peer_v": np.asarray(x["peer_v"])[0],
    }


OUTPUTS = {
    "y": (P, KT, NT), "delta_prompt": (P, H, P), "conv_prompt": (P, QKV_TILES, 3), "mem_k": (P, KT, MEM),
    "mem_v": (P, 2, D), "delta_sample": (P, H, NB, P), "conv_sample": (P, QKV_TILES, NB, 3), "vrows": (NS, 512),
}


def make(nc, x):
    arrays = layouts(x)
    io = {n: nc.dram_tensor("in_" + n, list(a.shape), F32, kind="ExternalInput").ap() for n, a in arrays.items()}
    io |= {n: nc.dram_tensor("out_" + n, list(s), F32, kind="ExternalOutput").ap() for n, s in OUTPUTS.items()}
    io["acts"] = nc.dram_tensor("acts", [NKEY // 4, P, 4, NT], F32, kind="Internal").ap()
    io["gates"] = nc.dram_tensor("gates", [NT // 32, P, P, 32], F32, kind="Internal").ap()
    build(nc, io)
    return {"in_" + n: a for n, a in arrays.items()}


def kernel(**inputs):
    import concourse.bacc as bacc
    from concourse.bass_utils import run_bass_kernel_spmd

    nc = bacc.Bacc("TRN2", target_bir_lowering=False, num_devices=1)
    arrays = make(nc, inputs)
    r = run_bass_kernel_spmd(nc, [arrays], core_ids=[0]).results[0]
    o = {n: np.asarray(r["out_" + n]) for n in OUTPUTS}
    y = token_major(o["y"])
    rows_of = lambda a: a.transpose(2, 1, 0).reshape(a.shape[2], -1)
    return (
        y[:SEQ].reshape(1, SEQ, D),
        y[SEQ:].reshape(NB, DS, D),
        np.ascontiguousarray(o["delta_prompt"].transpose(1, 0, 2))[None, None],
        np.ascontiguousarray(rows_of(o["conv_prompt"])).reshape(1, 1, 3, -1),
        np.ascontiguousarray(token_major(o["mem_k"])).reshape(1, 1, MEM, 4, 256),
        np.ascontiguousarray(o["mem_v"].transpose(1, 0, 2)).reshape(1, 1, MEM, 4, 256),
        np.ascontiguousarray(o["delta_sample"].transpose(2, 1, 0, 3))[None],
        np.ascontiguousarray(o["conv_sample"].transpose(2, 3, 1, 0)).reshape(1, NB, 3, -1),
        o["vrows"].reshape(1, NB, DS, 512),
    )
```
